# Optimizing a Trainium2 kernel written in Bass

```python
import math
import jax, jax.numpy as jnp
from jax import lax
import numpy as np

D_MODEL = 1024
BATCH = 1
SEQ = 512
DEPTH = 2

NSA_HEADS = 16
NSA_KV_GROUPS = 4
HEAD_DIM = 64
NSA_HPG = NSA_HEADS // NSA_KV_GROUPS
CMP_BLOCK = 32
CMP_STRIDE = 16
CMP_HIDDEN = 256
SEL_BLOCK = 64
SEL_TOPK = 8
WINDOW = 512
NSA_QBLOCK = 64
ROPE_THETA = 500000.0
ROPE_DIM = HEAD_DIM // 4
NSA_Q_WIDTH = NSA_HEADS * HEAD_DIM
NSA_KV_WIDTH = NSA_KV_GROUPS * HEAD_DIM
NSA_IN_WIDTH = NSA_Q_WIDTH + 6 * NSA_KV_WIDTH + 3 * NSA_HEADS

SSM_EXPAND = 2
SSM_D_INNER = SSM_EXPAND * D_MODEL
SSM_HEAD_DIM = 64
SSM_HEADS = SSM_D_INNER // SSM_HEAD_DIM
SSM_GROUPS = 4
SSM_HPG = SSM_HEADS // SSM_GROUPS
SSM_STATE = 128
SSM_CONV = 4
SSM_CHUNK = 128
SSM_CONV_DIM = SSM_D_INNER + 2 * SSM_GROUPS * SSM_STATE
SSM_IN_WIDTH = SSM_D_INNER + SSM_CONV_DIM + SSM_HEADS

FFN_HIDDEN = -(-8 * D_MODEL // (3 * 256)) * 256

N_NSA_LAYERS = (DEPTH + 1) // 2
N_SSM_LAYERS = DEPTH // 2
EPS = 1e-6

kernel_name = "nsa_mamba2_interleaved_hybrid"

def rms_norm(x, w):
    xf = x.astype(jnp.float32)
    xf = xf * lax.rsqrt(jnp.mean(xf * xf, axis=-1, keepdims=True) + EPS)
    return (xf * w.astype(jnp.float32)).astype(x.dtype)

def partial_rope(x, pos):
    half = ROPE_DIM // 2
    inv = jnp.power(jnp.float32(ROPE_THETA), -jnp.arange(half, dtype=jnp.float32) / half)
    ang = pos.astype(jnp.float32)[..., None] * inv
    ang = ang.reshape(ang.shape[:2] + (1,) * (x.ndim - 3) + (half,))
    cos, sin = jnp.cos(ang), jnp.sin(ang)
    xr = x[..., :ROPE_DIM].astype(jnp.float32)
    x1, x2 = xr[..., :half], xr[..., half:]
    rot = jnp.concatenate([x1 * cos - x2 * sin, x2 * cos + x1 * sin], axis=-1).astype(x.dtype)
    return jnp.concatenate([rot, x[..., ROPE_DIM:]], axis=-1)

def masked_softmax(s, mask):
    s = jnp.where(mask, s.astype(jnp.float32), -1e30)
    return jnp.where(mask, jax.nn.softmax(s, axis=-1), 0.0)

def nsa_mixer(h, pos, w_in, q_norm, k_norm, cmp_pe, cmp_w1, cmp_b1, cmp_w2, w_out):
    B, S, _ = h.shape
    G, HP, dh, QB = NSA_KV_GROUPS, NSA_HPG, HEAD_DIM, NSA_QBLOCK
    scale = dh ** -0.5
    cuts = list(np.cumsum([NSA_Q_WIDTH] + [NSA_KV_WIDTH] * 6))
    q, k_c, v_c, k_s, v_s, k_w, v_w, g = jnp.split(h @ w_in, cuts, axis=-1)
    q = partial_rope(rms_norm(q.reshape(B, S, G, HP, dh), q_norm), pos)

    nc = (S - CMP_BLOCK) // CMP_STRIDE + 1
    starts = np.arange(nc) * CMP_STRIDE
    blk_idx = starts[:, None] + np.arange(CMP_BLOCK)[None, :]
    cmp_end = starts + CMP_BLOCK - 1

    def compress(t, pe, w1, b1, w2):
        tb = t[:, blk_idx] + pe[:, None, :]
        tb = jnp.moveaxis(tb, 3, 2).reshape(B, nc, G, CMP_BLOCK * dh)
        return jax.nn.silu(tb @ w1 + b1) @ w2

    kc = compress(k_c.reshape(B, S, G, dh), cmp_pe[0], cmp_w1[0], cmp_b1[0], cmp_w2[0])
    vc = compress(v_c.reshape(B, S, G, dh), cmp_pe[1], cmp_w1[1], cmp_b1[1], cmp_w2[1])
    kc = partial_rope(rms_norm(kc, k_norm[0]), pos[:, cmp_end])
    s_c = jnp.einsum('bqghd,bcgd->bghqc', q, kc).astype(jnp.float32) * scale
    mask_c = jnp.asarray(cmp_end[None, :] <= np.arange(S)[:, None])
    p_c = masked_softmax(s_c, mask_c)
    o_c = jnp.einsum('bghqc,bcgd->bqghd', p_c.astype(vc.dtype), vc)

    sel_nb = S // SEL_BLOCK
    n_sel = min(SEL_TOPK, sel_nb)
    js = np.arange(sel_nb)[None, :] * SEL_BLOCK
    overlap = ((starts[:, None] < js + SEL_BLOCK) & (starts[:, None] + CMP_BLOCK > js)).astype(np.float32)
    imp = jnp.einsum('bghqc,cj->bgqj', p_c, jnp.asarray(overlap))
    t_blk = np.arange(S)[:, None] // SEL_BLOCK
    jb = np.arange(sel_nb)[None, :]
    forced = (jb == 0) | (jb == t_blk) | (jb == t_blk - 1)
    imp = jnp.where(forced, jnp.inf, jnp.where(jb > t_blk, -jnp.inf, imp))
    _, sel_idx = lax.top_k(imp, n_sel)

    def to_blocks(t):
        return t.reshape(B, sel_nb, SEL_BLOCK, G, dh).transpose(0, 3, 1, 2, 4)
    ks = partial_rope(rms_norm(k_s.reshape(B, S, G, dh), k_norm[1]), pos)
    ks_b, vs_b = to_blocks(ks), to_blocks(v_s.reshape(B, S, G, dh))
    kw = partial_rope(rms_norm(k_w.reshape(B, S, G, dh), k_norm[2]), pos)
    pad = ((0, 0), (WINDOW, 0), (0, 0), (0, 0))
    kw_pad, vw_pad = jnp.pad(kw, pad), jnp.pad(v_w.reshape(B, S, G, dh), pad)

    nqb = S // QB
    q_blocks = jnp.moveaxis(q.reshape(B, nqb, QB, G, HP, dh), 1, 0)
    idx_blocks = jnp.moveaxis(sel_idx.reshape(B, G, nqb, QB, n_sel), 2, 0)
    q_starts = jnp.arange(nqb, dtype=jnp.int32) * QB
    bi = jnp.arange(B)[:, None, None, None]
    gi = jnp.arange(G)[None, :, None, None]

    def block_step(args):
        q0, qb, ib = args
        tq = q0 + jnp.arange(QB, dtype=jnp.int32)
        kg = ks_b[bi, gi, ib]
        vg = vs_b[bi, gi, ib]
        s = jnp.einsum('bqghd,bgqnld->bghqnl', qb, kg).astype(jnp.float32) * scale
        kp = ib[..., None] * SEL_BLOCK + jnp.arange(SEL_BLOCK)
        m = (kp <= tq[:, None, None])[:, :, None].reshape(B, G, 1, QB, n_sel * SEL_BLOCK)
        p = masked_softmax(s.reshape(B, G, HP, QB, n_sel * SEL_BLOCK), m)
        o_s = jnp.einsum('bghqk,bgqkd->bqghd', p.astype(vg.dtype),
                         vg.reshape(B, G, QB, n_sel * SEL_BLOCK, dh))
        kwin = lax.dynamic_slice_in_dim(kw_pad, q0, WINDOW + QB, axis=1)
        vwin = lax.dynamic_slice_in_dim(vw_pad, q0, WINDOW + QB, axis=1)
        kpos = q0 - WINDOW + jnp.arange(WINDOW + QB, dtype=jnp.int32)
        mw = ((kpos[None, :] <= tq[:, None]) & (kpos[None, :] > tq[:, None] - WINDOW)
              & (kpos[None, :] >= 0))
        sw = jnp.einsum('bqghd,bkgd->bghqk', qb, kwin).astype(jnp.float32) * scale
        pw = masked_softmax(sw, mw)
        o_w = jnp.einsum('bghqk,bkgd->bqghd', pw.astype(vwin.dtype), vwin)
        return o_s, o_w

    o_s, o_w = lax.map(block_step, (q_starts, q_blocks, idx_blocks))
    o_s = jnp.moveaxis(o_s, 0, 1).reshape(B, S, G, HP, dh)
    o_w = jnp.moveaxis(o_w, 0, 1).reshape(B, S, G, HP, dh)

    gates = jax.nn.sigmoid(g.astype(jnp.float32)).reshape(B, S, G, HP, 3, 1)
    o = (gates[..., 0, :] * o_c + gates[..., 1, :] * o_s + gates[..., 2, :] * o_w).astype(h.dtype)
    return o.reshape(B, S, NSA_Q_WIDTH) @ w_out

def ssd_mixer(h, w_in, conv_w, conv_b, dt_bias, a_log, d_skip, norm_w, w_out):
    B, S, _ = h.shape
    G, HP, P, N, Q = SSM_GROUPS, SSM_HPG, SSM_HEAD_DIM, SSM_STATE, SSM_CHUNK
    f32 = jnp.float32
    z, xbc, dt = jnp.split(h @ w_in, [SSM_D_INNER, SSM_D_INNER + SSM_CONV_DIM], axis=-1)
    xbc = lax.conv_general_dilated(xbc, conv_w[:, None, :], window_strides=(1,),
                                   padding=[(SSM_CONV - 1, 0)],
                                   dimension_numbers=('NWC', 'WIO', 'NWC'),
                                   feature_group_count=SSM_CONV_DIM)
    xbc = jax.nn.silu(xbc + conv_b)
    xs, bm, cm = jnp.split(xbc, [SSM_D_INNER, SSM_D_INNER + G * N], axis=-1)
    xs = xs.reshape(B, S, G, HP, P)
    bm = bm.reshape(B, S, G, N)
    cm = cm.reshape(B, S, G, N)
    dt = jax.nn.softplus(dt.astype(f32) + dt_bias.astype(f32)).reshape(B, S, G, HP)
    A = -jnp.exp(a_log.astype(f32)).reshape(G, HP)

    nch = S // Q
    def chunks(t):
        return jnp.moveaxis(t.reshape((B, nch, Q) + t.shape[2:]), 1, 0)
    tril = jnp.asarray(np.tril(np.ones((Q, Q), dtype=bool)))[None, :, :, None, None]

    def step(state, inp):
        xc, dtc, bc, cc = inp
        bc, cc = bc.astype(f32), cc.astype(f32)
        cum = jnp.cumsum(dtc * A, axis=1)
        seg = cum[:, :, None] - cum[:, None]
        L = jnp.exp(jnp.where(tril, seg, -jnp.inf))
        xdt = xc.astype(f32) * dtc[..., None]
        cb = jnp.einsum('btgn,bsgn->btsg', cc, bc)
        y_diag = jnp.einsum('btsgh,bsghp->btghp', cb[..., None] * L, xdt)
        y_off = jnp.einsum('btgn,bghpn->btghp', cc, state) * jnp.exp(cum)[..., None]
        decay = jnp.exp(cum[:, -1:] - cum)
        new_state = (state * jnp.exp(cum[:, -1])[..., None, None]
                     + jnp.einsum('bsgn,bsghp->bghpn', bc, xdt * decay[..., None]))
        return new_state, y_diag + y_off

    state0 = jnp.zeros((B, G, HP, P, N), f32)
    _, y = lax.scan(step, state0, (chunks(xs), chunks(dt), chunks(bm), chunks(cm)))
    y = jnp.moveaxis(y, 0, 1).reshape(B, S, G, HP, P)
    y = y + d_skip.astype(f32).reshape(G, HP)[..., None] * xs.astype(f32)
    yg = (y.reshape(B, S, SSM_D_INNER) * jax.nn.silu(z.astype(f32))).reshape(B, S, G, SSM_D_INNER // G)
    yg = yg * lax.rsqrt(jnp.mean(yg * yg, axis=-1, keepdims=True) + EPS)
    y = (yg.reshape(B, S, SSM_D_INNER) * norm_w.astype(f32)).astype(h.dtype)
    return y @ w_out

def swiglu(h, w_gate, w_up, w_down):
    return (jax.nn.silu(h @ w_gate) * (h @ w_up)) @ w_down

def setup_inputs(seed: int = 0) -> dict:
    key = jax.random.key(seed)
    keys = iter(jax.random.split(key, 32))
    f32 = jnp.float32

    def nrm(shape, scale):
        return jax.random.normal(next(keys), shape, f32) * scale

    def gain(shape):
        return 1.0 + nrm(shape, 0.02)

    NA, NB = N_NSA_LAYERS, N_SSM_LAYERS
    x = nrm((BATCH, SEQ, D_MODEL), 1.0)
    positions = jnp.broadcast_to(jnp.arange(SEQ, dtype=jnp.int32), (BATCH, SEQ))
    mix_norm_w = gain((DEPTH, D_MODEL))
    ffn_norm_w = gain((DEPTH, D_MODEL))
    ffn_w_gate = nrm((DEPTH, D_MODEL, FFN_HIDDEN), D_MODEL ** -0.5)
    ffn_w_up = nrm((DEPTH, D_MODEL, FFN_HIDDEN), D_MODEL ** -0.5)
    ffn_w_down = nrm((DEPTH, FFN_HIDDEN, D_MODEL), FFN_HIDDEN ** -0.5)
    nsa_w_in = nrm((NA, D_MODEL, NSA_IN_WIDTH), D_MODEL ** -0.5)
    nsa_q_norm = gain((NA, HEAD_DIM))
    nsa_k_norm = gain((NA, 3, HEAD_DIM))
    nsa_cmp_pe = nrm((NA, 2, CMP_BLOCK, HEAD_DIM), 0.1)
    nsa_cmp_w1 = nrm((NA, 2, CMP_BLOCK * HEAD_DIM, CMP_HIDDEN), (CMP_BLOCK * HEAD_DIM) ** -0.5)
    nsa_cmp_b1 = nrm((NA, 2, CMP_HIDDEN), 0.01)
    nsa_cmp_w2 = nrm((NA, 2, CMP_HIDDEN, HEAD_DIM), CMP_HIDDEN ** -0.5)
    nsa_w_out = nrm((NA, NSA_Q_WIDTH, D_MODEL), NSA_Q_WIDTH ** -0.5)
    ssm_w_in = nrm((NB, D_MODEL, SSM_IN_WIDTH), D_MODEL ** -0.5)
    ssm_conv_w = nrm((NB, SSM_CONV, SSM_CONV_DIM), SSM_CONV ** -0.5)
    ssm_conv_b = nrm((NB, SSM_CONV_DIM), 0.01)
    dt0 = jnp.exp(jax.random.uniform(next(keys), (NB, SSM_HEADS), f32,
                                     minval=math.log(1e-3), maxval=math.log(1e-1)))
    ssm_dt_bias = dt0 + jnp.log(-jnp.expm1(-dt0))
    ssm_a_log = jnp.log(jax.random.uniform(next(keys), (NB, SSM_HEADS), f32, minval=1.0, maxval=16.0))
    ssm_d = gain((NB, SSM_HEADS))
    ssm_norm_w = gain((NB, SSM_D_INNER))
    ssm_w_out = nrm((NB, SSM_D_INNER, D_MODEL), SSM_D_INNER ** -0.5)
    return {"x": x, "positions": positions, "mix_norm_w": mix_norm_w, "ffn_norm_w": ffn_norm_w,
            "ffn_w_gate": ffn_w_gate, "ffn_w_up": ffn_w_up, "ffn_w_down": ffn_w_down,
            "nsa_w_in": nsa_w_in, "nsa_q_norm": nsa_q_norm, "nsa_k_norm": nsa_k_norm,
            "nsa_cmp_pe": nsa_cmp_pe, "nsa_cmp_w1": nsa_cmp_w1, "nsa_cmp_b1": nsa_cmp_b1,
            "nsa_cmp_w2": nsa_cmp_w2, "nsa_w_out": nsa_w_out,
            "ssm_w_in": ssm_w_in, "ssm_conv_w": ssm_conv_w, "ssm_conv_b": ssm_conv_b,
            "ssm_dt_bias": ssm_dt_bias, "ssm_a_log": ssm_a_log, "ssm_d": ssm_d,
            "ssm_norm_w": ssm_norm_w, "ssm_w_out": ssm_w_out}

def reference(x, positions, mix_norm_w, ffn_norm_w, ffn_w_gate, ffn_w_up, ffn_w_down,
              nsa_w_in, nsa_q_norm, nsa_k_norm, nsa_cmp_pe, nsa_cmp_w1, nsa_cmp_b1, nsa_cmp_w2, nsa_w_out,
              ssm_w_in, ssm_conv_w, ssm_conv_b, ssm_dt_bias, ssm_a_log, ssm_d, ssm_norm_w, ssm_w_out):
    h = x
    for i in range(DEPTH):
        j = i // 2
        hn = rms_norm(h, mix_norm_w[i])
        if i % 2 == 0:
            mix = nsa_mixer(hn, positions, nsa_w_in[j], nsa_q_norm[j], nsa_k_norm[j], nsa_cmp_pe[j],
                            nsa_cmp_w1[j], nsa_cmp_b1[j], nsa_cmp_w2[j], nsa_w_out[j])
        else:
            mix = ssd_mixer(hn, ssm_w_in[j], ssm_conv_w[j], ssm_conv_b[j], ssm_dt_bias[j],
                            ssm_a_log[j], ssm_d[j], ssm_norm_w[j], ssm_w_out[j])
        h = h + mix.astype(h.dtype)
        h = h + swiglu(rms_norm(h, ffn_norm_w[i]), ffn_w_gate[i], ffn_w_up[i], ffn_w_down[i]).astype(h.dtype)
    return h


_drawn_inputs = setup_inputs


def setup_inputs(seed=0):
    import zlib

    import numpy as np

    out = dict(_drawn_inputs(seed))
    spreads = {}
    factors = {'nsa_q_norm': 8.0,
     'nsa_k_norm': 8.0,
     'nsa_cmp_b1': 8.0,
     'ssm_conv_b': 6.308,
     'ssm_d': 5.088,
     'ssm_norm_w': 4.348}
    for name, (base, spread) in spreads.items():
        noise = np.random.default_rng([zlib.crc32(name.encode()), seed]).standard_normal(out[name].shape)
        drawn = base * np.exp(spread * noise) if base else spread * noise
        out[name] = __import__('jax').numpy.asarray(drawn.astype(out[name].dtype))
    for name, factor in factors.items():
        out[name] = (out[name] * factor).astype(out[name].dtype)
    return out
```

```python
from contextlib import ExitStack

import numpy as np

import concourse.bass as bass
from concourse import mybir

F32 = mybir.dt.float32
F32R = mybir.dt.float32r
BF16 = mybir.dt.bfloat16
I32 = mybir.dt.int32
ALU = mybir.AluOpType
ACT = mybir.ActivationFunctionType
AX = mybir.AxisListType.X

P = 128
SEQ, DM = 512, 1024
TT = SEQ // P
KT = DM // P
HEADS, GROUPS, HP, DH = 16, 4, 4, 64
CMP_BLOCK, CMP_STRIDE, CMP_HIDDEN = 32, 16, 256
NCMP = (SEQ - CMP_BLOCK) // CMP_STRIDE + 1
NJ = CMP_BLOCK // 2
SCALE = DH ** -0.5
ROPE_HALF, THETA = 8, 500000.0
SH, SG, SHP, SP_, SN = 32, 4, 8, 64, 128
DI = 2048
GW = DI // SG
FF = 2816
FT = FF // P
EPS = 1e-6
CH = 2048
NEG = -1e30
PI = float(np.float32(np.pi))

COL_MIX, COL_FFN, COL_SSMN, COL_CB, COL_CW, COL_B1, COL_PE = 0, 16, 32, 48, 72, 168, 172
NCOLS = COL_PE + 2 * NJ
ROW_W6, ROW_KC, ROW_D, ROW_DTB, ROW_AL, ROW_INV = 0, 384, 448, 480, 512, 544
NROWS = 552


class Tally:
    def __init__(self, sem):
        self.sem, self.n, self.off, self.first = sem, 0, 0, 0

    def inc(self, instruction):
        instruction.then_inc(self.sem, 1)
        self.n += 1

    def wait(self, engine):
        engine.wait_ge(self.sem, self.n + self.off)

    def enter(self, i, per):
        self.off, self.first = i * per, self.n

    def leave(self, turns, per):
        assert self.n - self.first == per, (self.n - self.first, per)
        self.n, self.off = self.first + turns * per, 0


def chunk_plan():
    at, n = {}, 0
    for name, count in (("kv_cmp", 2), ("gates", 1), ("qkv", 8), ("nsa_out", 4), ("up0", 2 * FT // 2),
                        ("down0", 12), ("xbc", 12), ("dt", 1), ("z", 8), ("ssm_out", 8),
                        ("up1", 2 * FT // 2), ("down1", 12)):
        at[name] = n
        n += count
    return at, n


CHUNK, NCHUNKS = chunk_plan()
EVAC, _t = {}, 0
for _name, _count in (("kv_cmp", 4), ("gates", 4), ("qkv", 16), ("nsa_out", 8), ("up0", FT), ("down0", 8),
                      ("xbc", 24), ("dt", 4), ("z", 16), ("ssm_out", 8), ("up1", FT), ("down1", 8)):
    EVAC[_name] = _t
    _t += _count


DVE_GROUP_STEPS, DVE_SCAN_STEPS = 90, 12


def trunk(nc, wstream, xT_in, cols_in, rows_in, pos_in, cw1_in, cw2_in, ident_in, tri_in, cmask_in, out):
    with ExitStack() as ctx:
        def sb(name, shape, dt=F32, c=ctx):
            return c.enter_context(nc.sbuf_tensor(name, shape, dt))

        def sem(name):
            return ctx.enter_context(nc.semaphore(name))

        class Region:
            def __init__(self, start):
                self.end = start

            def take(self, name, shape, dt=F32):
                t = nc.alloc_sbuf_tensor_at(name, shape, dt, offset=self.end)
                self.end += -(-int(np.prod(shape[1:])) * (2 if dt == BF16 else 4) // 32) * 32
                assert self.end <= nc.SBUF_PARTITION_SIZE_BYTES, (name, self.end)
                return t

        r = Region(-(-nc.sbuf_base // 32) * 32)
        cols = r.take("cols", [P, NCOLS])
        rows = r.take("rows", [P, NROWS])
        ident = r.take("ident", [P, P])
        tri = r.take("tri", [P, 3, P])
        ident_bf = r.take("ident_bf", [P, P], BF16)
        negmask_bf = r.take("negmask_bf", [P, P], BF16)
        stat = r.take("stat", [P, 64])
        mhalf = r.take("mhalf", [P, 8])
        wraw = r.take("wraw", [P, 2, CH])
        wh = r.take("wh", [P, 2, CH], F32R)
        wl = r.take("wl", [P, 2, CH], F32R)
        scratch_at = r.end
        diag = r.take("diag", [P, TT, P])
        tmp = r.take("tmp", [P, 2, SEQ])
        sq = r.take("sq", [P, 2, SEQ])
        sqacc = r.take("sqacc", [P, SEQ])
        a = Region(scratch_at)
        rp = a.take("rope_products", [P, 4, 6, ROPE_HALF])
        pc = a.take("pc", [P, TT, HP, 32])
        vz = a.take("vz", [P, HP, DH])
        sm = a.take("sm", [P, 6, 32])
        vst = a.take("vst", [P, TT, 2, DH])
        assert a.end <= r.end
        act_at = r.end
        xh = r.take("xh", [P, KT, SEQ], F32R)
        xl = r.take("xl", [P, KT, SEQ], F32R)
        res_at = r.end
        xT = r.take("xT", [P, KT, SEQ])
        a = Region(res_at)
        kvc = a.take("kvc", [P, TT, 512])
        tb2 = a.take("tb2", [P, 2, GROUPS, 256])
        assert a.end <= r.end
        a = Region(res_at)
        Pm = a.take("Pm", [P, 2, 2, SEQ])
        kB1 = a.take("kB1", [P, 2, SEQ], F32R)
        pcT = a.take("pcT", [P, SEQ])
        assert a.end <= r.end
        arena_at = r.end
        a = Region(arena_at)
        hh = a.take("hh", [P, FT, SEQ], F32R)
        hl = a.take("hl", [P, FT, SEQ], F32R)
        gate = a.take("gate", [P, 2, SEQ])
        hid = a.take("hid", [P, 2, SEQ])
        a = Region(arena_at)
        proj = a.take("proj", [P, TT, 8, DH])
        glin = a.take("glin", [P, TT, 48])
        cosT = a.take("cosT", [P, 5, ROPE_HALF])
        sinT = a.take("sinT", [P, 5, ROPE_HALF])
        ang = a.take("ang", [P, 10, 5 * ROPE_HALF])
        posi = a.take("posi", [P, 5], I32)
        B1c = a.take("B1c", [P, P], F32R)
        B2c = a.take("B2c", [P, P], F32R)
        VC4 = a.take("VC4", [P, GROUPS, DH])
        cmask = a.take("cmask", [P, 2, TT, 32])
        nsa_at = a.end
        tbT = a.take("tbT", [P, 2, NJ, GROUPS, 32])
        cw1 = a.take("cw1", [P, 2, NJ, CMP_HIDDEN])
        cw2 = a.take("cw2", [P, 2, 2, DH])
        hidK = a.take("hidK", [P, 2, P])
        hidV = a.take("hidV", [P, 2, GROUPS, HP, 32])
        kcn = a.take("kcn", [P, 2, DH])
        krp = a.take("krp", [P, 4, ROPE_HALF])
        a = Region(nsa_at)
        qA = a.take("qA", [P, HP, SEQ], F32R)
        qn = a.take("qn", [P, TT, 6, 2, DH])
        kB2 = a.take("kB2", [P, 2, SEQ], F32R)
        xo = a.take("xo", [P, KT, SEQ], F32R)
        xol = a.take("xol", [P, KT, SEQ], F32R)
        PT = a.take("PT", [P, 2, 2, TT, SEQ])
        a = Region(arena_at)
        xtok = a.take("xtok", [P, TT, DI])
        BCf = a.take("BCf", [P, 2, SG, SEQ])
        zraw = a.take("zraw", [P, TT, GW])
        zs = a.take("zs", [P, TT, GW])
        dtb = a.take("dtb", [P, 10, TT * SH])
        ex = a.take("ex", [P, 3, TT * SH])
        bc = a.take("bc", [P, TT, 2, P])
        btst = a.take("btst", [P, 2, P])
        Gm = a.take("Gm", [P, 2, 4, P])
        Lx = a.take("Lx", [P, 2, 2, 4, P])
        state = a.take("state", [P, GW])
        ybuf = a.take("ybuf", [P, 2, GW])
        ysq = a.take("ysq", [P, GW])
        cbm = a.take("cbm", [P, 2, P])
        yst = a.take("yst", [P, 2, 4])
        a = Region(arena_at)
        yT = a.take("yT", [P, TT, 16, P])
        a = Region(arena_at)
        yl = a.take("yl", [P, TT, 16, P], F32R)
        a = Region(act_at)
        yh = a.take("yh", [P, TT, 16, P], F32R)
        assert a.end <= res_at
        a = Region(scratch_at)
        xdt = a.take("xdt", [P, 2, GW])
        xdd = a.take("xdd", [P, 2, GW])
        dxs = a.take("dxs", [P, 2, GW])
        assert a.end <= act_at
        ps = ctx.enter_context(nc.psum_tensor("ps", [P, 8, SEQ], F32))

        params_landed, rest_landed, x_landed, cw_landed, x_again, out_stored = map(
            sem, ("params_landed", "rest_landed", "x_landed", "cw_landed", "x_again", "out_stored"))
        landed = [sem("even_chunk_landed"), sem("odd_chunk_landed")]
        hi_done = sem("weights_hi_done")
        lo_done = sem("weights_lo_done")
        products = sem("products_done")
        evac = sem("tiles_evacuated")
        masks_cast, zeroed, sq_done, acc_done, colsum_done, mean_done, rstd_done, diag_done, rbc_done = map(
            sem, ("masks_cast", "square_sum_zeroed", "squares_done", "square_sum_done", "colsum_done",
                  "mean_square_done", "rms_rstd_done", "diag_done", "rstd_broadcast_done"))
        scaled, xh_done, xl_done, vz_zeroed, vz_done = map(sem, ("norm_scaled", "xh_done", "xl_done", "vz_zeroed", "vz_done"))
        gate_done, hh_done, hl_done = map(sem, ("gate_done", "hidden_hi_done", "hidden_lo_done"))
        vec, act_self, pool_self = map(sem, ("vector_step", "scalar_step", "pool_step"))
        (mhalf_set, kvT, tb_act, tb_vec, tbT_done, hid_mm, hid_done, cmp_mm, kc_sq, kc_mean, kc_rstd, kcn_done, kcT, kc_hi,
         kc_lo, vc_done, angles_done, sincos_done, gates_exp, gates_done) = map(sem, (
             "mhalf_set", "kv_transposed", "taps_by_act", "taps_by_vec", "blocks_built", "cmp_hidden_mm", "cmp_hidden_done",
             "cmp_out_mm", "kc_squared", "kc_mean_square", "kc_rstd", "kc_normed", "kc_transposed", "kc_hi_done",
             "kc_lo_done", "vc_copied", "angles_done", "sincos_done", "gates_exp", "gates_done"))
        (qk_squared, qk_mean, qk_rstd, qk_normed, qkT, qkT_hi, qkT_lo, v_staged, cs_mm, cs_shifted, cs_exp, pc_done,
         pcT_mm, pcT_done, scores, negmax, expd, normed, pT_mm, pT_done, pv_done, o_hi, o_lo) = map(sem, (
             "qk_squared", "qk_mean_square", "qk_rstd", "qk_normed", "qk_transposed", "qk_hi_done", "qk_lo_done",
             "v_staged", "cmp_scores", "cmp_scores_shifted", "cmp_exp", "cmp_probs_done", "cmp_probs_transposed",
             "cmp_probsT_done", "scores_done", "negmax_done", "exp_done", "probs_normed", "probs_transposed",
             "probsT_done", "pv_done", "o_hi_done", "o_lo_done"))
        (silu_done, featT, featT_done, dt_in, dt_e, dt_u, dt_ln, dt_done, a_exp, staged, cum_mm, cum_exp, g_built,
         seg_mm, seg_exp, m_built, cb_mm, cb_done, xdt_done, y_mm, state_mm, y_done, state_done, z_silu, y_sq, y_var,
         y_rs, y_scaled, yT_mm, yT_done, yh_done, yl_done) = map(sem, (
             "conv_silu_done", "feature_transposed", "feature_T_done", "dt_biased", "dt_exp", "dt_u", "dt_ln",
             "dt_done", "a_exp", "chunk_staged", "cum_mm", "cum_exp", "g_built", "segments_mm", "segments_exp",
             "m_built", "cb_mm", "cb_done", "xdt_done", "y_mm", "state_mm", "y_done", "state_done", "z_silu", "y_squared",
             "y_mean_square", "y_rstd", "y_scaled", "yT_mm", "yT_done", "yh_done", "yl_done"))

        def at(n, i, per):
            return n if i is None else i * per + n

        def col(c, n=1):
            return cols[:, c:c + n]

        def after(engine, semaphore, value):
            if not isinstance(value, int) or value > 0:
                engine.wait_ge(semaphore, value)

        def scan_groups(engine, group, enter=None, leave=None):
            group(0, False)
            with engine.Fori(0, SG - 2) as i:
                if enter:
                    enter(i)
                group(i + 1, False)
            if leave:
                leave()
            group(SG - 1, True)

        Q4 = "p (h d) -> p h d"
        RES = {"nsa_out": [8], "ssm_out": [8, 8], "down0": [8, 8, 6], "down1": [8, 8, 6]}
        NORM = {"nsa_out": 1, "down0": 2, "ssm_out": 3}
        NORMCOL = [COL_MIX, COL_FFN, COL_MIX + KT, COL_FFN + KT]

        block = ctx.enter_context(nc.Block())

        @block.sync
        def _(sp):
            sp.dma_start(xT[:, :, :], xT_in).then_inc(x_landed, 16)
            sp.dma_start(cols[:, :], cols_in).then_inc(params_landed, 16)
            sp.dma_start(tri[:, :, :], tri_in).then_inc(params_landed, 16)
            sp.dma_start(ident[:, :], ident_in).then_inc(params_landed, 16)
            sp.dma_start(rows[:, :], rows_in).then_inc(params_landed, 16)
            for n in range(2):
                sp.dma_start(wraw[:, n, :], wstream[n]).then_inc(landed[n], 16)
            sp.dma_start(posi[:, :], pos_in).then_inc(rest_landed, 16)
            sp.dma_start(cmask[:, :, :, :], cmask_in).then_inc(rest_landed, 16)
            sp.dma_start(cw1[:, :, :, :], cw1_in).then_inc(cw_landed, 16)
            sp.dma_start(cw2[:, :, :, :], cw2_in).then_inc(cw_landed, 16)
            with sp.Fori(1, NCHUNKS // 2) as i:
                for k in range(2):
                    sp.wait_ge(lo_done, 2 * i + (k - 1))
                    sp.dma_start(wraw[:, k, :], wstream[bass.ds(2 * i + k, 1)].rearrange("a p n -> p (a n)")
                                 ).then_inc(landed[k], 16)
            for t in range(KT):
                sp.wait_ge(evac, EVAC["down1"] + t + 1)
                sp.dma_start(out[:, t, :], xT[:, t, :]).then_inc(out_stored, 16)
            sp.wait_ge(out_stored, 16 * KT)

        @block.tensor
        def _(pe):
            mm = pe.matmul

            def split_product(o, wa, xa, start, stop):
                mm(o, wa[0], xa[0], start=start, stop=False)
                mm(o, wa[0], xa[1], start=False, stop=False)
                return mm(o, wa[1], xa[0], start=False, stop=stop)

            def chunk_F(n, i, per, x, ks, banks, first, last, before=None, between=None):
                pe.wait_ge(lo_done, at(n + 1, i, per))
                s = n % 2
                for m in range(2):
                    if before:
                        before(m)
                    o = ps[:, banks[m], :]
                    for k, kt in enumerate(ks):
                        w = slice(k * 256 + m * P, k * 256 + (m + 1) * P)
                        hi, lo = x(kt)
                        oo = o if len(hi.shape) == 2 else o.rearrange("p (a b) -> p a b", b=P)
                        ins = split_product(oo, (wh[:, s, w], wl[:, s, w]), (hi, lo),
                                            first and k == 0, last and k == len(ks) - 1)
                    ins.then_inc(products, 1)
                    if between:
                        between(m)

            def chunk_T(n, i, per, ks, width, first, last, before=None):
                pe.wait_ge(lo_done, at(n + 1, i, per))
                s = n % 2
                for tt in range(TT):
                    if before:
                        before(tt)
                    for k, kt in enumerate(ks):
                        w = slice(k * width, (k + 1) * width)
                        t = slice(tt * P, (tt + 1) * P)
                        ins = split_product(ps[:, tt, 0:width], (xh[:, kt, t], xl[:, kt, t]),
                                            (wh[:, s, w], wl[:, s, w]), first and k == 0,
                                            last and k == len(ks) - 1)
                    if tt % 2:
                        ins.then_inc(products, 1)

            def norm(L):
                pe.wait_ge(acc_done, 8 * (L + 1))
                for tt in range(TT):
                    ins = mm(ps[:, 7, tt:tt + 1], sqacc[:, tt * P:(tt + 1) * P], tri[:, 2, 0:1], start=True, stop=True)
                ins.then_inc(colsum_done, 1)
                pe.wait_ge(diag_done, L + 1)
                mm(ps[:, 6, :], tri[:, 2, :], diag[:, :, :].rearrange("p t q -> p (t q)"), start=True, stop=True
                   ).then_inc(rbc_done, 1)
                pe.wait_ge(xl_done, 8 * (L + 1))

            def xs(kt):
                return xh[:, kt, :], xl[:, kt, :]

            def hs(kt):
                return hh[:, kt, :], hl[:, kt, :]

            def ys(kt):
                return yh[:, :, kt, :], yl[:, :, kt, :]

            def residual(name, x, ready=None):
                ks, n0, t0 = RES[name], CHUNK[name], EVAC[name]
                starts = [sum(ks[:q]) for q in range(len(ks))]
                per = 2 * len(ks)
                pe.wait_ge(evac, t0)
                with pe.Fori(0, 2) as i:
                    for p in range(2):
                        for q, nk in enumerate(ks):
                            def free(m):
                                if q == 0:
                                    pe.wait_ge(evac, i * 4 + (t0 + 2 * p + m - 3))
                            if ready and q == 1:
                                ready()
                            chunk_F(n0 + p * len(ks) + q, i, per, x, range(starts[q], starts[q] + nk),
                                    (2 * p, 2 * p + 1), q == 0, q == len(ks) - 1, before=free)

            def ffn(up, down, L):
                norm(L)
                n0, t0 = CHUNK[up], EVAC[up]
                pe.wait_ge(evac, t0)
                with pe.Fori(0, FT // 2) as i:
                    def free(m):
                        pe.wait_ge(evac, i * 2 + (t0 - 1 + m))
                    chunk_F(n0, i, 2, xs, range(KT), (0, 1), True, True, before=free)
                    chunk_F(n0 + 1, i, 2, xs, range(KT), (2, 3), True, True)
                pe.wait_ge(hl_done, FT * (1 + (L == 3)))
                residual(down, hs)

            pe.wait_ge(params_landed, 64)
            norm(0)
            for b in range(2):
                chunk_T(b, None, 0, range(4 * b, 4 * b + 4), 512, b == 0, b == 1)
            for kv in range(2):
                for gp in range(2):
                    for tt in range(TT):
                        pe.wait_ge(evac, tt + 1)
                        f = kv * 256 + gp * P
                        ins = pe.transpose(ps[:, 4 + 2 * kv + gp, tt * P:(tt + 1) * P], kvc[:, tt, f:f + P],
                                           ident[:, :])
                    ins.then_inc(kvT, 1)
            pe.wait_ge(evac, EVAC["gates"])
            chunk_T(CHUNK["gates"], None, 0, range(8), 48, True, True)
            pe.wait_ge(evac, EVAC["qkv"])
            for k in range(2):
                chunk_T(CHUNK["qkv"] + k, None, 0, range(4 * k, 4 * k + 4), 512, k == 0, k == 1)
            pe.wait_ge(cw_landed, 32)
            for kv in range(2):
                pe.wait_ge(tbT_done, 2 * (kv + 1))
                for ht in range(2):
                    r = 2 * kv + ht
                    for j in range(NJ):
                        ins = mm(ps[:, 4, r * P:(r + 1) * P], cw1[:, kv, j, ht * P:(ht + 1) * P],
                                 tbT[:, kv, j, :, :].rearrange("p g c -> p (g c)"), start=j == 0, stop=j == NJ - 1)
                    ins.then_inc(hid_mm, 1)
            pe.wait_ge(hid_done, 4)
            for ht in range(2):
                mm(ps[:, 5, 0:DH], hidK[:, ht, :], cw2[:, 0, ht, :], start=ht == 0, stop=ht == 1)
            for g in range(GROUPS):
                for ht in range(2):
                    lhs = hidV[:, ht, g, :, :].rearrange("p h c -> p (h c)")
                    ins = mm(ps[:, 6, g * DH:(g + 1) * DH], lhs, cw2[:, 1, ht, :], start=ht == 0, stop=ht == 1)
            ins.then_inc(cmp_mm, 1)
            pe.wait_ge(kcn_done, 1)
            pe.transpose(ps[:, 7, 0:P], kcn[:, :, :].rearrange("p a d -> p (a d)"), ident[:, :]
                         ).then_inc(kcT, 1)
            pe.wait_ge(kc_lo, 1)
            pe.wait_ge(masks_cast, 2)

            def qk_transposes(g):
                pe.wait_ge(qk_normed, g * 4 + 4)
                for h in range(6):
                    if h == 4 and not (isinstance(g, int) and g == 0):
                        pe.wait_ge(pT_done, g * 16)
                    for tt in range(TT):
                        ins = pe.transpose(ps[:, h, tt * P:(tt + 1) * P],
                                           qn[:, tt, h, :, :].rearrange("p a d -> p (a d)"), ident[:, :])
                    ins.then_inc(qkT, 1)

            def group(g, more):
                def qk(s):
                    h, i = divmod(s, TT)
                    w = (i + 1) * P
                    if s >= 2:
                        pe.wait_ge(expd, g * 32 + 2 * (s - 1))
                    for b in range(2):
                        o = ps[:, 2 * (s % 2) + b, :]
                        q = qA[:, h, i * P:(i + 1) * P]
                        mm(o[:, 0:w], q, kB1[:, b, 0:w], start=True, stop=False)
                        mm(o[:, 0:w], q, kB2[:, b, 0:w], start=False, stop=False)
                        ins = mm(o[:, i * P:w], ident_bf[:, :], negmask_bf[:, :], start=False, stop=True)
                    ins.then_inc(scores, 1)

                def cmp_scores():
                    pe.wait_ge(o_lo, g * 2)
                    for tt in range(TT):
                        for h in range(HP):
                            o = ps[:, 6, (tt * HP + h) * 32:(tt * HP + h + 1) * 32]
                            q = qA[:, h, tt * P:(tt + 1) * P]
                            mm(o, q, B1c[:, bass.ds(g * 32, 32)], start=True, stop=False)
                            ins = mm(o, q, B2c[:, bass.ds(g * 32, 32)], start=False, stop=True)
                    ins.then_inc(cs_mm, 1)

                def cmp_transposes():
                    pe.wait_ge(pc_done, g + 1)
                    for tt in range(TT):
                        ins = pe.transpose(ps[:, 6, tt * P:(tt + 1) * P], pc[:, tt, :, :].rearrange("p h c -> p (h c)"),
                                           ident[:, :])
                    ins.then_inc(pcT_mm, 1)

                def pT(s):
                    h, i = divmod(s, TT)
                    pe.wait_ge(normed, g * 32 + 2 * (s + 1))
                    if s:
                        pe.wait_ge(pT_done, g * 16 + s)
                    for b in range(2):
                        for j in range(i + 1):
                            ins = pe.transpose(ps[:, 4 + b, j * P:(j + 1) * P], Pm[:, s % 2, b, j * P:(j + 1) * P],
                                               ident[:, :])
                    ins.then_inc(pT_mm, 1)

                def pv(h):
                    o = ps[DH * (h % 2):DH * (h % 2 + 1), 6, :]
                    if h == 0:
                        pe.wait_ge(v_staged, g + 1)
                        pe.wait_ge(pcT_done, g + 1)
                        pe.wait_ge(vz_done, g * 4 + 4)
                    if h == 2:
                        pe.wait_ge(o_lo, g * 2 + 1)
                    pe.wait_ge(pT_done, g * 16 + 4 * (h + 1))
                    mm(o, vz[:, h, :], pcT[:, :], start=True, stop=False)
                    for b in range(2):
                        for j in range(TT):
                            ins = mm(o[:, j * P:], vst[:, j, b, :], PT[:, h % 2, b, j, j * P:], start=False,
                                     stop=b == 1 and j == TT - 1)
                    ins.then_inc(pv_done, 1)

                n0, t0 = CHUNK["qkv"] + 2, EVAC["qkv"] + 4

                def project(part):
                    tt, third = divmod(part, 3)
                    if part == 0:
                        pe.wait_ge(lo_done, g * 2 + (n0 + 2))
                    if third == 0:
                        pe.wait_ge(evac, g * 4 + (t0 + tt))
                    t = slice(tt * P, (tt + 1) * P)
                    for m in range(8 * third, 8 * third + 8):
                        kt, pss = divmod(m, 3)
                        slot, w = (n0 + kt // 4) % 2, slice((kt % 4) * 512, (kt % 4 + 1) * 512)
                        ins = mm(ps[:, 7, :], (xh, xl, xh)[pss][:, kt, t], (wh, wh, wl)[pss][:, slot, w],
                                 start=m == 0, stop=m == 23)
                    if third == 2:
                        ins.then_inc(products, 1)

                for k in range(18):
                    if k < 16:
                        qk(k)
                    if k == 0:
                        cmp_scores()
                    if k == 3:
                        cmp_transposes()
                    if k in (6, 10, 14):
                        pv((k - 6) // 4)
                    if k >= 2:
                        pT(k - 2)
                    if more and k < 12:
                        project(k)
                if more:
                    qk_transposes(g + 1)
                pv(3)

            qk_transposes(0)
            pe.wait_ge(qkT_lo, 6)
            with pe.Fori(0, GROUPS - 1) as g:
                group(g, True)
                pe.wait_ge(qkT_lo, g * 6 + 12)
            group(GROUPS - 1, False)
            pe.wait_ge(o_lo, 2 * GROUPS)
            residual("nsa_out", lambda kt: (xo[:, kt, :], xol[:, kt, :]))
            ffn("up0", "down0", 1)

            norm(2)
            n0, t0 = CHUNK["xbc"], EVAC["xbc"]
            pe.wait_ge(evac, t0)

            def conv_tiles(n, i, t, first_T, source):
                def free(m):
                    pe.wait_ge(evac, at(t + m - 3, i, 4))

                def transposes(j):
                    k = first_T + j
                    pe.wait_ge(silu_done, at(k + 9, i, 4))
                    pe.wait_ge(featT_done, at(max(k - 1, 0), i, 4))
                    for tt in range(TT):
                        ins = pe.transpose(ps[:, 4 + j % 2, tt * P:(tt + 1) * P],
                                           source(j)[:, tt * P:(tt + 1) * P], ident[:, :])
                    ins.then_inc(featT, 1)
                chunk_F(n, i, 2, xs, range(KT), (0, 1), True, True, before=free)
                if source:
                    transposes(0)

                def free2(m):
                    pe.wait_ge(evac, at(t + 2 + m - 3, i, 4))

                def between(m):
                    if source:
                        transposes(1 + m)
                chunk_F(n + 1, i, 2, xs, range(KT), (2, 3), True, True, before=free2, between=between)
                if source:
                    transposes(3)
            conv_tiles(n0, None, t0, 0, None)
            conv_tiles(n0 + 2, None, t0 + 4, 0, None)
            with pe.Fori(0, 4) as i:
                conv_tiles(n0 + 4, i, t0 + 8, 0, lambda j: sq[:, j % 2, :])
            pe.wait_ge(evac, EVAC["dt"])
            chunk_T(CHUNK["dt"], None, 0, range(8), SH, True, True)
            n0, t0 = CHUNK["z"], EVAC["z"]
            pe.wait_ge(evac, t0)
            for k in range(2):
                chunk_T(n0 + k, None, 0, range(4 * k, 4 * k + 4), 512, k == 0, k == 1)
            pe.wait_ge(dt_done, 1)
            for k in range(3):
                ins = mm(ps[:, 6, k * P:(k + 1) * P], tri[:, k, :], dtb[:, 1, :], start=True, stop=True)
            ins.then_inc(cum_mm, 1)
            pe.wait_ge(cum_exp, 1)
            pe.wait_ge(evac, t0 + 4)

            def decays(g, j):
                for q in range(2):
                    pe.wait_ge(g_built, g * 8 + (2 * j + q + 1))
                    after(pe, seg_exp, g * 8 + (2 * j + q - 1))
                    mm(ps[:, q, :], tri[:, 1, :], Gm[:, q, :, :].rearrange("p h t -> p (h t)"), start=True, stop=True
                       ).then_inc(seg_mm, 1)
                pe.wait_ge(staged, g * 4 + (j + 1))
                after(pe, cb_done, g * 4 + j)
                mm(ps[:, 6, 0:P], bc[:, j % TT, 0, :], bc[:, j % TT, 1, :], start=True, stop=True)
                pe.transpose(ps[:, 6, P:2 * P], bc[:, j % TT, 0, :], ident[:, :]).then_inc(cb_mm, 1)

            def to_features(g, j):
                pe.wait_ge(y_scaled, g * 4 + (j + 1))
                after(pe, yT_done, g * 4 + j)
                for f in range(4):
                    ins = pe.transpose(ps[:, 7, f * P:(f + 1) * P], ybuf[:, j % 2, f * P:(f + 1) * P], ident[:, :])
                ins.then_inc(yT_mm, 1)

            def group(g, last):
                def z_part(tt, third):
                    if third == 0:
                        if tt == 0:
                            pe.wait_ge(lo_done, g * 2 + (n0 + 4))
                        pe.wait_ge(evac, g * 4 + (t0 + 4 + tt))
                    t = slice(tt * P, (tt + 1) * P)
                    for m in range(8 * third, 8 * third + 8):
                        kt, pss = divmod(m, 3)
                        slot, w = (n0 + kt // 4) % 2, slice((kt % 4) * 512, (kt % 4 + 1) * 512)
                        ins = mm(ps[:, 5, :], (xh, xl, xh)[pss][:, kt, t], (wh, wh, wl)[pss][:, slot, w],
                                 start=m == 0, stop=m == 23)
                    if third == 2:
                        ins.then_inc(products, 1)

                places = {0: ((), (), (0, 1, 2)), 1: ((0,), (1,), (2,)), 2: ((0,), (1,), (2,)), 3: ((0, 1), (2,), ())}
                for k in range(TT):
                    if k < 3 or not last:
                        decays(g, k + 1)

                    def z_at(place):
                        for third in () if last else places[k][place]:
                            z_part(k, third)
                    z_at(0)
                    after(pe, y_done, g * 4 + k)
                    pe.wait_ge(xdt_done, g * 12 + 3 * (k + 1))
                    if k:
                        pe.wait_ge(state_done, g * 3 + k)
                        mm(ps[:, 3, :], bc[:, k, 1, :], state[:, :], start=True, stop=True)
                    if k < 3:
                        after(pe, state_done, g * 3 + k)
                        mm(ps[:, 4, :], btst[:, k % 2, :], xdd[:, k % 2, :], start=True, stop=True
                           ).then_inc(state_mm, 1)
                    for q in range(2):
                        pe.wait_ge(m_built, g * 8 + (2 * k + q + 1))
                        for h in range(4):
                            x = slice((4 * q + h) * SP_, (4 * q + h + 1) * SP_)
                            ins = mm(ps[:, 2, x], Lx[:, k % 2, q, h, :], xdt[:, k % 2, x], start=True, stop=True)
                        ins.then_inc(y_mm, 1)
                    z_at(1)
                    if k or not isinstance(g, int) or g:
                        to_features(g, k - 1)
                    z_at(2)
            decays(0, 0)
            scan_groups(pe, group)
            to_features(SG - 1, 3)
            pe.wait_ge(yl_done, TT)
            residual("ssm_out", ys, ready=lambda: pe.wait_ge(yl_done, TT + 1))
            ffn("up1", "down1", 3)

        @block.scalar
        def _(act):
            A = act.activation

            def split_hi(n, i=None, per=0):
                act.wait_ge(landed[n % 2], 16 * (n // 2 + 1) if i is None else i * (8 * per) + 16 * (n // 2 + 1))
                if n >= 2:
                    act.wait_ge(products, at(2 * (n - 1), i, 2 * per))
                A(wh[:, n % 2, :], wraw[:, n % 2, :], ACT.Copy).then_inc(hi_done, 1)

            def square(mt, L, i, per, t):
                if L:
                    act.wait_ge(evac, at(t + mt + 1, i, per))
                if L or mt >= 2:
                    act.wait_ge(acc_done, at(8 * L + mt - 1, i, per))
                src = xT[:, mt, :] if i is None else xT[:, bass.ds(i * per + mt, 1), :].rearrange("p a n -> p (a n)")
                A(sq[:, mt % 2, :], src, ACT.Square).then_inc(sq_done, 1)

            def norm(L):
                for kt in range(KT):
                    act.wait_ge(scaled, 8 * L + kt + 1)
                    A(xh[:, kt, :], tmp[:, kt % 2, :], ACT.Copy).then_inc(xh_done, 1)

            def residual(name):
                ks, n0, t0 = RES[name], CHUNK[name], EVAC[name]
                per = 2 * len(ks)
                ahead = name in ("nsa_out", "ssm_out")

                def turn(i, shift):
                    for p in range(2):
                        for q in range(len(ks)):
                            n = n0 + p * len(ks) + q + 1 + shift * per
                            if n < NCHUNKS and not ahead:
                                split_hi(n, i, per)
                            if ahead and q < len(ks) - 1:
                                split_hi(n + 1)
                        if name in NORM:
                            for m in range(2):
                                square(2 * p + m + 4 * shift, NORM[name], i, 4, t0)
                        if ahead and n + 1 <= n0 + 2 * per:
                            split_hi(n + 1)
                if n0 + 2 * per < NCHUNKS and not ahead:
                    with act.Fori(0, 2) as i:
                        turn(i, 0)
                else:
                    turn(None, 0)
                    turn(None, 1)
                if name in NORM:
                    norm(NORM[name])

            def ffn(up, down, L):
                n0, t0, h0 = CHUNK[up], EVAC[up], FT * (L == 3)
                with act.Fori(0, FT // 2) as i:
                    split_hi(n0 + 1, i, 2)
                    for j in range(2):
                        act.wait_ge(products, i * 4 + (2 * n0 + j + 1))
                        act.wait_ge(evac, i * 2 + (t0 - 1 + j))
                        A(gate[:, j, :], ps[:, j, :], ACT.Silu).then_inc(gate_done, 1)
                    split_hi(n0 + 2, i, 2)
                    for j in range(2):
                        act.wait_ge(evac, i * 2 + (t0 + j + 1))
                        A(hh[:, bass.ds(i * 2 + j, 1), :].rearrange("p a n -> p (a n)"), hid[:, j, :], ACT.Copy
                          ).then_inc(hh_done, 1)
                residual(down)

            act.wait_ge(x_landed, 16)
            for kt in range(KT):
                square(kt, 0, None, 0, 0)
            split_hi(0)
            norm(0)
            split_hi(1)
            split_hi(2)
            for tt in range(TT):
                act.wait_ge(products, 2 * 1 + 1 + tt // 2)
                A(kvc[:, tt, :], ps[:, tt, :], ACT.Copy).then_inc(evac, 1)
            for kv in range(2):
                for gp in range(2):
                    act.wait_ge(kvT, 2 * kv + gp + 1)
                    for lp in range(2):
                        A(tb2[lp * DH:(lp + 1) * DH, kv, gp * 2 + 1, :], ps[DH:P, 4 + 2 * kv + gp, lp::2], ACT.Copy
                          ).then_inc(tb_act, 1)
            act.wait_ge(angles_done, 1)
            A(sinT[:, :, :], ang[:, 8, :].rearrange("p (t f) -> p t f", f=8), ACT.Sin).then_inc(sincos_done, 1)
            A(cosT[:, :, :], ang[:, 9, :].rearrange("p (t f) -> p t f", f=8), ACT.Sin).then_inc(sincos_done, 1)
            split_hi(3)
            split_hi(4)
            for kv in range(2):
                for ht in range(2):
                    r = 2 * kv + ht
                    act.wait_ge(hid_mm, 4)
                    src, dst = ps[:, 4, r * P:(r + 1) * P], hidK[:, ht, :]
                    if kv:
                        src = src.rearrange("p (g c) -> p g c", g=GROUPS).unsqueeze(2).broadcast_to([P, GROUPS, HP, 32])
                        dst = hidV[:, ht, :, :, :]
                    A(dst, src, ACT.Silu, bias=col(COL_B1 + r)).then_inc(hid_done, 1)
            act.wait_ge(cmp_mm, 1)
            A(kcn[:, 0, :], ps[:, 5, 0:DH], ACT.Square).then_inc(kc_sq, 1)
            act.wait_ge(evac, EVAC["qkv"])
            A(glin[:, :, :], glin[:, :, :], ACT.Exp, scale=-1.0).then_inc(gates_exp, 1)
            act.wait_ge(kcT, 1)
            A(B1c[:, :], ps[:, 7, 0:P], ACT.Copy).then_inc(kc_hi, 1)
            n0, t0 = CHUNK["qkv"], EVAC["qkv"]

            def qkv_tile(tt, g, bank):
                if g is not None:
                    act.wait_ge(v_staged, g + 1)
                    act.wait_ge(qkT, g * 6 + 6)
                A(proj[:, tt, :, :].rearrange("p h d -> p (h d)"), ps[:, bank, :], ACT.Copy).then_inc(evac, 1)
                act.wait_ge(evac, t0 + tt + 1 if g is None else g * 4 + (t0 + 4 + tt + 1))
                A(qn[:, tt, :, 0, :], proj[:, tt, 0:6, :], ACT.Square).then_inc(qk_squared, 1)

            split_hi(5)
            for tt in range(TT):
                act.wait_ge(products, 2 * n0 + 3 + tt // 2)
                qkv_tile(tt, None, tt)
            split_hi(6)

            def transposed_hi(g):
                for h in range(6):
                    act.wait_ge(qkT, g * 6 + (h + 1))
                    dst = qA[:, h, :] if h < HP else kB1[:, h - HP, :]
                    A(dst, ps[:, h, :], ACT.Copy).then_inc(qkT_hi, 1)

            def group(g, more):
                def exps(s):
                    h, i = divmod(s, TT)
                    w, m = (i + 1) * P, 8 * (s % 2)
                    act.wait_ge(negmax, g * 16 + (s + 1))
                    if s >= 2:
                        act.wait_ge(pT_mm, g * 16 + (s - 1))
                    for b in range(2):
                        A(Pm[:, s % 2, b, 0:w], ps[:, 2 * (s % 2) + b, 0:w], ACT.Exp, bias=sm[:, 4, m + 2 + b:m + 3 + b],
                          scale=SCALE, accum_out=sm[:, 4, m + 4 + b:m + 5 + b]).then_inc(expd, 1)

                def pT_copy(s):
                    h, i = divmod(s, TT)
                    act.wait_ge(pT_mm, g * 16 + (s + 1))
                    if i == 0 and h >= 2:
                        act.wait_ge(pv_done, g * 4 + (h - 1))
                    A(PT[:, h % 2, :, 0:i + 1, i * P:(i + 1) * P],
                      ps[:, 4:6, 0:(i + 1) * P].rearrange("p b (j q) -> p b j q", q=P), ACT.Copy).then_inc(pT_done, 1)

                def o_copy(pr):
                    act.wait_ge(pv_done, g * 4 + 2 * (pr + 1))
                    A(xo[:, bass.ds(g * 2 + pr, 1), :].rearrange("p a n -> p (a n)"), ps[:, 6, :], ACT.Copy
                      ).then_inc(o_hi, 1)

                for k in range(18):
                    if 1 <= k <= 16:
                        exps(k - 1)
                    if k >= 2:
                        pT_copy(k - 2)
                    if k == 1:
                        act.wait_ge(cs_shifted, g + 1)
                        A(pc[:, :, :, :], pc[:, :, :, :], ACT.Exp, scale=SCALE).then_inc(cs_exp, 1)
                    if k == 4:
                        act.wait_ge(pcT_mm, g + 1)
                        A(pcT[:, :], ps[:, 6, :], ACT.Copy).then_inc(pcT_done, 1)
                    if k == 11:
                        o_copy(0)
                    if more and k in (3, 6, 9, 12):
                        tt = k // 3 - 1
                        act.wait_ge(products, g * 4 + (2 * (n0 + 2) + tt + 1))
                        qkv_tile(tt, g, 7)
                    if more and k in (14, 15):
                        act.wait_ge(products, g * 4 + 2 * (n0 + 4))
                        split_hi(n0 + 4 + k - 14, g, 2)
                if more:
                    transposed_hi(g + 1)
                o_copy(1)

            transposed_hi(0)
            with act.Fori(0, GROUPS - 1) as g:
                group(g, True)
            group(GROUPS - 1, False)
            act.wait_ge(o_lo, 2 * GROUPS)
            act.dma_start(xT[:, :, :], xT_in).then_inc(x_again, 16)
            residual("nsa_out")
            ffn("up0", "down0", 1)

            n0, t0 = CHUNK["xbc"], EVAC["xbc"]

            def conv_tiles(n, i, t, u, dst, first_T, tok):
                def silu(j):
                    act.wait_ge(evac, at(t + j + 1, i, 4))
                    if tok:
                        act.wait_ge(featT, at(max(first_T + j - 1, 0), i, 4))
                    c = col(COL_CB + u + j) if i is None else cols[:, bass.ds(i * 4 + (COL_CB + u + j), 1)]
                    A(dst(j), tmp[:, j % 2, :], ACT.Silu, bias=c).then_inc(silu_done, 1)

                def to_tokens(j):
                    if tok:
                        act.wait_ge(featT, at(first_T + j + 1, i, 4))
                        A(tok(j), ps[:, 4 + j % 2, :].rearrange("p (t f) -> p t f", f=P), ACT.Copy
                          ).then_inc(featT_done, 1)
                split_hi(n + 1, i, 2)
                silu(0)
                silu(1)
                split_hi(n + 2, i, 2)
                to_tokens(0)
                silu(2)
                to_tokens(1)
                silu(3)
                to_tokens(2)
                to_tokens(3)
            conv_tiles(n0, None, t0, 20, lambda j: BCf[:, 1, j, :], 0, None)
            conv_tiles(n0 + 2, None, t0 + 4, 16, lambda j: BCf[:, 0, j, :], 0, None)
            with act.Fori(0, 4) as i:
                conv_tiles(n0 + 4, i, t0 + 8, 0, lambda j: sq[:, j % 2, :], 0,
                           lambda j: xtok[:, :, bass.ds(i * 512 + j * P, P)])
            split_hi(CHUNK["z"])
            act.wait_ge(dt_in, 1)
            A(dtb[:, 2, :], dtb[:, 1, :], ACT.Exp, scale=-1.0).then_inc(dt_e, 1)
            A(dtb[:, 9, 0:SH], rows[:, ROW_AL:ROW_AL + SH], ACT.Exp).then_inc(a_exp, 1)
            act.wait_ge(dt_u, 1)
            A(dtb[:, 7, :], dtb[:, 3, :], ACT.Ln).then_inc(dt_ln, 1)
            n0, t0 = CHUNK["z"], EVAC["z"]
            split_hi(n0 + 1)
            for tt in range(TT):
                act.wait_ge(products, 2 * n0 + 3 + tt // 2)
                A(zs[:, tt, :], ps[:, tt, :], ACT.Silu).then_inc(evac, 1)
            act.wait_ge(cum_mm, 1)
            A(ex[:, :, :], ps[:, 6, 0:3 * P].rearrange("p (k h) -> p k h", k=3), ACT.Exp).then_inc(cum_exp, 1)

            def stage(g, j):
                c = j % TT
                after(act, y_mm, g * 8 + 2 * (j - 3))
                A(bc[:, c, :, :], BCf[:, :, bass.ds(g + j // TT, 1), c * P:(c + 1) * P].rearrange("p b a n -> p (b a) n"),
                  ACT.Copy).then_inc(staged, 1)

            def decays(g, j):
                for q in range(2):
                    act.wait_ge(seg_mm, g * 8 + (2 * j + q + 1))
                    after(act, y_mm, g * 8 + 2 * (j - 1))
                    A(Lx[:, j % 2, q, :, :], ps[:, q, :].rearrange("p (h t) -> p h t", h=4), ACT.Exp
                      ).then_inc(seg_exp, 1)

            def z_copy(g, tt):
                act.wait_ge(products, g * 4 + (2 * n0 + 4 + tt + 1))
                A(zraw[:, tt % TT, :], ps[:, 5, :], ACT.Copy).then_inc(evac, 1)

            def group(g, last):
                first = isinstance(g, int) and g == 0
                for k in range(TT):
                    if k:
                        if not last:
                            z_copy(g, k - 1)
                    elif not first:
                        z_copy(g, -1)
                    if k == 0:
                        act.wait_ge(products, g * 4 + (2 * n0 + 4))
                        split_hi(n0 + 2, g, 2)
                    if k < 3 or not last:
                        decays(g, k + 1)
                    if k < 2 or not last:
                        stage(g, k + 2)
                    if k == 0:
                        if not first:
                            act.wait_ge(evac, g * 4 + (t0 + 4))
                            act.wait_ge(y_done, g * 4)
                            A(zs[:, :, :], zraw[:, :, :], ACT.Silu).then_inc(z_silu, 1)
                        split_hi(n0 + 3, g, 2)
                    if last:
                        act.wait_ge(yT_done, 9 + k)
                        A(yh[:, k, 0:12, :], yT[:, k, 0:12, :], ACT.Copy).then_inc(yh_done, 1)
                    act.wait_ge(y_done, g * 4 + (k + 1))
                    after(act, y_sq, g * 4 + k)
                    A(ysq[:, :], ybuf[:, k % 2, :], ACT.Square, accum_out=yst[:, k % 2, 0:1]).then_inc(y_sq, 1)
            stage(0, 0)
            stage(0, 1)
            decays(0, 0)
            scan_groups(act, group)
            act.wait_ge(yT_done, 4 * SG)
            A(yh[:, :, 12:16, :], yT[:, :, 12:16, :], ACT.Copy).then_inc(yh_done, 1)
            residual("ssm_out")
            ffn("up1", "down1", 3)

        @block.vector
        def _(dve):
            V = Tally(vec)
            TTo, TS, STT = dve.tensor_tensor, dve.tensor_scalar, dve.scalar_tensor_tensor

            def step(ins):
                V.inc(ins)
                V.wait(dve)

            def split_lo(n, i=None, per=0):
                s = n % 2
                dve.wait_ge(hi_done, at(n + 1, i, per))
                TTo(wl[:, s, :], wraw[:, s, :], wh[:, s, :].bitcast(F32), ALU.subtract).then_inc(lo_done, 1)

            def norm(L):
                dve.wait_ge(colsum_done, L + 1)
                TS(stat[:, 0:4], ps[:, 7, 0:4], 1.0 / DM, EPS, ALU.mult, ALU.add).then_inc(mean_done, 1)
                dve.wait_ge(rstd_done, L + 1)
                for tt in range(TT):
                    ins = TS(diag[:, tt, :], ident[:, :], stat[:, 4 + tt:5 + tt], None, ALU.mult)
                ins.then_inc(diag_done, 1)
                dve.wait_ge(rbc_done, L + 1)

                def scale(kt):
                    if kt >= 2:
                        dve.wait_ge(xl_done, 8 * L + kt - 1)
                    STT(out=tmp[:, kt % 2, :], in0=xT[:, kt, :], scalar=col(NORMCOL[L] + kt), in1=ps[:, 6, :],
                        op0=ALU.mult, op1=ALU.mult).then_inc(scaled, 1)
                scale(0)
                for kt in range(KT):
                    if kt + 1 < KT:
                        scale(kt + 1)
                    dve.wait_ge(xh_done, 8 * L + kt + 1)
                    TTo(xl[:, kt, :], tmp[:, kt % 2, :], xh[:, kt, :].bitcast(F32), ALU.subtract).then_inc(xl_done, 1)

            def residual(name):
                ks, n0, t0 = RES[name], CHUNK[name], EVAC[name]
                per = 2 * len(ks)
                ahead = name in ("nsa_out", "ssm_out")

                def turn(i, shift):
                    for p in range(2):
                        for q in range(len(ks)):
                            n = n0 + p * len(ks) + q + 1 + shift * per
                            if n < NCHUNKS and not ahead:
                                split_lo(n, i, per)
                            if ahead and q < len(ks) - 1:
                                split_lo(n + 1)
                        for m in range(2):
                            t = 2 * p + m + 4 * shift
                            last = n0 + (p + 1) * len(ks) - 1 + shift * per
                            dve.wait_ge(products, at(2 * last + m + 1, i, 2 * per))
                            x = xT[:, t, :] if i is None else xT[:, bass.ds(i * 4 + t, 1), :].rearrange(
                                "p a n -> p (a n)")
                            TTo(x, ps[:, 2 * p + m, :], x, ALU.add).then_inc(evac, 1)
                        if ahead and n + 1 <= n0 + 2 * per:
                            split_lo(n + 1)
                if n0 + 2 * per < NCHUNKS and not ahead:
                    with dve.Fori(0, 2) as i:
                        turn(i, 0)
                else:
                    turn(None, 0)
                    turn(None, 1)
                if name in NORM:
                    norm(NORM[name])

            def ffn(up, down, L):
                n0, t0, h0 = CHUNK[up], EVAC[up], FT * (L == 3)
                with dve.Fori(0, FT // 2) as i:
                    split_lo(n0 + 1, i, 2)
                    split_lo(n0 + 2, i, 2)
                    for j in range(2):
                        dve.wait_ge(gate_done, i * 2 + (h0 + j + 1))
                        dve.wait_ge(products, i * 4 + (2 * n0 + 3 + j))
                        TTo(hid[:, j, :], gate[:, j, :], ps[:, 2 + j, :], ALU.mult).then_inc(evac, 1)
                        dve.wait_ge(hh_done, i * 2 + (h0 + j + 1))
                        h = bass.ds(i * 2 + j, 1)
                        TTo(hl[:, h, :].rearrange("p a n -> p (a n)"), hid[:, j, :],
                            hh[:, h, :].rearrange("p a n -> p (a n)").bitcast(F32), ALU.subtract).then_inc(hl_done, 1)
                residual(down)

            dve.wait_ge(params_landed, 64)
            split_lo(0)
            dve.tensor_copy(ident_bf[:, :], ident[:, :]).then_inc(masks_cast, 1)
            step(TTo(diag[:, 0, :], tri[:, 1, :], ident[:, :], ALU.add))
            TS(negmask_bf[:, :], diag[:, 0, :], -NEG, NEG, ALU.mult, ALU.add).then_inc(masks_cast, 1)
            norm(0)
            split_lo(1)
            split_lo(2)
            for kv in range(2):
                for gp in range(2):
                    dve.wait_ge(kvT, 2 * kv + gp + 1)
                    for lp in range(2):
                        dve.tensor_copy(tb2[lp * DH:(lp + 1) * DH, kv, gp * 2, :], ps[0:DH, 4 + 2 * kv + gp, lp::2]
                                        ).then_inc(tb_vec, 1)
            dve.wait_ge(tb_vec, 8)
            dve.wait_ge(tb_act, 8)
            V.inc(dve.memset(tbT[:, :, :, :, :].rearrange("p k j g c -> p (k j g) c")[:, :, NCMP:32], 0.0))
            for kv in range(2):
                for jh in range(2):
                    src = tb2[:, kv, :, 8 * jh:8 * jh + 248].rearrange("p g (c j) -> p j g c", j=8)
                    pe_ = col(COL_PE + kv * NJ + 8 * jh, 8).unsqueeze(2).unsqueeze(3).broadcast_to([P, 8, GROUPS, NCMP])
                    TTo(tbT[:, kv, 8 * jh:8 * jh + 8, :, 0:NCMP], src, pe_, ALU.add).then_inc(tbT_done, 1)
            dve.wait_ge(rest_landed, 32)
            step(dve.tensor_copy(stat[:, 16:21], posi[:, :]))
            a0 = ang[:, 0, :].rearrange("p (t f) -> p t f", f=8)
            step(TTo(a0, stat[:, 16:21].unsqueeze(2).broadcast_to([P, 5, 8]),
                     rows[:, ROW_INV:ROW_INV + 8].unsqueeze(1).broadcast_to([P, 5, 8]), ALU.mult))
            magic = 1.5 * 2.0 ** 23
            step(TS(ang[:, 1, :], ang[:, 0, :], float(1 / (2 * np.pi)), magic, ALU.mult, ALU.add))
            step(TS(ang[:, 2, :], ang[:, 1, :], magic, None, ALU.subtract))
            c1 = 6.28125
            c2 = float(np.float32(np.round((2 * np.pi - c1) * 2.0 ** 21) / 2.0 ** 21))
            c3 = float(np.float32(2 * np.pi - c1 - c2))
            for n, cc in enumerate((c1, c2, c3)):
                step(STT(out=ang[:, 3 + n, :], in0=ang[:, 2, :], scalar=-cc, in1=ang[:, 0 if n == 0 else 2 + n, :],
                         op0=ALU.mult, op1=ALU.add))
            step(TS(ang[:, 8, :], ang[:, 5, :], PI, -PI, ALU.min, ALU.max))
            step(TS(ang[:, 6, :], ang[:, 5, :], float(np.pi / 2), None, ALU.add))
            step(TS(ang[:, 7, :], ang[:, 6, :], PI, float(-2 * np.pi), ALU.is_gt, ALU.mult))
            step(TTo(ang[:, 6, :], ang[:, 6, :], ang[:, 7, :], ALU.add))
            TS(ang[:, 9, :], ang[:, 6, :], PI, -PI, ALU.min, ALU.max).then_inc(angles_done, 1)
            split_lo(3)
            split_lo(4)
            for tt in range(TT):
                dve.wait_ge(products, 2 * CHUNK["gates"] + 1 + tt // 2)
                dve.tensor_copy(glin[:, tt, :], ps[:, tt, 0:48]).then_inc(evac, 1)
            dve.wait_ge(kc_sq, 1)
            step(dve.tensor_reduce(stat[:, 8:9], kcn[:, 0, :], AX, ALU.add))
            TS(stat[:, 9:10], stat[:, 8:9], 1.0 / DH, EPS, ALU.mult, ALU.add).then_inc(kc_mean, 1)
            dve.tensor_copy(VC4[:, :, :], ps[:, 6, 0:GROUPS * DH].rearrange("p (g d) -> p g d", g=GROUPS)
                            ).then_inc(vc_done, 1)
            dve.wait_ge(kc_rstd, 1)
            step(STT(out=kcn[:, 0, :], in0=ps[:, 5, 0:DH], scalar=stat[:, 11:12], in1=rows[:, ROW_KC:ROW_KC + DH],
                     op0=ALU.mult, op1=ALU.mult))
            dve.wait_ge(sincos_done, 2)
            c_, s_ = cosT[:, 4, :], sinT[:, 4, :]
            x1, x2 = kcn[:, 0, 0:8], kcn[:, 0, 8:16]
            V.inc(TTo(krp[:, 0, :], x1, c_, ALU.mult))
            V.inc(TTo(krp[:, 1, :], x2, s_, ALU.mult))
            V.inc(TTo(krp[:, 2, :], x2, c_, ALU.mult))
            step(TTo(krp[:, 3, :], x1, s_, ALU.mult))
            step(TTo(x1, krp[:, 0, :], krp[:, 1, :], ALU.subtract))
            step(TTo(x2, krp[:, 2, :], krp[:, 3, :], ALU.add))
            dve.tensor_copy(kcn[:, 1, :], kcn[:, 0, :]).then_inc(kcn_done, 1)
            dve.wait_ge(gates_exp, 1)
            step(TS(glin[:, :, :], glin[:, :, :], 1.0, None, ALU.add))
            dve.reciprocal(glin[:, :, :], glin[:, :, :]).then_inc(gates_done, 1)
            dve.wait_ge(kc_hi, 1)
            TTo(B2c[:, :], ps[:, 7, 0:P], B1c[:, :].bitcast(F32), ALU.subtract).then_inc(kc_lo, 1)
            dve.wait_ge(gates_done, 1)
            n0 = CHUNK["qkv"]

            def qk_norm(tt, g):
                dve.wait_ge(qk_squared, g * 4 + (tt + 1))
                step(dve.tensor_reduce(sm[:, 0, 0:6], qn[:, tt, :, 0, :], AX, ALU.add))
                TS(sm[:, 1, 0:6], sm[:, 0, 0:6], 1.0 / DH, EPS, ALU.mult, ALU.add).then_inc(qk_mean, 1)
                dve.wait_ge(qk_rstd, g * 4 + (tt + 1))
                q6 = qn[:, tt, :, 0, :]
                step(TTo(q6, proj[:, tt, 0:6, :], sm[:, 3, 0:6].unsqueeze(2).broadcast_to([P, 6, DH]), ALU.mult))
                step(TTo(q6, q6, rows[:, ROW_W6:ROW_W6 + 384].rearrange("p (h d) -> p h d", d=DH), ALU.mult))
                cc = cosT[:, tt, :].unsqueeze(1).broadcast_to([P, 6, 8])
                ss = sinT[:, tt, :].unsqueeze(1).broadcast_to([P, 6, 8])
                x1, x2 = q6[:, :, 0:8], q6[:, :, 8:16]
                V.inc(TTo(rp[:, 0], x1, cc, ALU.mult))
                V.inc(TTo(rp[:, 1], x2, ss, ALU.mult))
                V.inc(TTo(rp[:, 2], x2, cc, ALU.mult))
                step(TTo(rp[:, 3], x1, ss, ALU.mult))
                V.inc(TTo(x1, rp[:, 0], rp[:, 1], ALU.subtract))
                step(TTo(x2, rp[:, 2], rp[:, 3], ALU.add))
                dve.tensor_copy(qn[:, tt, :, 1, :], q6).then_inc(qk_normed, 1)

            def transposed_lo(g):
                for h in range(6):
                    dve.wait_ge(qkT_hi, g * 6 + (h + 1))
                    if h < HP:
                        lo = qA[DH:P, h, :]
                        TTo(lo, ps[DH:P, h, :], lo.bitcast(F32), ALU.subtract).then_inc(qkT_lo, 1)
                    else:
                        TTo(kB2[:, h - HP, :], ps[:, h, :], kB1[:, h - HP, :].bitcast(F32), ALU.subtract
                            ).then_inc(qkT_lo, 1)

            def group(g, more):
                def stage_v():
                    dve.wait_ge(vz_zeroed, 1)
                    dve.wait_ge(pv_done, g * 4)
                    dve.tensor_copy(vst[:, :, :, :], proj[:, :, 6:8, :]).then_inc(v_staged, 1)
                    for h in range(HP):
                        b = slice(32 * h, 32 * (h + 1))
                        dve.tensor_copy(vz[b, h, :], VC4[b, bass.ds(g, 1), :].rearrange("p a d -> p (a d)")
                                        ).then_inc(vz_done, 1)

                pf = pc[:, :, :, :].rearrange("p t h c -> p (t h) c")
                gt = glin[:, :, bass.ds(g * 12, 12)].rearrange("p t (h b) -> p t h b", b=3)

                def cmp_shift():
                    dve.wait_ge(cs_mm, g + 1)
                    step(TTo(pc[:, :, :, :], ps[:, 6, :].rearrange("p (t h c) -> p t h c", t=TT, h=HP),
                             cmask[:, 0].unsqueeze(2).broadcast_to([P, TT, HP, 32]), ALU.add))
                    step(dve.tensor_reduce(sm[:, 0, 8:24], pf, AX, ALU.max))
                    TTo(pf, pf, sm[:, 0, 8:24].unsqueeze(2).broadcast_to([P, 16, 32]), ALU.subtract
                        ).then_inc(cs_shifted, 1)

                def cmp_probs():
                    dve.wait_ge(cs_exp, g + 1)
                    step(dve.tensor_reduce(sm[:, 1, 8:24], pf, AX, ALU.add))
                    step(dve.reciprocal(sm[:, 2, 8:24], sm[:, 1, 8:24]))
                    step(TTo(sm[:, 3, 8:24].rearrange("p (t h) -> p t h", t=TT),
                             sm[:, 2, 8:24].rearrange("p (t h) -> p t h", t=TT), gt[:, :, :, 0], ALU.mult))
                    step(TTo(pf, pf, sm[:, 3, 8:24].unsqueeze(2).broadcast_to([P, 16, 32]), ALU.mult))
                    TTo(pc[:, :, :, :], pc[:, :, :, :], cmask[:, 1].unsqueeze(2).broadcast_to([P, TT, HP, 32]), ALU.mult
                        ).then_inc(pc_done, 1)

                def maxima(s):
                    h, i = divmod(s, TT)
                    m = 8 * (s % 2)
                    dve.wait_ge(scores, g * 16 + (s + 1))
                    step(dve.tensor_reduce(sm[:, 4, m:m + 2], ps[:, 2 * (s % 2):2 * (s % 2) + 2, 0:(i + 1) * P], AX,
                                           ALU.max))
                    TS(sm[:, 4, m + 2:m + 4], sm[:, 4, m:m + 2], -SCALE, None, ALU.mult).then_inc(negmax, 1)

                def normalize(s):
                    h, i = divmod(s, TT)
                    m = 8 * (s % 2)
                    dve.wait_ge(expd, g * 32 + 2 * (s + 1))
                    step(dve.reciprocal(sm[:, 5, m:m + 2], sm[:, 4, m + 4:m + 6]))
                    step(TTo(sm[:, 5, m + 2:m + 4], sm[:, 5, m:m + 2], gt[:, i, h, 1:3], ALU.mult))
                    for b in range(2):
                        p_ = Pm[:, s % 2, b, 0:(i + 1) * P]
                        TS(p_, p_, sm[:, 5, m + 2 + b:m + 3 + b], None, ALU.mult).then_inc(normed, 1)

                def o_rest(pr):
                    dve.wait_ge(o_hi, g * 2 + (pr + 1))
                    o = bass.ds(g * 2 + pr, 1)
                    TTo(xol[:, o, :].rearrange("p a n -> p (a n)"), ps[:, 6, :],
                        xo[:, o, :].rearrange("p a n -> p (a n)").bitcast(F32), ALU.subtract).then_inc(o_lo, 1)

                for k in range(18):
                    if k < 16:
                        maxima(k)
                    if 1 <= k <= 16:
                        normalize(k - 1)
                    if k == 0:
                        stage_v()
                        cmp_shift()
                    if k == 1:
                        cmp_probs()
                    if k == 12:
                        o_rest(0)
                    if more and k in (4, 7, 10, 13):
                        qk_norm(k // 3 - 1, g + 1)
                    if more and k in (14, 15):
                        split_lo(n0 + 4 + k - 14, g, 2)
                if more:
                    transposed_lo(g + 1)
                o_rest(1)

            split_lo(5)
            for tt in range(TT):
                qk_norm(tt, 0)
            split_lo(6)
            transposed_lo(0)
            with dve.Fori(0, GROUPS - 1) as g:
                V.enter(g, DVE_GROUP_STEPS)
                group(g, True)
            V.leave(GROUPS - 1, DVE_GROUP_STEPS)
            group(GROUPS - 1, False)
            dve.wait_ge(x_again, 16)
            residual("nsa_out")
            ffn("up0", "down0", 1)

            n0, t0 = CHUNK["xbc"], EVAC["xbc"]

            def conv_tiles(n, i, t, u):
                def taps(j):
                    dve.wait_ge(products, at(2 * (n + j // 2) + j % 2 + 1, i, 4))
                    if i is not None or t + j >= t0 + 2:
                        dve.wait_ge(silu_done, at(t - t0 + j - 1, i, 4))

                    def w(tap):
                        c0 = COL_CW + tap * 24 + u + j
                        return col(c0) if i is None else cols[:, bass.ds(i * 4 + c0, 1)]
                    c = tmp[:, j % 2, :]
                    step(TS(c, ps[:, j, :], w(3), None, ALU.mult))
                    for d in range(1, 4):
                        ins = STT(out=c[:, d:], in0=ps[:, j, 0:SEQ - d], scalar=w(3 - d), in1=c[:, d:],
                                  op0=ALU.mult, op1=ALU.add)
                        if d < 3:
                            step(ins)
                        else:
                            ins.then_inc(evac, 1)
                split_lo(n + 1, i, 2)
                taps(0)
                taps(1)
                split_lo(n + 2, i, 2)
                taps(2)
                taps(3)
            conv_tiles(n0, None, t0, 20)
            conv_tiles(n0 + 2, None, t0 + 4, 16)
            with dve.Fori(0, 4) as i:
                V.enter(i, 12)
                conv_tiles(n0 + 4, i, t0 + 8, 0)
            V.leave(4, 12)
            split_lo(CHUNK["z"])
            bias = rows[:, ROW_DTB:ROW_DTB + SH]
            for tt in range(TT):
                dve.wait_ge(products, 2 * CHUNK["dt"] + 1 + tt // 2)
                TTo(dtb[:, 0, tt * SH:(tt + 1) * SH], ps[:, tt, 0:SH], bias, ALU.add).then_inc(evac, 1)
            dve.wait_ge(evac, EVAC["z"])
            step(TS(dtb[:, 4, :], dtb[:, 0, :], -1.0, None, ALU.mult))
            TTo(dtb[:, 1, :], dtb[:, 0, :], dtb[:, 4, :], ALU.max).then_inc(dt_in, 1)
            dve.wait_ge(dt_e, 1)
            TS(dtb[:, 3, :], dtb[:, 2, :], 1.0, None, ALU.add).then_inc(dt_u, 1)
            dve.wait_ge(dt_u, 1)
            step(TS(dtb[:, 4, :], dtb[:, 3, :], 1.0, None, ALU.subtract))
            step(TS(dtb[:, 5, :], dtb[:, 4, :], 0.0, None, ALU.is_equal))
            step(TTo(dtb[:, 4, :], dtb[:, 4, :], dtb[:, 5, :], ALU.add))
            step(dve.reciprocal(dtb[:, 6, :], dtb[:, 4, :]))
            dve.wait_ge(dt_ln, 1)
            step(TTo(dtb[:, 7, :], dtb[:, 7, :], dtb[:, 6, :], ALU.mult))
            step(TTo(dtb[:, 7, :], dtb[:, 7, :], dtb[:, 5, :], ALU.add))
            step(TTo(dtb[:, 7, :], dtb[:, 7, :], dtb[:, 2, :], ALU.mult))
            step(STT(out=dtb[:, 0, :], in0=dtb[:, 0, :], scalar=0.0, in1=dtb[:, 7, :], op0=ALU.max, op1=ALU.add))
            dve.wait_ge(a_exp, 1)
            STT(out=dtb[:, 1, :].rearrange("p (t h) -> p t h", t=TT), in0=dtb[:, 0, :].rearrange("p (t h) -> p t h", t=TT),
                scalar=-1.0, in1=dtb[:, 9, 0:SH].unsqueeze(1).broadcast_to([P, TT, SH]), op0=ALU.mult, op1=ALU.mult
                ).then_inc(dt_done, 1)
            dve.wait_ge(dt_done, 1)
            n0 = CHUNK["z"]
            split_lo(n0 + 1)
            dve.wait_ge(cum_exp, 1)

            def build_g(g, j):
                for q in range(2):
                    after(dve, seg_mm, g * 8 + (2 * j + q - 1))
                    at_ = g * SHP + ((j // TT) * SHP + (j % TT) * SH + 4 * q)
                    TTo(Gm[:, q, :, :], tri[:, 0, :].unsqueeze(1).broadcast_to([P, 4, P]),
                        dtb[:, 1, bass.ds(at_, 4)].unsqueeze(2).broadcast_to([P, 4, P]), ALU.mult).then_inc(g_built, 1)

            def stage(g, j):
                dve.wait_ge(cb_mm, g * 4 + (j + 1))
                after(dve, m_built, g * 8 + 2 * (j - 1))
                TTo(cbm[:, j % 2, :], ps[:, 6, 0:P], tri[:, 0, :], ALU.mult)
                after(dve, y_mm, g * 8 + 2 * (j - 1))
                dve.tensor_copy(btst[:, j % 2, :], ps[:, 6, P:2 * P]).then_inc(cb_done, 1)

            def mean_square(g, j):
                dve.wait_ge(y_sq, g * 4 + (j + 1))
                TS(yst[:, j % 2, 1:2], yst[:, j % 2, 0:1], 1.0 / GW, EPS, ALU.mult, ALU.add).then_inc(y_var, 1)

            def scale_y(g, j):
                dve.wait_ge(y_rs, g * 4 + (j + 1))
                y = ybuf[:, j % 2, :]
                TS(y, y, yst[:, j % 2, 2:3], None, ALU.mult).then_inc(y_scaled, 1)

            def to_features(g, j):
                dve.wait_ge(yT_mm, g * 4 + (j + 1))
                f = g * 4 + (j // TT) * 4
                w = cols[:, bass.ds(g * 4 + (COL_SSMN + (j // TT) * 4), 4)].unsqueeze(2).broadcast_to([P, 4, P])
                TTo(yT[:, j % TT, bass.ds(f, 4), :], ps[:, 7, :].rearrange("p (k n) -> p k n", k=4), w, ALU.mult
                    ).then_inc(yT_done, 1)

            def heads(ap):
                return ap.rearrange("p (h d) -> p h d", h=SHP)

            def group(g, last):
                first = isinstance(g, int) and g == 0

                def per_head(n, c):
                    return ex[:, n, bass.ds(g * SHP + c * SH, SHP)].unsqueeze(2).broadcast_to([P, SHP, SP_])
                for k in range(TT):
                    if k or not first:
                        mean_square(g, k - 1)
                    if k < 3 or not last:
                        stage(g, k + 1)
                    if k or not first:
                        scale_y(g, k - 1)
                    if k < 2 or not last:
                        build_g(g, k + 2)
                    if k == 0:
                        split_lo(n0 + 2, g, 2)
                        split_lo(n0 + 3, g, 2)
                    y = ybuf[:, k % 2, :]
                    after(dve, yT_mm, g * 4 + (k - 1))
                    if k < 3:
                        dve.wait_ge(state_mm, g * 3 + (k + 1))
                    if k:
                        dve.wait_ge(y_mm, g * 8 + (2 * k + 1))
                        V.inc(TTo(heads(y), heads(ps[:, 3, :]), per_head(0, k), ALU.mult))
                    if k in (1, 2):
                        step(TTo(heads(state[:, :]), heads(state[:, :]), per_head(2, k), ALU.mult))
                        TTo(state[:, :], state[:, :], ps[:, 4, :], ALU.add).then_inc(state_done, 1)
                    if k == 0:
                        dve.tensor_copy(state[:, :], ps[:, 4, :]).then_inc(state_done, 1)
                    dve.wait_ge(y_mm, g * 8 + 2 * (k + 1))
                    dve.wait_ge(xdt_done, g * 12 + 3 * (k + 1))
                    V.wait(dve)
                    step(TTo(y, y if k else dxs[:, k % 2, :], ps[:, 2, :], ALU.add))
                    if k:
                        step(TTo(y, y, dxs[:, k % 2, :], ALU.add))
                    if k == 0 and not first:
                        dve.wait_ge(z_silu, g)
                    TTo(y, y, zs[:, k, :], ALU.mult).then_inc(y_done, 1)
                    if k or not first:
                        to_features(g, k - 1)
                    if last:
                        dve.wait_ge(yh_done, k + 1)
                        dve.wait_ge(yT_done, 9 + k)
                        TTo(yl[:, k, 0:12, :], yT[:, k, 0:12, :], yh[:, k, 0:12, :].bitcast(F32), ALU.subtract
                            ).then_inc(yl_done, 1)
            build_g(0, 0)
            build_g(0, 1)
            stage(0, 0)
            scan_groups(dve, group, lambda i: V.enter(i, DVE_SCAN_STEPS), lambda: V.leave(SG - 2, DVE_SCAN_STEPS))
            mean_square(SG - 1, 3)
            scale_y(SG - 1, 3)
            to_features(SG - 1, 3)
            dve.wait_ge(yh_done, TT + 1)
            TTo(yl[:, :, 12:16, :], yT[:, :, 12:16, :], yh[:, :, 12:16, :].bitcast(F32), ALU.subtract).then_inc(yl_done, 1)
            residual("ssm_out")
            ffn("up1", "down1", 3)

        @block.gpsimd
        def _(pool):
            TTo = pool.tensor_tensor

            def rstd(dst, src, ready, value, done):
                pool.wait_ge(ready, value)
                n = src.shape[-1]
                TTo(dst, src, mhalf[:, 0:n], ALU.pow).then_inc(done, 1)
            pool.memset(mhalf[:, :], -0.5).then_inc(mhalf_set, 1)
            pool.wait_ge(mhalf_set, 1)

            def square_sum(L, loop):
                if L:
                    pool.wait_ge(colsum_done, L)
                pool.memset(sqacc[:, :], 0.0).then_inc(zeroed, 1)
                pool.wait_ge(zeroed, L + 1)

                def add(mt, i):
                    pool.wait_ge(sq_done, at(8 * L + mt + 1, i, 2))
                    pool.wait_ge(acc_done, at(8 * L + mt, i, 2))
                    TTo(sqacc[:, :], sqacc[:, :], sq[:, mt % 2, :], ALU.add).then_inc(acc_done, 1)
                with pool.Fori(0, 4) as i:
                    add(0, i)
                    add(1, i)
                rstd(stat[:, 4:8], stat[:, 0:4], mean_done, L + 1, rstd_done)
            square_sum(0, False)
            pool.wait_ge(xl_done, 8)
            pool.memset(vz[:, :, :], 0.0).then_inc(vz_zeroed, 1)
            pool.wait_ge(vz_zeroed, 1)
            rstd(stat[:, 11:12], stat[:, 9:10], kc_mean, 1, kc_rstd)
            for n in range(4):
                rstd(sm[:, 3, 0:6], sm[:, 1, 0:6], qk_mean, n + 1, qk_rstd)
            with pool.Fori(0, GROUPS - 1) as g:
                for n in range(4):
                    rstd(sm[:, 3, 0:6], sm[:, 1, 0:6], qk_mean, g * 4 + (n + 5), qk_rstd)
            pool.wait_ge(o_lo, 2 * GROUPS)
            square_sum(1, True)
            square_sum(2, True)
            pool.wait_ge(cum_exp, 1)

            def heads(ap):
                return ap.rearrange("p (h d) -> p h d", h=SHP)

            def inputs(g, j):
                c, b = j % TT, j % 2
                x = xtok[:, c, bass.ds(g * GW + (j // TT) * GW, GW)].rearrange("p (h d) -> p h d", d=SP_)
                hd = g * SHP + (j // TT) * SHP

                def per_head(row):
                    return row.unsqueeze(2).broadcast_to([P, SHP, SP_])
                after(pool, y_mm, g * 8 + 2 * (j - 1))
                after(pool, y_done, g * 4 + (j - 1))
                TTo(heads(xdt[:, b, :]), x, per_head(dtb[:, 0, bass.ds(hd + c * SH, SHP)]), ALU.mult).then_inc(xdt_done, 1)
                TTo(heads(dxs[:, b, :]), x, per_head(rows[:, bass.ds(hd + ROW_D, SHP)]), ALU.mult).then_inc(xdt_done, 1)
                pool.wait_ge(xdt_done, g * 12 + (3 * j + 1))
                TTo(heads(xdd[:, b, :]), heads(xdt[:, b, :]), per_head(ex[:, 1, bass.ds(hd + c * SH, SHP)]), ALU.mult
                    ).then_inc(xdt_done, 1)
                pool.wait_ge(cb_done, g * 4 + (j + 1))
                for q in range(2):
                    pool.wait_ge(seg_exp, g * 8 + (2 * j + q + 1))
                    TTo(Lx[:, b, q, :, :], Lx[:, b, q, :, :], cbm[:, b, :].unsqueeze(1).broadcast_to([P, 4, P]),
                        ALU.mult).then_inc(m_built, 1)

            def group(g, last):
                for k in range(TT):
                    if k or not isinstance(g, int) or g:
                        rstd(yst[:, (k - 1) % 2, 2:3], yst[:, (k - 1) % 2, 1:2], y_var, g * 4 + k, y_rs)
                    if k < 3 or not last:
                        inputs(g, k + 1)
            inputs(0, 0)
            scan_groups(pool, group)
            rstd(yst[:, 1, 2:3], yst[:, 1, 1:2], y_var, 4 * SG, y_rs)
            square_sum(3, True)


def kernel(x, positions, mix_norm_w, ffn_norm_w, ffn_w_gate, ffn_w_up, ffn_w_down, nsa_w_in, nsa_q_norm, nsa_k_norm,
           nsa_cmp_pe, nsa_cmp_w1, nsa_cmp_b1, nsa_cmp_w2, nsa_w_out, ssm_w_in, ssm_conv_w, ssm_conv_b, ssm_dt_bias,
           ssm_a_log, ssm_d, ssm_norm_w, ssm_w_out):
    import concourse.bacc as bacc
    from concourse.bass_utils import run_bass_kernel_spmd

    def arr(a):
        return np.asarray(a)

    def f_chunks(w, kgroups):
        out = []
        for c in range(0, w.shape[1], 256):
            k0 = 0
            for nk in kgroups:
                part = w[k0 * P:(k0 + nk) * P, c:c + 256].reshape(nk, P, 256).transpose(1, 0, 2).reshape(P, -1)
                out.append(np.pad(part, ((0, 0), (0, CH - part.shape[1]))))
                k0 += nk
        return out

    def t_chunks(w):
        out = []
        for c in range(0, w.shape[1], 512):
            for k0 in (0, 4):
                out.append(w[k0 * P:(k0 + 4) * P, c:c + 512].reshape(4, P, 512).transpose(1, 0, 2).reshape(P, -1))
        return out

    def n_chunk(w):
        part = w.reshape(KT, P, w.shape[1]).transpose(1, 0, 2).reshape(P, -1)
        return [np.pad(part, ((0, 0), (0, CH - part.shape[1])))]

    w_in, s_in = arr(nsa_w_in)[0], arr(ssm_w_in)[0]
    stream = t_chunks(w_in[:, 1024:1536])
    stream += n_chunk(w_in[:, 2560:2608])
    for g in range(GROUPS):
        at = [slice(g * 256, (g + 1) * 256)] + [slice(b + g * DH, b + (g + 1) * DH) for b in (1536, 2048, 1792, 2304)]
        stream += t_chunks(np.concatenate([w_in[:, a] for a in at], 1))
    stream += f_chunks(arr(nsa_w_out)[0], [8])

    def ffn_stream(layer):
        g = f_chunks(arr(ffn_w_gate)[layer], [8])
        u = f_chunks(arr(ffn_w_up)[layer], [8])
        return [c for pair in zip(g, u) for c in pair] + f_chunks(arr(ffn_w_down)[layer], [8, 8, 6])
    stream += ffn_stream(0)
    xbc = s_in[:, DI:DI + 3072]
    stream += f_chunks(np.concatenate([xbc[:, 2560:3072], xbc[:, 2048:2560], xbc[:, 0:2048]], 1), [8])
    stream += n_chunk(s_in[:, DI + 3072:])
    stream += t_chunks(s_in[:, 0:DI])
    stream += f_chunks(arr(ssm_w_out)[0], [8, 8])
    stream += ffn_stream(1)
    assert len(stream) == NCHUNKS

    def columns(a):
        return np.asarray(a).reshape(-1, P).T
    cols = np.concatenate(
        [columns(mix_norm_w), columns(ffn_norm_w), columns(ssm_norm_w), columns(ssm_conv_b), columns(ssm_conv_w),
         columns(nsa_cmp_b1), columns(nsa_cmp_pe)], 1)
    inv = np.power(np.float32(THETA), -np.arange(ROPE_HALF, dtype=np.float32) / ROPE_HALF).astype(np.float32)
    qn_, kn_ = arr(nsa_q_norm)[0], arr(nsa_k_norm)[0]
    row = np.concatenate([qn_, qn_, qn_, qn_, kn_[1], kn_[2], kn_[0], arr(ssm_d)[0], arr(ssm_dt_bias)[0],
                          arr(ssm_a_log)[0], inv])
    rows = np.broadcast_to(row, (P, NROWS))
    pos = arr(positions)[0]
    blocks = np.concatenate([pos[CMP_BLOCK - 1::CMP_STRIDE][:NCMP], pos[-1:]])
    pos5 = np.concatenate([pos.reshape(TT, P).T, np.tile(blocks, GROUPS)[:, None]], 1).astype(np.int32)
    idx = np.arange(P)
    tri = np.stack([idx[:, None] <= idx[None, :], idx[:, None] > idx[None, :], np.ones((P, P), bool)], 1)
    t = np.arange(SEQ).reshape(TT, P).T[:, :, None]
    cend = np.arange(32) * CMP_STRIDE + CMP_BLOCK - 1
    seen = (cend[None, None, :] <= t) & (np.arange(32) < NCMP)
    cmask = np.stack([np.where(seen, 0.0, NEG), seen], 1).astype(np.float32)
    arrays = {
        "wstream": np.stack(stream),
        "xT_in": arr(x)[0].T.reshape(KT, P, SEQ).transpose(1, 0, 2),
        "cols_in": cols,
        "rows_in": rows,
        "pos_in": pos5,
        "cw1_in": arr(nsa_cmp_w1)[0].reshape(2, NJ, P, CMP_HIDDEN).transpose(2, 0, 1, 3),
        "cw2_in": arr(nsa_cmp_w2)[0].reshape(2, 2, P, DH).transpose(2, 0, 1, 3),
        "ident_in": np.eye(P, dtype=np.float32),
        "tri_in": tri.astype(np.float32),
        "cmask_in": cmask,
    }
    arrays = {k: np.ascontiguousarray(v) for k, v in arrays.items()}
    nc = bacc.Bacc("TRN2", target_bir_lowering=False, num_devices=1, dynamic_dma_scratch_size=1024)
    args = [nc.dram_tensor(k, v.shape, mybir.dt.from_np(v.dtype), kind="ExternalInput").ap()
            for k, v in arrays.items()]
    out = nc.dram_tensor("out", (P, KT, SEQ), F32, kind="ExternalOutput").ap()
    trunk(nc, *args, out)
    r = run_bass_kernel_spmd(nc, [arrays], core_ids=[0])
    return r.results[0]["out"].transpose(1, 0, 2).reshape(DM, SEQ).T[None]
```

```python
from contextlib import ExitStack

import numpy as np

import concourse.bass as bass
from concourse import mybir

F32 = mybir.dt.float32
F32R = mybir.dt.float32r
BF16 = mybir.dt.bfloat16
I32 = mybir.dt.int32
ALU = mybir.AluOpType
ACT = mybir.ActivationFunctionType
AX = mybir.AxisListType.X

P = 128
SEQ, DM = 512, 1024
TT = SEQ // P
KT = DM // P
HEADS, GROUPS, HP, DH = 16, 4, 4, 64
CMP_BLOCK, CMP_STRIDE, CMP_HIDDEN = 32, 16, 256
NCMP = (SEQ - CMP_BLOCK) // CMP_STRIDE + 1
NJ = CMP_BLOCK // 2
SCALE = DH ** -0.5
ROPE_HALF, THETA = 8, 500000.0
SH, SG, SHP, SP_, SN = 32, 4, 8, 64, 128
DI = 2048
GW = DI // SG
FF = 2816
FT = FF // P
EPS = 1e-6
CH = 2048
NEG = -1e30
PI = float(np.float32(np.pi))

COL_MIX, COL_FFN, COL_SSMN, COL_CB, COL_CW, COL_B1, COL_PE = 0, 16, 32, 48, 72, 168, 172
NCOLS = COL_PE + 2 * NJ
ROW_W6, ROW_KC, ROW_D, ROW_DTB, ROW_AL, ROW_INV = 0, 384, 448, 480, 512, 544
NROWS = 552


class Tally:
    def __init__(self, sem):
        self.sem, self.n, self.off, self.first = sem, 0, 0, 0

    def inc(self, instruction):
        instruction.then_inc(self.sem, 1)
        self.n += 1

    def wait(self, engine):
        engine.wait_ge(self.sem, self.n + self.off)

    def enter(self, i, per):
        self.off, self.first = i * per, self.n

    def leave(self, turns, per):
        assert self.n - self.first == per, (self.n - self.first, per)
        self.n, self.off = self.first + turns * per, 0


def chunk_plan():
    at, n = {}, 0
    for name, count in (("kv_cmp", 2), ("gates", 1), ("qkv", 8), ("nsa_out", 4), ("up0", 2 * FT // 2),
                        ("down0", 12), ("xbc", 12), ("dt", 1), ("z", 8), ("ssm_out", 8),
                        ("up1", 2 * FT // 2), ("down1", 12)):
        at[name] = n
        n += count
    return at, n


CHUNK, NCHUNKS = chunk_plan()
EVAC, _t = {}, 0
for _name, _count in (("kv_cmp", 4), ("gates", 1), ("qkv", 16), ("nsa_out", 8), ("up0", FT), ("down0", 8),
                      ("xbc", 24), ("dt", 1), ("z", 16), ("ssm_out", 8), ("up1", FT), ("down1", 8)):
    EVAC[_name] = _t
    _t += _count


DVE_GROUP_STEPS, DVE_SCAN_STEPS = 90, 12


def trunk(nc, wstream, xT_in, cols_in, rows_in, pos_in, cw1_in, cw2_in, ident_in, tri_in, cmask_in, out):
    with ExitStack() as ctx:
        def sb(name, shape, dt=F32, c=ctx):
            return c.enter_context(nc.sbuf_tensor(name, shape, dt))

        def sem(name):
            return ctx.enter_context(nc.semaphore(name))

        class Region:
            def __init__(self, start):
                self.end = start

            def take(self, name, shape, dt=F32):
                t = nc.alloc_sbuf_tensor_at(name, shape, dt, offset=self.end)
                self.end += -(-int(np.prod(shape[1:])) * (2 if dt == BF16 else 4) // 32) * 32
                assert self.end <= nc.SBUF_PARTITION_SIZE_BYTES, (name, self.end)
                return t

        r = Region(-(-nc.sbuf_base // 32) * 32)
        cols = r.take("cols", [P, NCOLS])
        rows = r.take("rows", [P, NROWS])
        ident = r.take("ident", [P, P])
        tri = r.take("tri", [P, 3, P])
        ident_bf = r.take("ident_bf", [P, P], BF16)
        negmask_bf = r.take("negmask_bf", [P, P], BF16)
        stat = r.take("stat", [P, 64])
        mhalf = r.take("mhalf", [P, 8])
        wraw = r.take("wraw", [P, 2, CH])
        wh = r.take("wh", [P, 2, CH], F32R)
        wl = r.take("wl", [P, 2, CH], F32R)
        scratch_at = r.end
        diag = r.take("diag", [P, TT, P])
        tmp = r.take("tmp", [P, 2, SEQ])
        sq = r.take("sq", [P, 2, SEQ])
        sqacc = r.take("sqacc", [P, SEQ])
        a = Region(scratch_at)
        rp = a.take("rope_products", [P, 4, 6, ROPE_HALF])
        pc = a.take("pc", [P, TT, HP, 32])
        vz = a.take("vz", [P, HP, DH])
        sm = a.take("sm", [P, 6, 32])
        vst = a.take("vst", [P, TT, 2, DH])
        assert a.end <= r.end
        act_at = r.end
        xh = r.take("xh", [P, KT, SEQ], F32R)
        xl = r.take("xl", [P, KT, SEQ], F32R)
        res_at = r.end
        xT = r.take("xT", [P, KT, SEQ])
        a = Region(res_at)
        kvc = a.take("kvc", [P, TT, 512])
        tb2 = a.take("tb2", [P, 2, GROUPS, 256])
        assert a.end <= r.end
        a = Region(res_at)
        Pm = a.take("Pm", [P, 2, 2, SEQ])
        kB1 = a.take("kB1", [P, 2, SEQ], F32R)
        pcT = a.take("pcT", [P, SEQ])
        assert a.end <= r.end
        arena_at = r.end
        a = Region(arena_at)
        hh = a.take("hh", [P, FT, SEQ], F32R)
        hl = a.take("hl", [P, FT, SEQ], F32R)
        gate = a.take("gate", [P, 2, SEQ])
        hid = a.take("hid", [P, 2, SEQ])
        a = Region(arena_at)
        proj = a.take("proj", [P, TT, 8, DH])
        glin = a.take("glin", [P, TT, 48])
        gates_f = a.take("gates_f", [48, SEQ])
        cosT = a.take("cosT", [P, 5, ROPE_HALF])
        sinT = a.take("sinT", [P, 5, ROPE_HALF])
        ang = a.take("ang", [P, 10, 5 * ROPE_HALF])
        posi = a.take("posi", [P, 5], I32)
        B1c = a.take("B1c", [P, P], F32R)
        B2c = a.take("B2c", [P, P], F32R)
        VC4 = a.take("VC4", [P, GROUPS, DH])
        cmask = a.take("cmask", [P, 2, TT, 32])
        qA = a.take("qA", [P, HP, SEQ], F32R)
        qn = a.take("qn", [P, TT, 6, 2, DH])
        kB2 = a.take("kB2", [P, 2, SEQ], F32R)
        nsa_at = a.end
        tbT = a.take("tbT", [P, 2, NJ, GROUPS, 32])
        cw1 = a.take("cw1", [P, 2, NJ, CMP_HIDDEN])
        cw2 = a.take("cw2", [P, 2, 2, DH])
        hidK = a.take("hidK", [P, 2, P])
        hidV = a.take("hidV", [P, 2, GROUPS, HP, 32])
        kcn = a.take("kcn", [P, 2, DH])
        krp = a.take("krp", [P, 4, ROPE_HALF])
        a = Region(nsa_at)
        xo = a.take("xo", [P, KT, SEQ], F32R)
        xol = a.take("xol", [P, KT, SEQ], F32R)
        PT = a.take("PT", [P, 2, 2, TT, SEQ])
        a = Region(arena_at)
        xtok = a.take("xtok", [P, TT, DI])
        BCf = a.take("BCf", [P, 2, SG, SEQ])
        zraw = a.take("zraw", [P, TT, GW])
        zs = a.take("zs", [P, TT, GW])
        dtb = a.take("dtb", [P, 10, TT * SH])
        dt_f = a.take("dt_f", [SH, SEQ])
        ex = a.take("ex", [P, 3, TT * SH])
        bc = a.take("bc", [P, TT, 2, P])
        btst = a.take("btst", [P, 2, P])
        Gm = a.take("Gm", [P, 2, 4, P])
        Lx = a.take("Lx", [P, 2, 2, 4, P])
        state = a.take("state", [P, GW])
        ybuf = a.take("ybuf", [P, 2, GW])
        ysq = a.take("ysq", [P, GW])
        cbm = a.take("cbm", [P, 2, P])
        yst = a.take("yst", [P, 2, 4])
        a = Region(arena_at)
        yT = a.take("yT", [P, TT, 16, P])
        a = Region(arena_at)
        yl = a.take("yl", [P, TT, 16, P], F32R)
        a = Region(act_at)
        yh = a.take("yh", [P, TT, 16, P], F32R)
        assert a.end <= res_at
        a = Region(scratch_at)
        xdt = a.take("xdt", [P, 2, GW])
        xdd = a.take("xdd", [P, 2, GW])
        dxs = a.take("dxs", [P, 2, GW])
        assert a.end <= act_at
        ps = ctx.enter_context(nc.psum_tensor("ps", [P, 8, SEQ], F32))

        cols_landed, params_landed, rest_landed, cw_landed, x_again, out_stored = map(
            sem, ("cols_landed", "params_landed", "rest_landed", "cw_landed", "x_again", "out_stored"))
        x_landed = [sem(f"x{k}_landed") for k in range(4)]
        landed = [sem("even_chunk_landed"), sem("odd_chunk_landed")]
        hi_done = sem("weights_hi_done")
        lo_done = sem("weights_lo_done")
        products = sem("products_done")
        evac = sem("tiles_evacuated")
        masks_cast, zeroed, sq_done, acc_done, colsum_done, mean_done, rstd_done, diag_done, rbc_done = map(
            sem, ("masks_cast", "square_sum_zeroed", "squares_done", "square_sum_done", "colsum_done",
                  "mean_square_done", "rms_rstd_done", "diag_done", "rstd_broadcast_done"))
        scaled, xh_done, xl_done, vz_zeroed, vz_done = map(sem, ("norm_scaled", "xh_done", "xl_done", "vz_zeroed", "vz_done"))
        gate_in, gate_done, hh_done, hl_done = map(sem, ("gate_normed", "gate_done", "hidden_hi_done", "hidden_lo_done"))
        vec, act_self, pool_self = map(sem, ("vector_step", "scalar_step", "pool_step"))
        (mhalf_set, kvT, tb_act, tb_vec, tbT_done, hid_mm, hid_done, cmp_mm, kc_sq, kc_mean, kc_rstd, kcn_done, kcT, kc_hi,
         kc_lo, vc_done, angles_done, sincos_done, gates_exp, gates_done, gates_out, gates_T) = map(sem, (
             "mhalf_set", "kv_transposed", "taps_by_act", "taps_by_vec", "blocks_built", "cmp_hidden_mm", "cmp_hidden_done",
             "cmp_out_mm", "kc_squared", "kc_mean_square", "kc_rstd", "kc_normed", "kc_transposed", "kc_hi_done",
             "kc_lo_done", "vc_copied", "angles_done", "sincos_done", "gates_exp", "gates_done", "gates_copied", "gates_transposed"))
        (qk_squared, qk_mean, qk_rstd, qk_normed, qkT, qkT_hi, qkT_lo, v_staged, cs_mm, cs_shifted, cs_exp, pc_done,
         pcT_mm, pcT_done, scores, negmax, expd, normed, pT_mm, pT_done, pv_done, o_hi, o_lo) = map(sem, (
             "qk_squared", "qk_mean_square", "qk_rstd", "qk_normed", "qk_transposed", "qk_hi_done", "qk_lo_done",
             "v_staged", "cmp_scores", "cmp_scores_shifted", "cmp_exp", "cmp_probs_done", "cmp_probs_transposed",
             "cmp_probsT_done", "scores_done", "negmax_done", "exp_done", "probs_normed", "probs_transposed",
             "probsT_done", "pv_done", "o_hi_done", "o_lo_done"))
        (silu_done, featT, featT_done, dt_out, dt_T, dt_in, dt_e, dt_u, dt_ln, dt_done, a_exp, staged, cum_mm, cum_exp, g_built,
         seg_mm, seg_exp, m_built, cb_mm, cb_done, xdt_done, y_mm, state_mm, y_done, state_done, z_silu, y_sq, y_var,
         y_rs, y_scaled, yT_mm, yT_done, yh_done, yl_done) = map(sem, (
             "conv_silu_done", "feature_transposed", "feature_T_done", "dt_copied", "dt_transposed",
             "dt_biased", "dt_exp", "dt_u", "dt_ln",
             "dt_done", "a_exp", "chunk_staged", "cum_mm", "cum_exp", "g_built", "segments_mm", "segments_exp",
             "m_built", "cb_mm", "cb_done", "xdt_done", "y_mm", "state_mm", "y_done", "state_done", "z_silu", "y_squared",
             "y_mean_square", "y_rstd", "y_scaled", "yT_mm", "yT_done", "yh_done", "yl_done"))

        def at(n, i, per):
            return n if i is None else i * per + n

        def col(c, n=1):
            return cols[:, c:c + n]

        def after(engine, semaphore, value):
            if not isinstance(value, int) or value > 0:
                engine.wait_ge(semaphore, value)

        def scan_groups(engine, group, enter=None, leave=None):
            group(0, False)
            with engine.Fori(0, SG - 2) as i:
                if enter:
                    enter(i)
                group(i + 1, False)
            if leave:
                leave()
            group(SG - 1, True)

        Q4 = "p (h d) -> p h d"
        RES = {"nsa_out": [8], "ssm_out": [8, 8], "down0": [8, 8, 6], "down1": [8, 8, 6]}
        NORM = {"nsa_out": 1, "down0": 2, "ssm_out": 3}
        NORMCOL = [COL_MIX, COL_FFN, COL_MIX + KT, COL_FFN + KT]

        block = ctx.enter_context(nc.Block())

        @block.sync
        def _(sp):
            sp.dma_start(cols[:, :], cols_in).then_inc(cols_landed, 16)
            for k in range(4):
                sp.dma_start(xT[:, 2 * k:2 * k + 2, :], xT_in[:, 2 * k:2 * k + 2, :]).then_inc(x_landed[k], 16)
                if k == 0:
                    sp.dma_start(wraw[:, 0, :], wstream[0]).then_inc(landed[0], 16)
            sp.dma_start(wraw[:, 1, :], wstream[1]).then_inc(landed[1], 16)
            sp.dma_start(tri[:, :, :], tri_in).then_inc(params_landed, 16)
            sp.dma_start(ident[:, :], ident_in).then_inc(params_landed, 16)
            sp.dma_start(rows[:, :], rows_in).then_inc(params_landed, 16)
            sp.dma_start(posi[:, :], pos_in).then_inc(rest_landed, 16)
            sp.dma_start(cmask[:, :, :, :], cmask_in).then_inc(rest_landed, 16)
            sp.dma_start(cw1[:, :, :, :], cw1_in).then_inc(cw_landed, 16)
            sp.dma_start(cw2[:, :, :, :], cw2_in).then_inc(cw_landed, 16)
            with sp.Fori(1, NCHUNKS // 2) as i:
                for k in range(2):
                    sp.wait_ge(lo_done, 2 * i + (k - 1))
                    sp.dma_start(wraw[:, k, :], wstream[bass.ds(2 * i + k, 1)].rearrange("a p n -> p (a n)")
                                 ).then_inc(landed[k], 16)
            for t in range(KT):
                sp.wait_ge(evac, EVAC["down1"] + t + 1)
                sp.dma_start(out[:, t, :], xT[:, t, :]).then_inc(out_stored, 16)
            sp.wait_ge(out_stored, 16 * KT)

        @block.tensor
        def _(pe):
            mm = pe.matmul

            def split_product(o, wa, xa, start, stop):
                mm(o, wa[0], xa[0], start=start, stop=False)
                mm(o, wa[0], xa[1], start=False, stop=False)
                return mm(o, wa[1], xa[0], start=False, stop=stop)

            def fresh(L):
                return lambda kt: pe.wait_ge(xl_done, 8 * L + kt + 1)

            def chunk_F(n, i, per, x, ks, banks, first, last, before=None, between=None, each=None):
                pe.wait_ge(lo_done, at(n + 1, i, per))
                s = n % 2
                for m in range(2):
                    if before:
                        before(m)
                    o = ps[:, banks[m], :]
                    for k, kt in enumerate(ks):
                        w = slice(k * 256 + m * P, k * 256 + (m + 1) * P)
                        if each and m == 0:
                            each(kt)
                        hi, lo = x(kt)
                        oo = o if len(hi.shape) == 2 else o.rearrange("p (a b) -> p a b", b=P)
                        ins = split_product(oo, (wh[:, s, w], wl[:, s, w]), (hi, lo),
                                            first and k == 0, last and k == len(ks) - 1)
                    ins.then_inc(products, 1)
                    if between:
                        between(m)

            def chunk_T(n, i, per, ks, width, first, last, before=None, each=None, bank=0):
                pe.wait_ge(lo_done, at(n + 1, i, per))
                s = n % 2
                for tt in range(TT):
                    if before:
                        before(tt)
                    for k, kt in enumerate(ks):
                        w = slice(k * width, (k + 1) * width)
                        t = slice(tt * P, (tt + 1) * P)
                        if each and tt == 0:
                            each(kt)
                        ins = split_product(ps[:, bank + tt, 0:width], (xh[:, kt, t], xl[:, kt, t]),
                                            (wh[:, s, w], wl[:, s, w]), first and k == 0,
                                            last and k == len(ks) - 1)
                    if tt % 2:
                        ins.then_inc(products, 1)

            def narrow(n, width, bank):
                pe.wait_ge(lo_done, n + 1)
                s = n % 2
                for kt in range(KT):
                    w = slice(kt * width, (kt + 1) * width)
                    ins = split_product(ps[0:width, bank, :], (wh[:, s, w], wl[:, s, w]), (xh[:, kt, :], xl[:, kt, :]),
                                        kt == 0, kt == KT - 1)
                    if kt == KT // 2:
                        ins.then_inc(products, 1)
                ins.then_inc(products, 1)

            def narrow_T(src, width, bank, ready, done):
                pe.wait_ge(ready, 1)
                for tt in range(TT):
                    ins = pe.transpose(ps[:, bank, tt * width:(tt + 1) * width], src[:, tt * P:(tt + 1) * P],
                                       ident[0:width, 0:width])
                ins.then_inc(done, 1)

            def column_sums(L):
                pe.wait_ge(acc_done, 8 * (L + 1))
                for tt in range(TT):
                    ins = mm(ps[:, 7, tt:tt + 1], sqacc[:, tt * P:(tt + 1) * P], tri[:, 2, 0:1], start=True, stop=True)
                ins.then_inc(colsum_done, 1)

            def broadcast(L):
                pe.wait_ge(diag_done, L)
                mm(ps[:, 6, :], tri[:, 2, :], diag[:, :, :].rearrange("p t q -> p (t q)"), start=True, stop=True
                   ).then_inc(rbc_done, 1)

            def xs(kt):
                return xh[:, kt, :], xl[:, kt, :]

            def hs(kt):
                return hh[:, kt, :], hl[:, kt, :]

            def ys(kt):
                return yh[:, :, kt, :], yl[:, :, kt, :]

            def residual(name, x, ready=None):
                ks, n0, t0 = RES[name], CHUNK[name], EVAC[name]
                starts = [sum(ks[:q]) for q in range(len(ks))]
                per = 2 * len(ks)
                pe.wait_ge(evac, t0)
                with pe.Fori(0, 2) as i:
                    for p in range(2):
                        for q, nk in enumerate(ks):
                            def free(m):
                                if q == 0:
                                    pe.wait_ge(evac, i * 4 + (t0 + 2 * p + m - 3))
                            if ready and q == 1:
                                ready()
                            chunk_F(n0 + p * len(ks) + q, i, per, x, range(starts[q], starts[q] + nk),
                                    (2 * p, 2 * p + 1), q == 0, q == len(ks) - 1, before=free)

            def ffn(up, down, L):
                n0, t0 = CHUNK[up], EVAC[up]
                pe.wait_ge(evac, t0)

                def between(m):
                    broadcast(L) if m else column_sums(L)
                chunk_F(n0, None, 0, xs, range(KT), (0, 1), True, True, between=between, each=fresh(L))
                chunk_F(n0 + 1, None, 0, xs, range(KT), (2, 3), True, True)
                with pe.Fori(0, FT // 2 - 1) as i:
                    def free(m):
                        pe.wait_ge(evac, i * 2 + (t0 + 1 + m))
                    chunk_F(n0 + 2, i, 2, xs, range(KT), (0, 1), True, True, before=free)
                    chunk_F(n0 + 3, i, 2, xs, range(KT), (2, 3), True, True)
                pe.wait_ge(hl_done, FT * (1 + (L == 3)))
                residual(down, hs)

            chunk_T(0, None, 0, range(4), 512, True, False, each=fresh(0))
            pe.wait_ge(params_landed, 48)
            column_sums(0)
            chunk_T(1, None, 0, range(4, 8), 512, False, True, each=fresh(0))
            for kv in range(2):
                for gp in range(2):
                    for tt in range(TT):
                        pe.wait_ge(evac, tt + 1)
                        f = kv * 256 + gp * P
                        ins = pe.transpose(ps[:, 4 + 2 * kv + gp, tt * P:(tt + 1) * P], kvc[:, tt, f:f + P],
                                           ident[:, :])
                    ins.then_inc(kvT, 1)
            pe.wait_ge(tb_act, 2)
            pe.wait_ge(tb_vec, 2)
            narrow(CHUNK["gates"], 48, 4)
            for k in range(2):
                chunk_T(CHUNK["qkv"] + k, None, 0, range(4 * k, 4 * k + 4), 512, k == 0, k == 1)
                if k == 0:
                    pe.wait_ge(tb_act, 4)
                    pe.wait_ge(tb_vec, 4)
                    narrow_T(gates_f, 48, 5, gates_out, gates_T)
            pe.wait_ge(cw_landed, 32)
            for kv in range(2):
                pe.wait_ge(tbT_done, 2 * (kv + 1))
                for ht in range(2):
                    r = 2 * kv + ht
                    for j in range(NJ):
                        ins = mm(ps[:, 6, r * P:(r + 1) * P], cw1[:, kv, j, ht * P:(ht + 1) * P],
                                 tbT[:, kv, j, :, :].rearrange("p g c -> p (g c)"), start=j == 0, stop=j == NJ - 1)
                    ins.then_inc(hid_mm, 1)

            def qk_transposes(g):
                pe.wait_ge(qk_normed, g * 4 + 4)
                for h in range(6):
                    if h == 4 and not (isinstance(g, int) and g == 0):
                        pe.wait_ge(pT_done, g * 16)
                    for tt in range(TT):
                        ins = pe.transpose(ps[:, h, tt * P:(tt + 1) * P],
                                           qn[:, tt, h, :, :].rearrange("p a d -> p (a d)"), ident[:, :])
                    ins.then_inc(qkT, 1)

            def group(g, more):
                def qk(s):
                    h, i = divmod(s, TT)
                    w = (i + 1) * P
                    if s >= 2:
                        pe.wait_ge(expd, g * 32 + 2 * (s - 1))
                    for b in range(2):
                        o = ps[:, 2 * (s % 2) + b, :]
                        q = qA[:, h, i * P:(i + 1) * P]
                        mm(o[:, 0:w], q, kB1[:, b, 0:w], start=True, stop=False)
                        mm(o[:, 0:w], q, kB2[:, b, 0:w], start=False, stop=False)
                        ins = mm(o[:, i * P:w], ident_bf[:, :], negmask_bf[:, :], start=False, stop=True)
                    ins.then_inc(scores, 1)

                def cmp_scores():
                    pe.wait_ge(o_lo, g * 2)
                    for tt in range(TT):
                        for h in range(HP):
                            o = ps[:, 6, (tt * HP + h) * 32:(tt * HP + h + 1) * 32]
                            q = qA[:, h, tt * P:(tt + 1) * P]
                            mm(o, q, B1c[:, bass.ds(g * 32, 32)], start=True, stop=False)
                            ins = mm(o, q, B2c[:, bass.ds(g * 32, 32)], start=False, stop=True)
                    ins.then_inc(cs_mm, 1)

                def cmp_transposes():
                    pe.wait_ge(pc_done, g + 1)
                    for tt in range(TT):
                        ins = pe.transpose(ps[:, 6, tt * P:(tt + 1) * P], pc[:, tt, :, :].rearrange("p h c -> p (h c)"),
                                           ident[:, :])
                    ins.then_inc(pcT_mm, 1)

                def pT(s):
                    h, i = divmod(s, TT)
                    pe.wait_ge(normed, g * 32 + 2 * (s + 1))
                    if s:
                        pe.wait_ge(pT_done, g * 16 + s)
                    for b in range(2):
                        for j in range(i + 1):
                            ins = pe.transpose(ps[:, 4 + b, j * P:(j + 1) * P], Pm[:, s % 2, b, j * P:(j + 1) * P],
                                               ident[:, :])
                    ins.then_inc(pT_mm, 1)

                def pv(h):
                    o = ps[DH * (h % 2):DH * (h % 2 + 1), 6, :]
                    if h == 0:
                        pe.wait_ge(v_staged, g + 1)
                        pe.wait_ge(pcT_done, g + 1)
                        pe.wait_ge(vz_done, g * 4 + 4)
                    if h == 2:
                        pe.wait_ge(o_lo, g * 2 + 1)
                    pe.wait_ge(pT_done, g * 16 + 4 * (h + 1))
                    mm(o, vz[:, h, :], pcT[:, :], start=True, stop=False)
                    for b in range(2):
                        for j in range(TT):
                            ins = mm(o[:, j * P:], vst[:, j, b, :], PT[:, h % 2, b, j, j * P:], start=False,
                                     stop=b == 1 and j == TT - 1)
                    ins.then_inc(pv_done, 1)

                n0, t0 = CHUNK["qkv"] + 2, EVAC["qkv"] + 4

                def project(part):
                    tt, third = divmod(part, 3)
                    if part == 0:
                        pe.wait_ge(lo_done, g * 2 + (n0 + 2))
                    if third == 0:
                        pe.wait_ge(evac, g * 4 + (t0 + tt))
                    t = slice(tt * P, (tt + 1) * P)
                    for m in range(8 * third, 8 * third + 8):
                        kt, pss = divmod(m, 3)
                        slot, w = (n0 + kt // 4) % 2, slice((kt % 4) * 512, (kt % 4 + 1) * 512)
                        ins = mm(ps[:, 7, :], (xh, xl, xh)[pss][:, kt, t], (wh, wh, wl)[pss][:, slot, w],
                                 start=m == 0, stop=m == 23)
                    if third == 2:
                        ins.then_inc(products, 1)

                for k in range(18):
                    if k < 16:
                        qk(k)
                    if k == 0:
                        cmp_scores()
                    if k == 3:
                        cmp_transposes()
                    if k in (6, 10, 14):
                        pv((k - 6) // 4)
                    if k >= 2:
                        pT(k - 2)
                    if more and k < 12:
                        project(k)
                if more:
                    qk_transposes(g + 1)
                pv(3)

            pe.wait_ge(evac, EVAC["qkv"])
            qk_transposes(0)
            pe.wait_ge(hid_done, 4)
            for ht in range(2):
                mm(ps[:, 7, 0:DH], hidK[:, ht, :], cw2[:, 0, ht, :], start=ht == 0, stop=ht == 1)
            for g in range(GROUPS):
                for ht in range(2):
                    lhs = hidV[:, ht, g, :, :].rearrange("p h c -> p (h c)")
                    ins = mm(ps[:, 7, (g + 1) * DH:(g + 2) * DH], lhs, cw2[:, 1, ht, :], start=ht == 0, stop=ht == 1)
            ins.then_inc(cmp_mm, 1)
            pe.wait_ge(kcn_done, 1)
            pe.transpose(ps[:, 7, 3 * P:4 * P], kcn[:, :, :].rearrange("p a d -> p (a d)"), ident[:, :]
                         ).then_inc(kcT, 1)
            pe.wait_ge(kc_lo, 1)
            pe.wait_ge(masks_cast, 2)
            pe.wait_ge(qkT_lo, 6)
            with pe.Fori(0, GROUPS - 1) as g:
                group(g, True)
                pe.wait_ge(qkT_lo, g * 6 + 12)
            group(GROUPS - 1, False)
            pe.wait_ge(o_lo, 2 * GROUPS)
            residual("nsa_out", lambda kt: (xo[:, kt, :], xol[:, kt, :]))
            ffn("up0", "down0", 1)

            column_sums(2)
            broadcast(2)
            n0, t0 = CHUNK["xbc"], EVAC["xbc"]
            pe.wait_ge(evac, t0)

            def transposes(turn, j):
                pe.wait_ge(silu_done, turn * 4 + (8 + j + 1))
                after(pe, featT_done, turn * 4 + (j - 1))
                for tt in range(TT):
                    ins = pe.transpose(ps[:, 4 + j % 2, tt * P:(tt + 1) * P], sq[:, j % 2, tt * P:(tt + 1) * P],
                                       ident[:, :])
                ins.then_inc(featT, 1)

            def conv_tiles(n, i, t, turn=None, each=None):
                def free(m):
                    pe.wait_ge(evac, at(t + m - 3, i, 4))

                def free2(m):
                    pe.wait_ge(evac, at(t + 2 + m - 3, i, 4))

                def between(m):
                    if turn is not None and not (isinstance(turn, int) and m == 0):
                        transposes(turn, m - 1) if m else transposes(turn - 1, 3)

                def between2(m):
                    if turn is not None:
                        transposes(turn, 1 + m)
                chunk_F(n, i, 2, xs, range(KT), (0, 1), True, True, before=free, between=between, each=each)
                chunk_F(n + 1, i, 2, xs, range(KT), (2, 3), True, True, before=free2, between=between2)
            conv_tiles(n0, None, t0, each=fresh(2))
            conv_tiles(n0 + 2, None, t0 + 4)
            conv_tiles(n0 + 4, None, t0 + 8, 0)
            with pe.Fori(0, 3) as i:
                conv_tiles(n0 + 6, i, t0 + 12, i + 1)
            narrow(CHUNK["dt"], SH, 6)
            transposes(3, 3)
            narrow_T(dt_f, SH, 7, dt_out, dt_T)
            n0, t0 = CHUNK["z"], EVAC["z"]
            pe.wait_ge(evac, EVAC["dt"])

            def z_bank(tt):
                if tt >= 2:
                    pe.wait_ge(featT_done, 13 + tt)
            chunk_T(n0, None, 0, range(4), 512, True, False, before=z_bank, bank=2)
            pe.wait_ge(dt_done, 1)
            for k in range(3):
                ins = mm(ps[:, 6, k * P:(k + 1) * P], tri[:, k, :], dtb[:, 1, :], start=True, stop=True)
            ins.then_inc(cum_mm, 1)

            def decays(g, j):
                for q in range(2):
                    pe.wait_ge(g_built, g * 8 + (2 * j + q + 1))
                    after(pe, seg_exp, g * 8 + (2 * j + q - 1))
                    mm(ps[:, q, :], tri[:, 1, :], Gm[:, q, :, :].rearrange("p h t -> p (h t)"), start=True, stop=True
                       ).then_inc(seg_mm, 1)
                pe.wait_ge(staged, g * 4 + (j + 1))
                after(pe, cb_done, g * 4 + j)
                mm(ps[:, 6, 0:P], bc[:, j % TT, 0, :], bc[:, j % TT, 1, :], start=True, stop=True)
                pe.transpose(ps[:, 6, P:2 * P], bc[:, j % TT, 0, :], ident[:, :]).then_inc(cb_mm, 1)

            def to_features(g, j):
                pe.wait_ge(y_scaled, g * 4 + (j + 1))
                after(pe, yT_done, g * 4 + j)
                for f in range(4):
                    ins = pe.transpose(ps[:, 7, f * P:(f + 1) * P], ybuf[:, j % 2, f * P:(f + 1) * P], ident[:, :])
                ins.then_inc(yT_mm, 1)

            def group(g, last):
                def z_part(tt, third):
                    if third == 0:
                        if tt == 0:
                            pe.wait_ge(lo_done, g * 2 + (n0 + 4))
                        pe.wait_ge(evac, g * 4 + (t0 + 4 + tt))
                    t = slice(tt * P, (tt + 1) * P)
                    for m in range(8 * third, 8 * third + 8):
                        kt, pss = divmod(m, 3)
                        slot, w = (n0 + kt // 4) % 2, slice((kt % 4) * 512, (kt % 4 + 1) * 512)
                        ins = mm(ps[:, 5, :], (xh, xl, xh)[pss][:, kt, t], (wh, wh, wl)[pss][:, slot, w],
                                 start=m == 0, stop=m == 23)
                    if third == 2:
                        ins.then_inc(products, 1)

                places = {0: ((), (), (0, 1, 2)), 1: ((0,), (1,), (2,)), 2: ((0,), (1,), (2,)), 3: ((0, 1), (2,), ())}
                for k in range(TT):
                    if k < 3 or not last:
                        decays(g, k + 1)

                    def z_at(place):
                        for third in () if last else places[k][place]:
                            z_part(k, third)
                    z_at(0)
                    after(pe, y_done, g * 4 + k)
                    pe.wait_ge(xdt_done, g * 12 + 3 * (k + 1))
                    if k:
                        pe.wait_ge(state_done, g * 3 + k)
                        mm(ps[:, 3, :], bc[:, k, 1, :], state[:, :], start=True, stop=True)
                    if k < 3:
                        after(pe, state_done, g * 3 + k)
                        mm(ps[:, 4, :], btst[:, k % 2, :], xdd[:, k % 2, :], start=True, stop=True
                           ).then_inc(state_mm, 1)
                    for q in range(2):
                        pe.wait_ge(m_built, g * 8 + (2 * k + q + 1))
                        for h in range(4):
                            x = slice((4 * q + h) * SP_, (4 * q + h + 1) * SP_)
                            ins = mm(ps[:, 2, x], Lx[:, k % 2, q, h, :], xdt[:, k % 2, x], start=True, stop=True)
                        ins.then_inc(y_mm, 1)
                    z_at(1)
                    if k or not isinstance(g, int) or g:
                        to_features(g, k - 1)
                    z_at(2)
            pe.wait_ge(cum_exp, 1)
            decays(0, 0)
            chunk_T(n0 + 1, None, 0, range(4, 8), 512, False, True, bank=2)
            pe.wait_ge(evac, t0 + 4)
            scan_groups(pe, group)
            to_features(SG - 1, 3)
            pe.wait_ge(yl_done, TT)
            residual("ssm_out", ys, ready=lambda: pe.wait_ge(yl_done, TT + 1))
            ffn("up1", "down1", 3)

        @block.scalar
        def _(act):
            A = act.activation

            def split_hi(n, i=None, per=0):
                act.wait_ge(landed[n % 2], 16 * (n // 2 + 1) if i is None else i * (8 * per) + 16 * (n // 2 + 1))
                if n >= 2:
                    act.wait_ge(products, at(2 * (n - 1), i, 2 * per))
                A(wh[:, n % 2, :], wraw[:, n % 2, :], ACT.Copy).then_inc(hi_done, 1)

            def square(mt, L, i, per, t):
                if L:
                    act.wait_ge(evac, at(t + mt + 1, i, per))
                if L or mt >= 2:
                    act.wait_ge(acc_done, at(8 * L + mt - 1, i, per))
                src = xT[:, mt, :] if i is None else xT[:, bass.ds(i * per + mt, 1), :].rearrange("p a n -> p (a n)")
                A(sq[:, mt % 2, :], src, ACT.Square).then_inc(sq_done, 1)

            def x_hi(L, kt):
                A(xh[:, kt, :], xT[:, kt, :], ACT.Copy, scale=col(NORMCOL[L] + kt)).then_inc(xh_done, 1)

            def norm(L):
                for kt in range(KT):
                    if L == 2:
                        act.wait_ge(scaled, kt + 1)
                        A(xh[:, kt, :], tmp[:, kt % 2, :], ACT.Copy).then_inc(xh_done, 1)
                    else:
                        x_hi(L, kt)

            def residual(name):
                ks, n0, t0 = RES[name], CHUNK[name], EVAC[name]
                per = 2 * len(ks)
                ahead = name in ("nsa_out", "ssm_out")

                def turn(i, shift):
                    for p in range(2):
                        for q in range(len(ks)):
                            n = n0 + p * len(ks) + q + 1 + shift * per
                            if n < NCHUNKS and not ahead:
                                split_hi(n, i, per)
                            if ahead and q < len(ks) - 1:
                                split_hi(n + 1)
                        if name in NORM:
                            for m in range(2):
                                square(2 * p + m + 4 * shift, NORM[name], i, 4, t0)
                        if ahead and n + 1 <= n0 + 2 * per:
                            split_hi(n + 1)
                if n0 + 2 * per < NCHUNKS and not ahead:
                    with act.Fori(0, 2) as i:
                        turn(i, 0)
                else:
                    turn(None, 0)
                    turn(None, 1)
                if name in NORM:
                    norm(NORM[name])

            def ffn(up, down, L):
                n0, t0, h0 = CHUNK[up], EVAC[up], FT * (L == 3)
                with act.Fori(0, FT // 2) as i:
                    split_hi(n0 + 1, i, 2)
                    for j in range(2):
                        act.wait_ge(gate_in, i * 2 + (h0 + j + 1))
                        A(gate[:, j, :], gate[:, j, :], ACT.Silu).then_inc(gate_done, 1)
                    split_hi(n0 + 2, i, 2)
                    for j in range(2):
                        act.wait_ge(evac, i * 2 + (t0 + j + 1))
                        A(hh[:, bass.ds(i * 2 + j, 1), :].rearrange("p a n -> p (a n)"), hid[:, j, :], ACT.Copy
                          ).then_inc(hh_done, 1)
                residual(down)

            act.wait_ge(cols_landed, 16)
            for kt in range(KT):
                if kt % 2 == 0:
                    act.wait_ge(x_landed[kt // 2], 16)
                x_hi(0, kt)
                if kt == 1:
                    split_hi(0)
            square(0, 0, None, 0, 0)
            square(1, 0, None, 0, 0)
            split_hi(1)
            for kt in range(2, KT):
                square(kt, 0, None, 0, 0)
            split_hi(2)
            act.wait_ge(rstd_done, 1)
            for tt in range(TT):
                act.wait_ge(products, 2 * 1 + 1 + tt // 2)
                A(kvc[:, tt, :], ps[:, tt, :], ACT.Copy, scale=stat[:, 24 + tt:25 + tt]).then_inc(evac, 1)
            split_hi(3)
            for kv in range(2):
                for gp in range(2):
                    act.wait_ge(kvT, 2 * kv + gp + 1)
                    for lp in range(2):
                        A(tb2[lp * DH:(lp + 1) * DH, kv, gp * 2 + 1, :], ps[DH:P, 4 + 2 * kv + gp, lp::2], ACT.Copy
                          ).then_inc(tb_act, 1)
            act.wait_ge(products, 2 * CHUNK["gates"] + 2)
            A(gates_f[:, :], ps[0:48, 4, :], ACT.Copy).then_inc(gates_out, 1)
            split_hi(4)
            act.wait_ge(angles_done, 1)
            A(sinT[:, :, :], ang[:, 8, :].rearrange("p (t f) -> p t f", f=8), ACT.Sin).then_inc(sincos_done, 1)
            A(cosT[:, :, :], ang[:, 9, :].rearrange("p (t f) -> p t f", f=8), ACT.Sin).then_inc(sincos_done, 1)
            n0, t0 = CHUNK["qkv"], EVAC["qkv"]

            def qkv_tile(tt, g, bank):
                if g is not None:
                    act.wait_ge(v_staged, g + 1)
                    act.wait_ge(qkT, g * 6 + 6)
                A(proj[:, tt, :, :].rearrange("p h d -> p (h d)"), ps[:, bank, :], ACT.Copy,
                  scale=stat[:, 24 + tt:25 + tt]).then_inc(evac, 1)
                act.wait_ge(evac, t0 + tt + 1 if g is None else g * 4 + (t0 + 4 + tt + 1))
                A(qn[:, tt, :, 0, :], proj[:, tt, 0:6, :], ACT.Square).then_inc(qk_squared, 1)

            split_hi(5)
            for tt in range(TT):
                act.wait_ge(products, 2 * n0 + 3 + tt // 2)
                qkv_tile(tt, None, tt)
            split_hi(6)
            act.wait_ge(evac, EVAC["qkv"])
            A(glin[:, :, :], glin[:, :, :], ACT.Exp, scale=-1.0).then_inc(gates_exp, 1)
            act.wait_ge(hid_mm, 4)
            for kv in range(2):
                for ht in range(2):
                    r = 2 * kv + ht
                    src, dst = ps[:, 6, r * P:(r + 1) * P], hidK[:, ht, :]
                    if kv:
                        src = src.rearrange("p (g c) -> p g c", g=GROUPS).unsqueeze(2).broadcast_to([P, GROUPS, HP, 32])
                        dst = hidV[:, ht, :, :, :]
                    A(dst, src, ACT.Silu, bias=col(COL_B1 + r)).then_inc(hid_done, 1)

            def transposed_hi(g):
                for h in range(6):
                    act.wait_ge(qkT, g * 6 + (h + 1))
                    dst = qA[:, h, :] if h < HP else kB1[:, h - HP, :]
                    A(dst, ps[:, h, :], ACT.Copy).then_inc(qkT_hi, 1)

            def group(g, more):
                def exps(s):
                    h, i = divmod(s, TT)
                    w, m = (i + 1) * P, 8 * (s % 2)
                    act.wait_ge(negmax, g * 16 + (s + 1))
                    if s >= 2:
                        act.wait_ge(pT_mm, g * 16 + (s - 1))
                    for b in range(2):
                        A(Pm[:, s % 2, b, 0:w], ps[:, 2 * (s % 2) + b, 0:w], ACT.Exp, bias=sm[:, 4, m + 2 + b:m + 3 + b],
                          scale=SCALE, accum_out=sm[:, 4, m + 4 + b:m + 5 + b]).then_inc(expd, 1)

                def pT_copy(s):
                    h, i = divmod(s, TT)
                    act.wait_ge(pT_mm, g * 16 + (s + 1))
                    if i == 0 and h >= 2:
                        act.wait_ge(pv_done, g * 4 + (h - 1))
                    A(PT[:, h % 2, :, 0:i + 1, i * P:(i + 1) * P],
                      ps[:, 4:6, 0:(i + 1) * P].rearrange("p b (j q) -> p b j q", q=P), ACT.Copy).then_inc(pT_done, 1)

                def o_copy(pr):
                    act.wait_ge(pv_done, g * 4 + 2 * (pr + 1))
                    A(xo[:, bass.ds(g * 2 + pr, 1), :].rearrange("p a n -> p (a n)"), ps[:, 6, :], ACT.Copy
                      ).then_inc(o_hi, 1)

                for k in range(18):
                    if 1 <= k <= 16:
                        exps(k - 1)
                    if k >= 2:
                        pT_copy(k - 2)
                    if k == 1:
                        act.wait_ge(cs_shifted, g + 1)
                        A(pc[:, :, :, :], pc[:, :, :, :], ACT.Exp, scale=SCALE).then_inc(cs_exp, 1)
                    if k == 4:
                        act.wait_ge(pcT_mm, g + 1)
                        A(pcT[:, :], ps[:, 6, :], ACT.Copy).then_inc(pcT_done, 1)
                    if k == 11:
                        o_copy(0)
                    if more and k in (3, 6, 9, 12):
                        tt = k // 3 - 1
                        act.wait_ge(products, g * 4 + (2 * (n0 + 2) + tt + 1))
                        qkv_tile(tt, g, 7)
                    if more and k in (14, 15):
                        act.wait_ge(products, g * 4 + 2 * (n0 + 4))
                        split_hi(n0 + 4 + k - 14, g, 2)
                if more:
                    transposed_hi(g + 1)
                o_copy(1)

            transposed_hi(0)
            act.wait_ge(cmp_mm, 1)
            A(kcn[:, 0, :], ps[:, 7, 0:DH], ACT.Square).then_inc(kc_sq, 1)
            act.wait_ge(kcT, 1)
            A(B1c[:, :], ps[:, 7, 3 * P:4 * P], ACT.Copy).then_inc(kc_hi, 1)
            with act.Fori(0, GROUPS - 1) as g:
                group(g, True)
            group(GROUPS - 1, False)
            act.wait_ge(o_lo, 2 * GROUPS)
            act.dma_start(xT[:, :, :], xT_in).then_inc(x_again, 16)
            residual("nsa_out")
            ffn("up0", "down0", 1)

            n0, t0 = CHUNK["xbc"], EVAC["xbc"]

            def to_tokens(turn, j):
                act.wait_ge(featT, turn * 4 + (j + 1))
                A(xtok[:, :, bass.ds(turn * 512 + j * P, P)], ps[:, 4 + j % 2, :].rearrange("p (t f) -> p t f", f=P),
                  ACT.Copy).then_inc(featT_done, 1)

            def conv_tiles(n, i, t, u, dst, turn=None):
                def silu(j):
                    act.wait_ge(evac, at(t + j + 1, i, 4))
                    if turn is not None:
                        after(act, featT, turn * 4 + (j - 1))
                    c = col(COL_CB + u + j) if i is None else cols[:, bass.ds(i * 4 + (COL_CB + u + j), 1)]
                    A(dst(j), tmp[:, j % 2, :], ACT.Silu, bias=c).then_inc(silu_done, 1)
                split_hi(n + 1, i, 2)
                silu(0)
                if turn is not None and not isinstance(turn, int):
                    to_tokens(turn - 1, 3)
                silu(1)
                split_hi(n + 2, i, 2)
                if turn is not None:
                    to_tokens(turn, 0)
                silu(2)
                if turn is not None:
                    to_tokens(turn, 1)
                silu(3)
                if turn is not None:
                    to_tokens(turn, 2)
            conv_tiles(n0, None, t0, 20, lambda j: BCf[:, 1, j, :])
            conv_tiles(n0 + 2, None, t0 + 4, 16, lambda j: BCf[:, 0, j, :])
            conv_tiles(n0 + 4, None, t0 + 8, 0, lambda j: sq[:, j % 2, :], 0)
            with act.Fori(0, 3) as i:
                conv_tiles(n0 + 6, i, t0 + 12, 4, lambda j: sq[:, j % 2, :], i + 1)
            split_hi(CHUNK["z"])
            to_tokens(3, 3)
            act.wait_ge(products, 2 * CHUNK["dt"] + 2)
            A(dt_f[:, :], ps[0:SH, 6, :], ACT.Copy).then_inc(dt_out, 1)
            n0, t0 = CHUNK["z"], EVAC["z"]
            split_hi(n0 + 1)
            act.wait_ge(dt_in, 1)
            A(dtb[:, 2, :], dtb[:, 1, :], ACT.Exp, scale=-1.0).then_inc(dt_e, 1)
            A(dtb[:, 9, 0:SH], rows[:, ROW_AL:ROW_AL + SH], ACT.Exp).then_inc(a_exp, 1)
            act.wait_ge(dt_u, 1)
            A(dtb[:, 7, :], dtb[:, 3, :], ACT.Ln).then_inc(dt_ln, 1)
            act.wait_ge(cum_mm, 1)
            A(ex[:, :, :], ps[:, 6, 0:3 * P].rearrange("p (k h) -> p k h", k=3), ACT.Exp).then_inc(cum_exp, 1)

            def stage(g, j):
                c = j % TT
                after(act, y_mm, g * 8 + 2 * (j - 3))
                A(bc[:, c, :, :], BCf[:, :, bass.ds(g + j // TT, 1), c * P:(c + 1) * P].rearrange("p b a n -> p (b a) n"),
                  ACT.Copy).then_inc(staged, 1)

            def decays(g, j):
                for q in range(2):
                    act.wait_ge(seg_mm, g * 8 + (2 * j + q + 1))
                    after(act, y_mm, g * 8 + 2 * (j - 1))
                    A(Lx[:, j % 2, q, :, :], ps[:, q, :].rearrange("p (h t) -> p h t", h=4), ACT.Exp
                      ).then_inc(seg_exp, 1)

            def z_copy(g, tt):
                act.wait_ge(products, g * 4 + (2 * n0 + 4 + tt + 1))
                A(zraw[:, tt % TT, :], ps[:, 5, :], ACT.Copy).then_inc(evac, 1)

            def group(g, last):
                first = isinstance(g, int) and g == 0
                for k in range(TT):
                    if k:
                        if not last:
                            z_copy(g, k - 1)
                    elif not first:
                        z_copy(g, -1)
                    if k == 0:
                        act.wait_ge(products, g * 4 + (2 * n0 + 4))
                        split_hi(n0 + 2, g, 2)
                    if k < 3 or not last:
                        decays(g, k + 1)
                    if k < 2 or not last:
                        stage(g, k + 2)
                    if k == 0:
                        if not first:
                            act.wait_ge(evac, g * 4 + (t0 + 4))
                            act.wait_ge(y_done, g * 4)
                            A(zs[:, :, :], zraw[:, :, :], ACT.Silu).then_inc(z_silu, 1)
                        split_hi(n0 + 3, g, 2)
                    if last:
                        act.wait_ge(yT_done, 9 + k)
                        A(yh[:, k, 0:12, :], yT[:, k, 0:12, :], ACT.Copy).then_inc(yh_done, 1)
                    act.wait_ge(y_done, g * 4 + (k + 1))
                    after(act, y_sq, g * 4 + k)
                    A(ysq[:, :], ybuf[:, k % 2, :], ACT.Square, accum_out=yst[:, k % 2, 0:1]).then_inc(y_sq, 1)
            stage(0, 0)
            stage(0, 1)
            decays(0, 0)
            for tt in range(TT):
                act.wait_ge(products, 2 * n0 + 3 + tt // 2)
                A(zs[:, tt, :], ps[:, 2 + tt, :], ACT.Silu).then_inc(evac, 1)
            scan_groups(act, group)
            act.wait_ge(yT_done, 4 * SG)
            A(yh[:, :, 12:16, :], yT[:, :, 12:16, :], ACT.Copy).then_inc(yh_done, 1)
            residual("ssm_out")
            ffn("up1", "down1", 3)

        @block.vector
        def _(dve):
            V = Tally(vec)
            TTo, TS, STT = dve.tensor_tensor, dve.tensor_scalar, dve.scalar_tensor_tensor

            def step(ins):
                V.inc(ins)
                V.wait(dve)

            def split_lo(n, i=None, per=0):
                s = n % 2
                dve.wait_ge(hi_done, at(n + 1, i, per))
                TTo(wl[:, s, :], wraw[:, s, :], wh[:, s, :].bitcast(F32), ALU.subtract).then_inc(lo_done, 1)

            def x_lo(L, kt):
                dve.wait_ge(xh_done, 8 * L + kt + 1)
                STT(out=xl[:, kt, :], in0=xT[:, kt, :], scalar=col(NORMCOL[L] + kt), in1=xh[:, kt, :].bitcast(F32),
                    op0=ALU.mult, op1=ALU.subtract).then_inc(xl_done, 1)

            def mean_square(L):
                dve.wait_ge(colsum_done, L + 1)
                TS(stat[:, 0:4], ps[:, 7, 0:4], 1.0 / DM, EPS, ALU.mult, ALU.add).then_inc(mean_done, 1)

            def diagonal(L):
                dve.wait_ge(rstd_done, L + 1)
                for tt in range(TT):
                    ins = TS(diag[:, tt, :], ident[:, :], stat[:, 4 + tt:5 + tt], None, ALU.mult)
                ins.then_inc(diag_done, 1)

            def norm(L):
                if L != 2:
                    for kt in range(KT):
                        x_lo(L, kt)
                mean_square(L)
                diagonal(L)
                if L != 2:
                    return
                dve.wait_ge(rbc_done, L)

                def scale(kt):
                    if kt >= 2:
                        dve.wait_ge(xl_done, 8 * L + kt - 1)
                    STT(out=tmp[:, kt % 2, :], in0=xT[:, kt, :], scalar=col(NORMCOL[L] + kt), in1=ps[:, 6, :],
                        op0=ALU.mult, op1=ALU.mult).then_inc(scaled, 1)
                scale(0)
                for kt in range(KT):
                    if kt + 1 < KT:
                        scale(kt + 1)
                    dve.wait_ge(xh_done, 8 * L + kt + 1)
                    TTo(xl[:, kt, :], tmp[:, kt % 2, :], xh[:, kt, :].bitcast(F32), ALU.subtract).then_inc(xl_done, 1)

            def residual(name):
                ks, n0, t0 = RES[name], CHUNK[name], EVAC[name]
                per = 2 * len(ks)
                ahead = name in ("nsa_out", "ssm_out")

                def turn(i, shift):
                    for p in range(2):
                        for q in range(len(ks)):
                            n = n0 + p * len(ks) + q + 1 + shift * per
                            if n < NCHUNKS and not ahead:
                                split_lo(n, i, per)
                            if ahead and q < len(ks) - 1:
                                split_lo(n + 1)
                        for m in range(2):
                            t = 2 * p + m + 4 * shift
                            last = n0 + (p + 1) * len(ks) - 1 + shift * per
                            dve.wait_ge(products, at(2 * last + m + 1, i, 2 * per))
                            x = xT[:, t, :] if i is None else xT[:, bass.ds(i * 4 + t, 1), :].rearrange(
                                "p a n -> p (a n)")
                            TTo(x, ps[:, 2 * p + m, :], x, ALU.add).then_inc(evac, 1)
                        if ahead and n + 1 <= n0 + 2 * per:
                            split_lo(n + 1)
                if n0 + 2 * per < NCHUNKS and not ahead:
                    with dve.Fori(0, 2) as i:
                        turn(i, 0)
                else:
                    turn(None, 0)
                    turn(None, 1)
                if name in NORM:
                    norm(NORM[name])

            def ffn(up, down, L):
                n0, t0, h0 = CHUNK[up], EVAC[up], FT * (L == 3)

                def turn(i):
                    split_lo(n0 + 1, i, 2)
                    if isinstance(i, int):
                        dve.wait_ge(rbc_done, L)
                        step(dve.tensor_copy(tmp[:, 0, :], ps[:, 6, :]))
                    for j in range(2):
                        dve.wait_ge(products, i * 4 + (2 * n0 + j + 1))
                        dve.wait_ge(evac, i * 2 + (t0 - 1 + j))
                        TTo(gate[:, j, :], ps[:, j, :], tmp[:, 0, :], ALU.mult).then_inc(gate_in, 1)
                    split_lo(n0 + 2, i, 2)
                    for j in range(2):
                        dve.wait_ge(products, i * 4 + (2 * n0 + 3 + j))
                        after(dve, hh_done, i * 2 + (h0 + j - 1))
                        step(TTo(hid[:, j, :], ps[:, 2 + j, :], tmp[:, 0, :], ALU.mult))
                        dve.wait_ge(gate_done, i * 2 + (h0 + j + 1))
                        TTo(hid[:, j, :], hid[:, j, :], gate[:, j, :], ALU.mult).then_inc(evac, 1)
                        dve.wait_ge(hh_done, i * 2 + (h0 + j + 1))
                        h = bass.ds(i * 2 + j, 1)
                        TTo(hl[:, h, :].rearrange("p a n -> p (a n)"), hid[:, j, :],
                            hh[:, h, :].rearrange("p a n -> p (a n)").bitcast(F32), ALU.subtract).then_inc(hl_done, 1)
                turn(0)
                with dve.Fori(0, FT // 2 - 1) as i:
                    V.enter(i, 2)
                    turn(i + 1)
                V.leave(FT // 2 - 1, 2)
                residual(down)

            dve.wait_ge(cols_landed, 16)
            for kt in range(KT):
                if kt % 2 == 0:
                    dve.wait_ge(x_landed[kt // 2], 16)
                x_lo(0, kt)
                if kt == 1:
                    split_lo(0)
            split_lo(1)
            dve.wait_ge(params_landed, 48)
            dve.tensor_copy(ident_bf[:, :], ident[:, :]).then_inc(masks_cast, 1)
            step(TTo(diag[:, 0, :], tri[:, 1, :], ident[:, :], ALU.add))
            TS(negmask_bf[:, :], diag[:, 0, :], -NEG, NEG, ALU.mult, ALU.add).then_inc(masks_cast, 1)
            mean_square(0)
            split_lo(2)
            for kv in range(2):
                for gp in range(2):
                    dve.wait_ge(kvT, 2 * kv + gp + 1)
                    for lp in range(2):
                        dve.tensor_copy(tb2[lp * DH:(lp + 1) * DH, kv, gp * 2, :], ps[0:DH, 4 + 2 * kv + gp, lp::2]
                                        ).then_inc(tb_vec, 1)
            split_lo(3)
            dve.wait_ge(tb_vec, 8)
            dve.wait_ge(tb_act, 8)
            V.inc(dve.memset(tbT[:, :, :, :, :].rearrange("p k j g c -> p (k j g) c")[:, :, NCMP:32], 0.0))
            for kv in range(2):
                for jh in range(2):
                    src = tb2[:, kv, :, 8 * jh:8 * jh + 248].rearrange("p g (c j) -> p j g c", j=8)
                    pe_ = col(COL_PE + kv * NJ + 8 * jh, 8).unsqueeze(2).unsqueeze(3).broadcast_to([P, 8, GROUPS, NCMP])
                    TTo(tbT[:, kv, 8 * jh:8 * jh + 8, :, 0:NCMP], src, pe_, ALU.add).then_inc(tbT_done, 1)
            split_lo(4)
            dve.wait_ge(rest_landed, 32)
            step(dve.tensor_copy(stat[:, 16:21], posi[:, :]))
            a0 = ang[:, 0, :].rearrange("p (t f) -> p t f", f=8)
            step(TTo(a0, stat[:, 16:21].unsqueeze(2).broadcast_to([P, 5, 8]),
                     rows[:, ROW_INV:ROW_INV + 8].unsqueeze(1).broadcast_to([P, 5, 8]), ALU.mult))
            magic = 1.5 * 2.0 ** 23
            step(TS(ang[:, 1, :], ang[:, 0, :], float(1 / (2 * np.pi)), magic, ALU.mult, ALU.add))
            step(TS(ang[:, 2, :], ang[:, 1, :], magic, None, ALU.subtract))
            c1 = 6.28125
            c2 = float(np.float32(np.round((2 * np.pi - c1) * 2.0 ** 21) / 2.0 ** 21))
            c3 = float(np.float32(2 * np.pi - c1 - c2))
            for n, cc in enumerate((c1, c2, c3)):
                step(STT(out=ang[:, 3 + n, :], in0=ang[:, 2, :], scalar=-cc, in1=ang[:, 0 if n == 0 else 2 + n, :],
                         op0=ALU.mult, op1=ALU.add))
            step(TS(ang[:, 8, :], ang[:, 5, :], PI, -PI, ALU.min, ALU.max))
            step(TS(ang[:, 6, :], ang[:, 5, :], float(np.pi / 2), None, ALU.add))
            step(TS(ang[:, 7, :], ang[:, 6, :], PI, float(-2 * np.pi), ALU.is_gt, ALU.mult))
            step(TTo(ang[:, 6, :], ang[:, 6, :], ang[:, 7, :], ALU.add))
            TS(ang[:, 9, :], ang[:, 6, :], PI, -PI, ALU.min, ALU.max).then_inc(angles_done, 1)
            dve.wait_ge(gates_T, 1)
            TTo(glin[:, :, :], ps[:, 5, 0:TT * 48].rearrange("p (t f) -> p t f", t=TT),
                stat[:, 24:28].unsqueeze(2).broadcast_to([P, TT, 48]), ALU.mult).then_inc(evac, 1)
            n0 = CHUNK["qkv"]

            def qk_norm(tt, g):
                dve.wait_ge(qk_squared, g * 4 + (tt + 1))
                step(dve.tensor_reduce(sm[:, 0, 0:6], qn[:, tt, :, 0, :], AX, ALU.add))
                TS(sm[:, 1, 0:6], sm[:, 0, 0:6], 1.0 / DH, EPS, ALU.mult, ALU.add).then_inc(qk_mean, 1)
                dve.wait_ge(qk_rstd, g * 4 + (tt + 1))
                q6 = qn[:, tt, :, 0, :]
                step(TTo(q6, proj[:, tt, 0:6, :], sm[:, 3, 0:6].unsqueeze(2).broadcast_to([P, 6, DH]), ALU.mult))
                step(TTo(q6, q6, rows[:, ROW_W6:ROW_W6 + 384].rearrange("p (h d) -> p h d", d=DH), ALU.mult))
                cc = cosT[:, tt, :].unsqueeze(1).broadcast_to([P, 6, 8])
                ss = sinT[:, tt, :].unsqueeze(1).broadcast_to([P, 6, 8])
                x1, x2 = q6[:, :, 0:8], q6[:, :, 8:16]
                V.inc(TTo(rp[:, 0], x1, cc, ALU.mult))
                V.inc(TTo(rp[:, 1], x2, ss, ALU.mult))
                V.inc(TTo(rp[:, 2], x2, cc, ALU.mult))
                step(TTo(rp[:, 3], x1, ss, ALU.mult))
                V.inc(TTo(x1, rp[:, 0], rp[:, 1], ALU.subtract))
                step(TTo(x2, rp[:, 2], rp[:, 3], ALU.add))
                dve.tensor_copy(qn[:, tt, :, 1, :], q6).then_inc(qk_normed, 1)

            def transposed_lo(g):
                for h in range(6):
                    dve.wait_ge(qkT_hi, g * 6 + (h + 1))
                    if h < HP:
                        lo = qA[DH:P, h, :]
                        TTo(lo, ps[DH:P, h, :], lo.bitcast(F32), ALU.subtract).then_inc(qkT_lo, 1)
                    else:
                        TTo(kB2[:, h - HP, :], ps[:, h, :], kB1[:, h - HP, :].bitcast(F32), ALU.subtract
                            ).then_inc(qkT_lo, 1)

            def group(g, more):
                def stage_v():
                    dve.wait_ge(vz_zeroed, 1)
                    dve.wait_ge(pv_done, g * 4)
                    dve.tensor_copy(vst[:, :, :, :], proj[:, :, 6:8, :]).then_inc(v_staged, 1)
                    for h in range(HP):
                        b = slice(32 * h, 32 * (h + 1))
                        dve.tensor_copy(vz[b, h, :], VC4[b, bass.ds(g, 1), :].rearrange("p a d -> p (a d)")
                                        ).then_inc(vz_done, 1)

                pf = pc[:, :, :, :].rearrange("p t h c -> p (t h) c")
                gt = glin[:, :, bass.ds(g * 12, 12)].rearrange("p t (h b) -> p t h b", b=3)

                def cmp_shift():
                    dve.wait_ge(cs_mm, g + 1)
                    step(TTo(pc[:, :, :, :], ps[:, 6, :].rearrange("p (t h c) -> p t h c", t=TT, h=HP),
                             cmask[:, 0].unsqueeze(2).broadcast_to([P, TT, HP, 32]), ALU.add))
                    step(dve.tensor_reduce(sm[:, 0, 8:24], pf, AX, ALU.max))
                    TTo(pf, pf, sm[:, 0, 8:24].unsqueeze(2).broadcast_to([P, 16, 32]), ALU.subtract
                        ).then_inc(cs_shifted, 1)

                def cmp_probs():
                    dve.wait_ge(cs_exp, g + 1)
                    step(dve.tensor_reduce(sm[:, 1, 8:24], pf, AX, ALU.add))
                    step(dve.reciprocal(sm[:, 2, 8:24], sm[:, 1, 8:24]))
                    step(TTo(sm[:, 3, 8:24].rearrange("p (t h) -> p t h", t=TT),
                             sm[:, 2, 8:24].rearrange("p (t h) -> p t h", t=TT), gt[:, :, :, 0], ALU.mult))
                    step(TTo(pf, pf, sm[:, 3, 8:24].unsqueeze(2).broadcast_to([P, 16, 32]), ALU.mult))
                    TTo(pc[:, :, :, :], pc[:, :, :, :], cmask[:, 1].unsqueeze(2).broadcast_to([P, TT, HP, 32]), ALU.mult
                        ).then_inc(pc_done, 1)

                def maxima(s):
                    h, i = divmod(s, TT)
                    m = 8 * (s % 2)
                    dve.wait_ge(scores, g * 16 + (s + 1))
                    step(dve.tensor_reduce(sm[:, 4, m:m + 2], ps[:, 2 * (s % 2):2 * (s % 2) + 2, 0:(i + 1) * P], AX,
                                           ALU.max))
                    TS(sm[:, 4, m + 2:m + 4], sm[:, 4, m:m + 2], -SCALE, None, ALU.mult).then_inc(negmax, 1)

                def normalize(s):
                    h, i = divmod(s, TT)
                    m = 8 * (s % 2)
                    dve.wait_ge(expd, g * 32 + 2 * (s + 1))
                    step(dve.reciprocal(sm[:, 5, m:m + 2], sm[:, 4, m + 4:m + 6]))
                    step(TTo(sm[:, 5, m + 2:m + 4], sm[:, 5, m:m + 2], gt[:, i, h, 1:3], ALU.mult))
                    for b in range(2):
                        p_ = Pm[:, s % 2, b, 0:(i + 1) * P]
                        TS(p_, p_, sm[:, 5, m + 2 + b:m + 3 + b], None, ALU.mult).then_inc(normed, 1)

                def o_rest(pr):
                    dve.wait_ge(o_hi, g * 2 + (pr + 1))
                    o = bass.ds(g * 2 + pr, 1)
                    TTo(xol[:, o, :].rearrange("p a n -> p (a n)"), ps[:, 6, :],
                        xo[:, o, :].rearrange("p a n -> p (a n)").bitcast(F32), ALU.subtract).then_inc(o_lo, 1)

                for k in range(18):
                    if k < 16:
                        maxima(k)
                    if 1 <= k <= 16:
                        normalize(k - 1)
                    if k == 0:
                        stage_v()
                        cmp_shift()
                    if k == 1:
                        cmp_probs()
                    if k == 12:
                        o_rest(0)
                    if more and k in (4, 7, 10, 13):
                        qk_norm(k // 3 - 1, g + 1)
                    if more and k in (14, 15):
                        split_lo(n0 + 4 + k - 14, g, 2)
                if more:
                    transposed_lo(g + 1)
                o_rest(1)

            split_lo(5)
            dve.wait_ge(sincos_done, 2)
            for tt in range(TT):
                qk_norm(tt, 0)
            split_lo(6)
            dve.wait_ge(gates_exp, 1)
            step(TS(glin[:, :, :], glin[:, :, :], 1.0, None, ALU.add))
            dve.reciprocal(glin[:, :, :], glin[:, :, :]).then_inc(gates_done, 1)
            transposed_lo(0)
            dve.wait_ge(kc_sq, 1)
            step(dve.tensor_reduce(stat[:, 8:9], kcn[:, 0, :], AX, ALU.add))
            TS(stat[:, 9:10], stat[:, 8:9], 1.0 / DH, EPS, ALU.mult, ALU.add).then_inc(kc_mean, 1)
            dve.tensor_copy(VC4[:, :, :], ps[:, 7, DH:(GROUPS + 1) * DH].rearrange("p (g d) -> p g d", g=GROUPS)
                            ).then_inc(vc_done, 1)
            dve.wait_ge(kc_rstd, 1)
            step(STT(out=kcn[:, 0, :], in0=ps[:, 7, 0:DH], scalar=stat[:, 11:12], in1=rows[:, ROW_KC:ROW_KC + DH],
                     op0=ALU.mult, op1=ALU.mult))
            c_, s_ = cosT[:, 4, :], sinT[:, 4, :]
            x1, x2 = kcn[:, 0, 0:8], kcn[:, 0, 8:16]
            V.inc(TTo(krp[:, 0, :], x1, c_, ALU.mult))
            V.inc(TTo(krp[:, 1, :], x2, s_, ALU.mult))
            V.inc(TTo(krp[:, 2, :], x2, c_, ALU.mult))
            step(TTo(krp[:, 3, :], x1, s_, ALU.mult))
            step(TTo(x1, krp[:, 0, :], krp[:, 1, :], ALU.subtract))
            step(TTo(x2, krp[:, 2, :], krp[:, 3, :], ALU.add))
            dve.tensor_copy(kcn[:, 1, :], kcn[:, 0, :]).then_inc(kcn_done, 1)
            dve.wait_ge(kc_hi, 1)
            TTo(B2c[:, :], ps[:, 7, 3 * P:4 * P], B1c[:, :].bitcast(F32), ALU.subtract).then_inc(kc_lo, 1)
            dve.wait_ge(gates_done, 1)
            with dve.Fori(0, GROUPS - 1) as g:
                V.enter(g, DVE_GROUP_STEPS)
                group(g, True)
            V.leave(GROUPS - 1, DVE_GROUP_STEPS)
            group(GROUPS - 1, False)
            dve.wait_ge(x_again, 16)
            residual("nsa_out")
            ffn("up0", "down0", 1)

            n0, t0 = CHUNK["xbc"], EVAC["xbc"]

            def conv_tiles(n, i, t, u):
                def taps(j):
                    dve.wait_ge(products, at(2 * (n + j // 2) + j % 2 + 1, i, 4))
                    if i is not None or t + j >= t0 + 2:
                        dve.wait_ge(silu_done, at(t - t0 + j - 1, i, 4))

                    def w(tap):
                        c0 = COL_CW + tap * 24 + u + j
                        return col(c0) if i is None else cols[:, bass.ds(i * 4 + c0, 1)]
                    c = tmp[:, j % 2, :]
                    step(TS(c, ps[:, j, :], w(3), None, ALU.mult))
                    for d in range(1, 4):
                        ins = STT(out=c[:, d:], in0=ps[:, j, 0:SEQ - d], scalar=w(3 - d), in1=c[:, d:],
                                  op0=ALU.mult, op1=ALU.add)
                        if d < 3:
                            step(ins)
                        else:
                            ins.then_inc(evac, 1)
                split_lo(n + 1, i, 2)
                taps(0)
                taps(1)
                split_lo(n + 2, i, 2)
                taps(2)
                taps(3)
            conv_tiles(n0, None, t0, 20)
            conv_tiles(n0 + 2, None, t0 + 4, 16)
            with dve.Fori(0, 4) as i:
                V.enter(i, 12)
                conv_tiles(n0 + 4, i, t0 + 8, 0)
            V.leave(4, 12)
            split_lo(CHUNK["z"])
            bias = rows[:, ROW_DTB:ROW_DTB + SH]
            dve.wait_ge(dt_T, 1)
            TTo(dtb[:, 0, :].rearrange("p (t h) -> p t h", t=TT), ps[:, 7, 0:TT * SH].rearrange("p (t h) -> p t h", t=TT),
                bias.unsqueeze(1).broadcast_to([P, TT, SH]), ALU.add).then_inc(evac, 1)
            dve.wait_ge(evac, EVAC["z"])
            step(TS(dtb[:, 4, :], dtb[:, 0, :], -1.0, None, ALU.mult))
            TTo(dtb[:, 1, :], dtb[:, 0, :], dtb[:, 4, :], ALU.max).then_inc(dt_in, 1)
            split_lo(CHUNK["z"] + 1)
            dve.wait_ge(dt_e, 1)
            TS(dtb[:, 3, :], dtb[:, 2, :], 1.0, None, ALU.add).then_inc(dt_u, 1)
            dve.wait_ge(dt_u, 1)
            step(TS(dtb[:, 4, :], dtb[:, 3, :], 1.0, None, ALU.subtract))
            step(TS(dtb[:, 5, :], dtb[:, 4, :], 0.0, None, ALU.is_equal))
            step(TTo(dtb[:, 4, :], dtb[:, 4, :], dtb[:, 5, :], ALU.add))
            step(dve.reciprocal(dtb[:, 6, :], dtb[:, 4, :]))
            dve.wait_ge(dt_ln, 1)
            step(TTo(dtb[:, 7, :], dtb[:, 7, :], dtb[:, 6, :], ALU.mult))
            step(TTo(dtb[:, 7, :], dtb[:, 7, :], dtb[:, 5, :], ALU.add))
            step(TTo(dtb[:, 7, :], dtb[:, 7, :], dtb[:, 2, :], ALU.mult))
            step(STT(out=dtb[:, 0, :], in0=dtb[:, 0, :], scalar=0.0, in1=dtb[:, 7, :], op0=ALU.max, op1=ALU.add))
            dve.wait_ge(a_exp, 1)
            STT(out=dtb[:, 1, :].rearrange("p (t h) -> p t h", t=TT), in0=dtb[:, 0, :].rearrange("p (t h) -> p t h", t=TT),
                scalar=-1.0, in1=dtb[:, 9, 0:SH].unsqueeze(1).broadcast_to([P, TT, SH]), op0=ALU.mult, op1=ALU.mult
                ).then_inc(dt_done, 1)
            dve.wait_ge(dt_done, 1)
            n0 = CHUNK["z"]

            def build_g(g, j):
                for q in range(2):
                    after(dve, seg_mm, g * 8 + (2 * j + q - 1))
                    at_ = g * SHP + ((j // TT) * SHP + (j % TT) * SH + 4 * q)
                    TTo(Gm[:, q, :, :], tri[:, 0, :].unsqueeze(1).broadcast_to([P, 4, P]),
                        dtb[:, 1, bass.ds(at_, 4)].unsqueeze(2).broadcast_to([P, 4, P]), ALU.mult).then_inc(g_built, 1)

            def stage(g, j):
                dve.wait_ge(cb_mm, g * 4 + (j + 1))
                after(dve, m_built, g * 8 + 2 * (j - 1))
                TTo(cbm[:, j % 2, :], ps[:, 6, 0:P], tri[:, 0, :], ALU.mult)
                after(dve, y_mm, g * 8 + 2 * (j - 1))
                dve.tensor_copy(btst[:, j % 2, :], ps[:, 6, P:2 * P]).then_inc(cb_done, 1)

            def y_mean_square(g, j):
                dve.wait_ge(y_sq, g * 4 + (j + 1))
                TS(yst[:, j % 2, 1:2], yst[:, j % 2, 0:1], 1.0 / GW, EPS, ALU.mult, ALU.add).then_inc(y_var, 1)

            def scale_y(g, j):
                dve.wait_ge(y_rs, g * 4 + (j + 1))
                y = ybuf[:, j % 2, :]
                TS(y, y, yst[:, j % 2, 2:3], None, ALU.mult).then_inc(y_scaled, 1)

            def to_features(g, j):
                dve.wait_ge(yT_mm, g * 4 + (j + 1))
                f = g * 4 + (j // TT) * 4
                w = cols[:, bass.ds(g * 4 + (COL_SSMN + (j // TT) * 4), 4)].unsqueeze(2).broadcast_to([P, 4, P])
                TTo(yT[:, j % TT, bass.ds(f, 4), :], ps[:, 7, :].rearrange("p (k n) -> p k n", k=4), w, ALU.mult
                    ).then_inc(yT_done, 1)

            def heads(ap):
                return ap.rearrange("p (h d) -> p h d", h=SHP)

            def group(g, last):
                first = isinstance(g, int) and g == 0

                def per_head(n, c):
                    return ex[:, n, bass.ds(g * SHP + c * SH, SHP)].unsqueeze(2).broadcast_to([P, SHP, SP_])
                for k in range(TT):
                    if k or not first:
                        y_mean_square(g, k - 1)
                    if k < 3 or not last:
                        stage(g, k + 1)
                    if k or not first:
                        scale_y(g, k - 1)
                    if k < 2 or not last:
                        build_g(g, k + 2)
                    if k == 0:
                        split_lo(n0 + 2, g, 2)
                        split_lo(n0 + 3, g, 2)
                    y = ybuf[:, k % 2, :]
                    after(dve, yT_mm, g * 4 + (k - 1))
                    if k < 3:
                        dve.wait_ge(state_mm, g * 3 + (k + 1))
                    if k:
                        dve.wait_ge(y_mm, g * 8 + (2 * k + 1))
                        V.inc(TTo(heads(y), heads(ps[:, 3, :]), per_head(0, k), ALU.mult))
                    if k in (1, 2):
                        step(TTo(heads(state[:, :]), heads(state[:, :]), per_head(2, k), ALU.mult))
                        TTo(state[:, :], state[:, :], ps[:, 4, :], ALU.add).then_inc(state_done, 1)
                    if k == 0:
                        dve.tensor_copy(state[:, :], ps[:, 4, :]).then_inc(state_done, 1)
                    dve.wait_ge(y_mm, g * 8 + 2 * (k + 1))
                    dve.wait_ge(xdt_done, g * 12 + 3 * (k + 1))
                    V.wait(dve)
                    step(TTo(y, y if k else dxs[:, k % 2, :], ps[:, 2, :], ALU.add))
                    if k:
                        step(TTo(y, y, dxs[:, k % 2, :], ALU.add))
                    if k == 0 and not first:
                        dve.wait_ge(z_silu, g)
                    TTo(y, y, zs[:, k, :], ALU.mult).then_inc(y_done, 1)
                    if k or not first:
                        to_features(g, k - 1)
                    if last:
                        dve.wait_ge(yh_done, k + 1)
                        dve.wait_ge(yT_done, 9 + k)
                        TTo(yl[:, k, 0:12, :], yT[:, k, 0:12, :], yh[:, k, 0:12, :].bitcast(F32), ALU.subtract
                            ).then_inc(yl_done, 1)
            build_g(0, 0)
            dve.wait_ge(cum_exp, 1)
            stage(0, 0)
            build_g(0, 1)
            scan_groups(dve, group, lambda i: V.enter(i, DVE_SCAN_STEPS), lambda: V.leave(SG - 2, DVE_SCAN_STEPS))
            y_mean_square(SG - 1, 3)
            scale_y(SG - 1, 3)
            to_features(SG - 1, 3)
            dve.wait_ge(yh_done, TT + 1)
            TTo(yl[:, :, 12:16, :], yT[:, :, 12:16, :], yh[:, :, 12:16, :].bitcast(F32), ALU.subtract).then_inc(yl_done, 1)
            residual("ssm_out")
            ffn("up1", "down1", 3)

        @block.gpsimd
        def _(pool):
            TTo = pool.tensor_tensor

            def rstd(dst, src, ready, value, done):
                pool.wait_ge(ready, value)
                n = src.shape[-1]
                TTo(dst, src, mhalf[:, 0:n], ALU.pow).then_inc(done, 1)
            pool.memset(mhalf[:, :], -0.5).then_inc(mhalf_set, 1)
            pool.wait_ge(mhalf_set, 1)

            def square_sum(L):
                if L:
                    pool.wait_ge(colsum_done, L)
                pool.memset(sqacc[:, :], 0.0).then_inc(zeroed, 1)
                pool.wait_ge(zeroed, L + 1)

                def add(mt, i):
                    pool.wait_ge(sq_done, at(8 * L + mt + 1, i, 2))
                    pool.wait_ge(acc_done, at(8 * L + mt, i, 2))
                    TTo(sqacc[:, :], sqacc[:, :], sq[:, mt % 2, :], ALU.add).then_inc(acc_done, 1)
                with pool.Fori(0, 4) as i:
                    add(0, i)
                    add(1, i)
                r0 = 4 if L else 24
                rstd(stat[:, r0:r0 + 4], stat[:, 0:4], mean_done, L + 1, rstd_done)
            square_sum(0)
            pool.wait_ge(rstd_done, 1)
            pool.wait_ge(masks_cast, 2)
            pool.memset(vz[:, :, :], 0.0).then_inc(vz_zeroed, 1)
            pool.wait_ge(vz_zeroed, 1)
            for n in range(4):
                rstd(sm[:, 3, 0:6], sm[:, 1, 0:6], qk_mean, n + 1, qk_rstd)
            rstd(stat[:, 11:12], stat[:, 9:10], kc_mean, 1, kc_rstd)
            with pool.Fori(0, GROUPS - 1) as g:
                for n in range(4):
                    rstd(sm[:, 3, 0:6], sm[:, 1, 0:6], qk_mean, g * 4 + (n + 5), qk_rstd)
            pool.wait_ge(o_lo, 2 * GROUPS)
            square_sum(1)
            square_sum(2)
            pool.wait_ge(cum_exp, 1)

            def heads(ap):
                return ap.rearrange("p (h d) -> p h d", h=SHP)

            def inputs(g, j):
                c, b = j % TT, j % 2
                x = xtok[:, c, bass.ds(g * GW + (j // TT) * GW, GW)].rearrange("p (h d) -> p h d", d=SP_)
                hd = g * SHP + (j // TT) * SHP

                def per_head(row):
                    return row.unsqueeze(2).broadcast_to([P, SHP, SP_])
                after(pool, y_mm, g * 8 + 2 * (j - 1))
                after(pool, y_done, g * 4 + (j - 1))
                TTo(heads(xdt[:, b, :]), x, per_head(dtb[:, 0, bass.ds(hd + c * SH, SHP)]), ALU.mult).then_inc(xdt_done, 1)
                TTo(heads(dxs[:, b, :]), x, per_head(rows[:, bass.ds(hd + ROW_D, SHP)]), ALU.mult).then_inc(xdt_done, 1)
                pool.wait_ge(xdt_done, g * 12 + (3 * j + 1))
                TTo(heads(xdd[:, b, :]), heads(xdt[:, b, :]), per_head(ex[:, 1, bass.ds(hd + c * SH, SHP)]), ALU.mult
                    ).then_inc(xdt_done, 1)
                pool.wait_ge(cb_done, g * 4 + (j + 1))
                for q in range(2):
                    pool.wait_ge(seg_exp, g * 8 + (2 * j + q + 1))
                    TTo(Lx[:, b, q, :, :], Lx[:, b, q, :, :], cbm[:, b, :].unsqueeze(1).broadcast_to([P, 4, P]),
                        ALU.mult).then_inc(m_built, 1)

            def group(g, last):
                for k in range(TT):
                    if k or not isinstance(g, int) or g:
                        rstd(yst[:, (k - 1) % 2, 2:3], yst[:, (k - 1) % 2, 1:2], y_var, g * 4 + k, y_rs)
                    if k < 3 or not last:
                        inputs(g, k + 1)
            inputs(0, 0)
            scan_groups(pool, group)
            rstd(yst[:, 1, 2:3], yst[:, 1, 1:2], y_var, 4 * SG, y_rs)
            square_sum(3)


def kernel(x, positions, mix_norm_w, ffn_norm_w, ffn_w_gate, ffn_w_up, ffn_w_down, nsa_w_in, nsa_q_norm, nsa_k_norm,
           nsa_cmp_pe, nsa_cmp_w1, nsa_cmp_b1, nsa_cmp_w2, nsa_w_out, ssm_w_in, ssm_conv_w, ssm_conv_b, ssm_dt_bias,
           ssm_a_log, ssm_d, ssm_norm_w, ssm_w_out):
    import concourse.bacc as bacc
    from concourse.bass_utils import run_bass_kernel_spmd

    def arr(a):
        return np.asarray(a)

    def f_chunks(w, kgroups):
        out = []
        for c in range(0, w.shape[1], 256):
            k0 = 0
            for nk in kgroups:
                part = w[k0 * P:(k0 + nk) * P, c:c + 256].reshape(nk, P, 256).transpose(1, 0, 2).reshape(P, -1)
                out.append(np.pad(part, ((0, 0), (0, CH - part.shape[1]))))
                k0 += nk
        return out

    def t_chunks(w):
        out = []
        for c in range(0, w.shape[1], 512):
            for k0 in (0, 4):
                out.append(w[k0 * P:(k0 + 4) * P, c:c + 512].reshape(4, P, 512).transpose(1, 0, 2).reshape(P, -1))
        return out

    def n_chunk(w):
        part = w.reshape(KT, P, w.shape[1]).transpose(1, 0, 2).reshape(P, -1)
        return [np.pad(part, ((0, 0), (0, CH - part.shape[1])))]

    w_in, s_in = arr(nsa_w_in)[0], arr(ssm_w_in)[0]
    stream = t_chunks(w_in[:, 1024:1536])
    stream += n_chunk(w_in[:, 2560:2608])
    for g in range(GROUPS):
        at = [slice(g * 256, (g + 1) * 256)] + [slice(b + g * DH, b + (g + 1) * DH) for b in (1536, 2048, 1792, 2304)]
        stream += t_chunks(np.concatenate([w_in[:, a] for a in at], 1))
    stream += f_chunks(arr(nsa_w_out)[0], [8])

    def ffn_stream(layer):
        g = f_chunks(arr(ffn_w_gate)[layer], [8])
        u = f_chunks(arr(ffn_w_up)[layer], [8])
        return [c for pair in zip(g, u) for c in pair] + f_chunks(arr(ffn_w_down)[layer], [8, 8, 6])
    stream += ffn_stream(0)
    xbc = s_in[:, DI:DI + 3072]
    stream += f_chunks(np.concatenate([xbc[:, 2560:3072], xbc[:, 2048:2560], xbc[:, 0:2048]], 1), [8])
    stream += n_chunk(s_in[:, DI + 3072:])
    stream += t_chunks(s_in[:, 0:DI])
    stream += f_chunks(arr(ssm_w_out)[0], [8, 8])
    stream += ffn_stream(1)
    assert len(stream) == NCHUNKS

    def columns(a):
        return np.asarray(a).reshape(-1, P).T
    cols = np.concatenate(
        [columns(mix_norm_w), columns(ffn_norm_w), columns(ssm_norm_w), columns(ssm_conv_b), columns(ssm_conv_w),
         columns(nsa_cmp_b1), columns(nsa_cmp_pe)], 1)
    inv = np.power(np.float32(THETA), -np.arange(ROPE_HALF, dtype=np.float32) / ROPE_HALF).astype(np.float32)
    qn_, kn_ = arr(nsa_q_norm)[0], arr(nsa_k_norm)[0]
    row = np.concatenate([qn_, qn_, qn_, qn_, kn_[1], kn_[2], kn_[0], arr(ssm_d)[0], arr(ssm_dt_bias)[0],
                          arr(ssm_a_log)[0], inv])
    rows = np.broadcast_to(row, (P, NROWS))
    pos = arr(positions)[0]
    blocks = np.concatenate([pos[CMP_BLOCK - 1::CMP_STRIDE][:NCMP], pos[-1:]])
    pos5 = np.concatenate([pos.reshape(TT, P).T, np.tile(blocks, GROUPS)[:, None]], 1).astype(np.int32)
    idx = np.arange(P)
    tri = np.stack([idx[:, None] <= idx[None, :], idx[:, None] > idx[None, :], np.ones((P, P), bool)], 1)
    t = np.arange(SEQ).reshape(TT, P).T[:, :, None]
    cend = np.arange(32) * CMP_STRIDE + CMP_BLOCK - 1
    seen = (cend[None, None, :] <= t) & (np.arange(32) < NCMP)
    cmask = np.stack([np.where(seen, 0.0, NEG), seen], 1).astype(np.float32)
    arrays = {
        "wstream": np.stack(stream),
        "xT_in": arr(x)[0].T.reshape(KT, P, SEQ).transpose(1, 0, 2),
        "cols_in": cols,
        "rows_in": rows,
        "pos_in": pos5,
        "cw1_in": arr(nsa_cmp_w1)[0].reshape(2, NJ, P, CMP_HIDDEN).transpose(2, 0, 1, 3),
        "cw2_in": arr(nsa_cmp_w2)[0].reshape(2, 2, P, DH).transpose(2, 0, 1, 3),
        "ident_in": np.eye(P, dtype=np.float32),
        "tri_in": tri.astype(np.float32),
        "cmask_in": cmask,
    }
    arrays = {k: np.ascontiguousarray(v) for k, v in arrays.items()}
    nc = bacc.Bacc("TRN2", target_bir_lowering=False, num_devices=1, dynamic_dma_scratch_size=1024)
    args = [nc.dram_tensor(k, v.shape, mybir.dt.from_np(v.dtype), kind="ExternalInput").ap()
            for k, v in arrays.items()]
    out = nc.dram_tensor("out", (P, KT, SEQ), F32, kind="ExternalOutput").ap()
    trunk(nc, *args, out)
    r = run_bass_kernel_spmd(nc, [arrays], core_ids=[0])
    return r.results[0]["out"].transpose(1, 0, 2).reshape(DM, SEQ).T[None]
```

```python
from contextlib import ExitStack

import numpy as np

import concourse.bass as bass
from concourse import mybir

F32 = mybir.dt.float32
F32R = mybir.dt.float32r
BF16 = mybir.dt.bfloat16
I32 = mybir.dt.int32
ALU = mybir.AluOpType
ACT = mybir.ActivationFunctionType
AX = mybir.AxisListType.X

P = 128
SEQ, DM = 512, 1024
TT = SEQ // P
KT = DM // P
HEADS, GROUPS, HP, DH = 16, 4, 4, 64
CMP_BLOCK, CMP_STRIDE, CMP_HIDDEN = 32, 16, 256
NCMP = (SEQ - CMP_BLOCK) // CMP_STRIDE + 1
NJ = CMP_BLOCK // 2
SCALE = DH ** -0.5
ROPE_HALF, THETA = 8, 500000.0
SH, SG, SHP, SP_, SN = 32, 4, 8, 64, 128
DI = 2048
GW = DI // SG
FF = 2816
FT = FF // P
EPS = 1e-6
CH = 2048
NEG = -1e30
PI = float(np.float32(np.pi))

COL_MIX, COL_FFN, COL_SSMN, COL_CB, COL_CW, COL_B1, COL_PE = 0, 16, 32, 48, 72, 168, 172
NCOLS = COL_PE + 2 * NJ
ROW_W6, ROW_KC, ROW_D, ROW_DTB, ROW_AL, ROW_INV = 0, 384, 448, 480, 512, 544
NROWS = 552


class Tally:
    def __init__(self, sem):
        self.sem, self.n, self.off, self.first = sem, 0, 0, 0

    def inc(self, instruction):
        instruction.then_inc(self.sem, 1)
        self.n += 1

    def wait(self, engine):
        engine.wait_ge(self.sem, self.n + self.off)

    def enter(self, i, per):
        self.off, self.first = i * per, self.n

    def leave(self, turns, per):
        assert self.n - self.first == per, (self.n - self.first, per)
        self.n, self.off = self.first + turns * per, 0


def chunk_plan():
    at, n = {}, 0
    for name, count in (("kv_cmp", 2), ("gates", 1), ("qkv", 8), ("nsa_out", 4), ("up0", 2 * FT // 2),
                        ("down0", 12), ("xbc", 12), ("dt", 1), ("z", 8), ("ssm_out", 8),
                        ("up1", 2 * FT // 2), ("down1", 12)):
        at[name] = n
        n += count
    return at, n


CHUNK, NCHUNKS = chunk_plan()
EVAC, _t = {}, 0
for _name, _count in (("kv_cmp", 4), ("gates", 1), ("qkv", 16), ("nsa_out", 8), ("up0", FT), ("down0", 8),
                      ("xbc", 24), ("dt", 1), ("z", 16), ("ssm_out", 8), ("up1", FT), ("down1", 8)):
    EVAC[_name] = _t
    _t += _count


DVE_GROUP_STEPS, DVE_SCAN_STEPS = 58, 12


def trunk(nc, wstream, xT_in, cols_in, rows_in, pos_in, cw1_in, cw2_in, ident_in, tri_in, cmask_in, out):
    with ExitStack() as ctx:
        def sb(name, shape, dt=F32, c=ctx):
            return c.enter_context(nc.sbuf_tensor(name, shape, dt))

        def sem(name):
            return ctx.enter_context(nc.semaphore(name))

        class Region:
            def __init__(self, start):
                self.end = start

            def take(self, name, shape, dt=F32):
                t = nc.alloc_sbuf_tensor_at(name, shape, dt, offset=self.end)
                self.end += -(-int(np.prod(shape[1:])) * (2 if dt == BF16 else 4) // 32) * 32
                assert self.end <= nc.SBUF_PARTITION_SIZE_BYTES, (name, self.end)
                return t

        r = Region(-(-nc.sbuf_base // 32) * 32)
        cols = r.take("cols", [P, NCOLS])
        rows = r.take("rows", [P, NROWS])
        ident = r.take("ident", [P, P])
        tri = r.take("tri", [P, 3, P])
        ident_bf = r.take("ident_bf", [P, P], BF16)
        negmask_bf = r.take("negmask_bf", [P, P], BF16)
        stat = r.take("stat", [P, 64])
        mhalf = r.take("mhalf", [P, 8])
        wraw = r.take("wraw", [P, 2, CH])
        wh = r.take("wh", [P, 2, CH], F32R)
        wl = r.take("wl", [P, 2, CH], F32R)
        scratch_at = r.end
        diag = r.take("diag", [P, TT, P])
        tmp = r.take("tmp", [P, 2, SEQ])
        sq = r.take("sq", [P, 2, SEQ])
        sqacc = r.take("sqacc", [P, SEQ])
        a = Region(scratch_at)
        rp = a.take("rope_products", [P, 4, 6, ROPE_HALF])
        pc = a.take("pc", [P, TT, HP, 32])
        vz = a.take("vz", [P, HP, DH])
        sm = a.take("sm", [P, 6, 32])
        vst = a.take("vst", [P, TT, 2, DH])
        assert a.end <= r.end
        act_at = r.end
        xh = r.take("xh", [P, KT, SEQ], F32R)
        xl = r.take("xl", [P, KT, SEQ], F32R)
        res_at = r.end
        xT = r.take("xT", [P, KT, SEQ])
        a = Region(res_at)
        kvc = a.take("kvc", [P, TT, 512])
        tb2 = a.take("tb2", [P, 2, GROUPS, 256])
        assert a.end <= r.end
        a = Region(res_at)
        Pm = a.take("Pm", [P, 2, 2, SEQ])
        kB1 = a.take("kB1", [P, 2, SEQ], F32R)
        pcT = a.take("pcT", [P, SEQ])
        assert a.end <= r.end
        arena_at = r.end
        a = Region(arena_at)
        hh = a.take("hh", [P, FT, SEQ], F32R)
        hl = a.take("hl", [P, FT, SEQ], F32R)
        gate = a.take("gate", [P, 2, SEQ])
        hid = a.take("hid", [P, 2, SEQ])
        a = Region(arena_at)
        proj = a.take("proj", [P, TT, 8, DH])
        glin = a.take("glin", [P, TT, 48])
        gates_f = a.take("gates_f", [48, SEQ])
        cosT = a.take("cosT", [P, 5, ROPE_HALF])
        sinT = a.take("sinT", [P, 5, ROPE_HALF])
        ang = a.take("ang", [P, 10, 5 * ROPE_HALF])
        posi = a.take("posi", [P, 5], I32)
        Bc = a.take("Bc", [P, 2, P], F32R)
        Bh = a.take("Bh", [P, 2, HP * (P + 32)], F32R)
        VC4 = a.take("VC4", [P, GROUPS, DH])
        cmask = a.take("cmask", [P, 2, TT, 32])
        qA = a.take("qA", [P, HP, SEQ], F32R)
        qn = a.take("qn", [P, TT, 6, 2, DH])
        kB2 = a.take("kB2", [P, 2, SEQ], F32R)
        nsa_at = a.end
        tbT = a.take("tbT", [P, 2, NJ, GROUPS, 32])
        cw1 = a.take("cw1", [P, 2, NJ, CMP_HIDDEN])
        cw2 = a.take("cw2", [P, 2, 2, DH])
        hidK = a.take("hidK", [P, 2, P])
        hidV = a.take("hidV", [P, 2, GROUPS, HP, 32])
        hid_rows = a.take("hid_rows", [P, 2, CMP_HIDDEN])
        kcn = a.take("kcn", [P, 2, DH])
        krp = a.take("krp", [P, 4, ROPE_HALF])
        a = Region(nsa_at)
        xo = a.take("xo", [P, KT, SEQ], F32R)
        xol = a.take("xol", [P, KT, SEQ], F32R)
        PT = a.take("PT", [P, 2, 2, TT, SEQ])
        a = Region(arena_at)
        xtok = a.take("xtok", [P, TT, DI])
        BCf = a.take("BCf", [P, 2, SG, SEQ])
        conv_at = a.end
        zraw = a.take("zraw", [P, TT, GW])
        zs = a.take("zs", [P, TT, GW])
        dtb = a.take("dtb", [P, 10, TT * SH])
        dt_f = a.take("dt_f", [SH, SEQ])
        ex = a.take("ex", [P, 3, TT * SH])
        bc = a.take("bc", [P, TT, 2, P])
        btst = a.take("btst", [P, 2, P])
        Gm = a.take("Gm", [P, 2, 4, P])
        Lx = a.take("Lx", [P, 2, 2, 4, P])
        state = a.take("state", [P, GW])
        ybuf = a.take("ybuf", [P, 2, GW])
        ysq = a.take("ysq", [P, GW])
        cbm = a.take("cbm", [P, 2, P])
        yst = a.take("yst", [P, 2, 4])
        a = Region(conv_at)
        rbs = a.take("rbs", [P, SEQ])
        raw = a.take("raw", [P, 2, SEQ])
        xf = a.take("xf", [P, 4, SEQ])
        assert a.end <= conv_at + 8 * TT * GW
        a = Region(arena_at)
        yT = a.take("yT", [P, TT, 16, P])
        a = Region(arena_at)
        yl = a.take("yl", [P, TT, 16, P], F32R)
        a = Region(act_at)
        yh = a.take("yh", [P, TT, 16, P], F32R)
        assert a.end <= res_at
        a = Region(scratch_at)
        xdt = a.take("xdt", [P, 2, GW])
        xdd = a.take("xdd", [P, 2, GW])
        dxs = a.take("dxs", [P, 2, GW])
        assert a.end <= act_at
        ps = ctx.enter_context(nc.psum_tensor("ps", [P, 8, SEQ], F32))

        cols_landed, params_landed, rest_landed, cw_landed, x_again, out_stored = map(
            sem, ("cols_landed", "params_landed", "rest_landed", "cw_landed", "x_again", "out_stored"))
        x_landed = [sem(f"x{k}_landed") for k in range(4)]
        landed = [sem("even_chunk_landed"), sem("odd_chunk_landed")]
        hi_done = sem("weights_hi_done")
        lo_done = sem("weights_lo_done")
        products = sem("products_done")
        evac = sem("tiles_evacuated")
        masks_cast, zeroed, sq_done, acc_done, colsum_done, mean_done, rstd_done, diag_done, rbc_done = map(
            sem, ("masks_cast", "square_sum_zeroed", "squares_done", "square_sum_done", "colsum_done",
                  "mean_square_done", "rms_rstd_done", "diag_done", "rstd_broadcast_done"))
        xh_done, xl_done, vz_zeroed, vz_done = map(sem, ("xh_done", "xl_done", "vz_zeroed", "vz_done"))
        gate_in, gate_done, hh_done, hl_done = map(sem, ("gate_normed", "gate_done", "hidden_hi_done", "hidden_lo_done"))
        vec, pool_self = map(sem, ("vector_step", "pool_step"))
        (mhalf_set, kvT, tb_act, tb_vec, tbT_done, rows_mm, rows_copied, hid_mm, hid_done, cmp_mm, kc_sq, kc_mean, kc_rstd, kcn_done, kcT, kc_hi, kc_padded, kc_staged,
         kc_lo, vc_done, angles_done, sincos_done, gates_exp, gates_done, gates_out, gates_T) = map(sem, (
             "mhalf_set", "kv_transposed", "taps_by_act", "taps_by_vec", "blocks_built", "cmp_hidden_rows", "cmp_hidden_rows_copied", "cmp_hidden_mm", "cmp_hidden_done",
             "cmp_out_mm", "kc_squared", "kc_mean_square", "kc_rstd", "kc_normed", "kc_transposed", "kc_hi_done", "kc_padded", "kc_staged",
             "kc_lo_done", "vc_copied", "angles_done", "sincos_done", "gates_exp", "gates_done", "gates_copied", "gates_transposed"))
        (qk_squared, qk_mean, qk_rstd, qk_rotated, qk_normed, qkT, qkT_hi, qkT_lo, v_staged, csT_mm, csT_done, cs_mm, cs_shifted, cs_exp, pc_done,
         pcT_mm, pcT_done, scores, negmax, expd, normed, pT_mm, pT_done, pv_done, o_hi, o_lo) = map(sem, (
             "qk_squared", "qk_mean_square", "qk_rstd", "qk_rotated", "qk_normed", "qk_transposed", "qk_hi_done", "qk_lo_done",
             "v_staged", "cmp_scoresT", "cmp_scoresT_copied", "cmp_scores", "cmp_scores_shifted", "cmp_exp", "cmp_probs_done", "cmp_probs_transposed",
             "cmp_probsT_done", "scores_done", "negmax_done", "exp_done", "probs_normed", "probs_transposed",
             "probsT_done", "pv_done", "o_hi_done", "o_lo_done"))
        (silu_done, featT, featT_done, dt_out, dt_T, dt_in, dt_e, dt_u, dt_ln, dt_done, a_exp, staged, cum_mm, cum_exp, g_built,
         seg_mm, seg_exp, m_built, cb_mm, cb_done, xdt_done, y_mm, state_mm, y_done, state_done, z_silu, z_mm, y_sq, y_var,
         y_rs, y_scaled, yT_mm, yT_done, yh_done, yl_done) = map(sem, (
             "conv_silu_done", "feature_transposed", "feature_T_done", "dt_copied", "dt_transposed",
             "dt_biased", "dt_exp", "dt_u", "dt_ln",
             "dt_done", "a_exp", "chunk_staged", "cum_mm", "cum_exp", "g_built", "segments_mm", "segments_exp",
             "m_built", "cb_mm", "cb_done", "xdt_done", "y_mm", "state_mm", "y_done", "state_done", "z_silu", "z_tile_done", "y_squared",
             "y_mean_square", "y_rstd", "y_scaled", "yT_mm", "yT_done", "yh_done", "yl_done"))

        def at(n, i, per):
            return n if i is None else i * per + n

        def col(c, n=1):
            return cols[:, c:c + n]

        def after(engine, semaphore, value):
            if not isinstance(value, int) or value > 0:
                engine.wait_ge(semaphore, value)

        def scan_groups(engine, group, enter=None, leave=None):
            group(0, False)
            with engine.Fori(0, SG - 2) as i:
                if enter:
                    enter(i)
                group(i + 1, False)
            if leave:
                leave()
            group(SG - 1, True)

        Q4 = "p (h d) -> p h d"
        RES = {"nsa_out": [8], "ssm_out": [8, 8], "down0": [8, 8, 6], "down1": [8, 8, 6]}
        NORM = {"nsa_out": 1, "down0": 2, "ssm_out": 3}
        EARLY = ("nsa_out", "down0")
        NORMCOL = [COL_MIX, COL_FFN, COL_MIX + KT, COL_FFN + KT]

        block = ctx.enter_context(nc.Block())

        @block.sync
        def _(sp):
            sp.dma_start(cols[:, :], cols_in).then_inc(cols_landed, 16)
            for k in range(4):
                sp.dma_start(xT[:, 2 * k:2 * k + 2, :], xT_in[:, 2 * k:2 * k + 2, :]).then_inc(x_landed[k], 16)
                if k == 0:
                    sp.dma_start(wraw[:, 0, :], wstream[0]).then_inc(landed[0], 16)
            sp.dma_start(wraw[:, 1, :], wstream[1]).then_inc(landed[1], 16)
            sp.dma_start(tri[:, :, :], tri_in).then_inc(params_landed, 16)
            sp.dma_start(ident[:, :], ident_in).then_inc(params_landed, 16)
            sp.dma_start(rows[:, :], rows_in).then_inc(params_landed, 16)
            sp.dma_start(posi[:, :], pos_in).then_inc(rest_landed, 16)
            sp.dma_start(cmask[:, :, :, :], cmask_in).then_inc(rest_landed, 16)
            sp.dma_start(cw1[:, :, :, :], cw1_in).then_inc(cw_landed, 16)
            sp.dma_start(cw2[:, :, :, :], cw2_in).then_inc(cw_landed, 16)
            with sp.Fori(1, NCHUNKS // 2) as i:
                for k in range(2):
                    sp.wait_ge(lo_done, 2 * i + (k - 1))
                    sp.dma_start(wraw[:, k, :], wstream[bass.ds(2 * i + k, 1)].rearrange("a p n -> p (a n)")
                                 ).then_inc(landed[k], 16)
            for t in range(KT):
                sp.wait_ge(evac, EVAC["down1"] + t + 1)
                sp.dma_start(out[:, t, :], xT[:, t, :]).then_inc(out_stored, 16)
            sp.wait_ge(out_stored, 16 * KT)

        @block.tensor
        def _(pe):
            mm = pe.matmul

            def split_product(o, wa, xa, start, stop):
                mm(o, wa[0], xa[0], start=start, stop=False)
                mm(o, wa[0], xa[1], start=False, stop=False)
                return mm(o, wa[1], xa[0], start=False, stop=stop)

            def fresh(L):
                return lambda kt: pe.wait_ge(xl_done, 8 * L + kt + 1)

            def chunk_F(n, i, per, x, ks, banks, first, last, before=None, between=None, each=None):
                pe.wait_ge(lo_done, at(n + 1, i, per))
                s = n % 2
                for m in range(2):
                    if before:
                        before(m)
                    o = ps[:, banks[m], :]
                    for k, kt in enumerate(ks):
                        w = slice(k * 256 + m * P, k * 256 + (m + 1) * P)
                        if each and m == 0:
                            each(kt)
                        hi, lo = x(kt)
                        oo = o if len(hi.shape) == 2 else o.rearrange("p (a b) -> p a b", b=P)
                        ins = split_product(oo, (wh[:, s, w], wl[:, s, w]), (hi, lo),
                                            first and k == 0, last and k == len(ks) - 1)
                    ins.then_inc(products, 1)
                    if between:
                        between(m)

            def chunk_T(n, i, per, ks, width, first, last, before=None, each=None, bank=0):
                pe.wait_ge(lo_done, at(n + 1, i, per))
                s = n % 2
                for tt in range(TT):
                    if before:
                        before(tt)
                    for k, kt in enumerate(ks):
                        w = slice(k * width, (k + 1) * width)
                        t = slice(tt * P, (tt + 1) * P)
                        if each and tt == 0:
                            each(kt)
                        ins = split_product(ps[:, bank + tt, 0:width], (xh[:, kt, t], xl[:, kt, t]),
                                            (wh[:, s, w], wl[:, s, w]), first and k == 0,
                                            last and k == len(ks) - 1)
                    if tt % 2:
                        ins.then_inc(products, 1)

            def narrow(n, width, bank):
                pe.wait_ge(lo_done, n + 1)
                s = n % 2
                for kt in range(KT):
                    w = slice(kt * width, (kt + 1) * width)
                    ins = split_product(ps[0:width, bank, :], (wh[:, s, w], wl[:, s, w]), (xh[:, kt, :], xl[:, kt, :]),
                                        kt == 0, kt == KT - 1)
                    if kt == KT // 2:
                        ins.then_inc(products, 1)
                ins.then_inc(products, 1)

            def narrow_T(src, width, bank, ready, done):
                pe.wait_ge(ready, 1)
                for tt in range(TT):
                    ins = pe.transpose(ps[:, bank, tt * width:(tt + 1) * width], src[:, tt * P:(tt + 1) * P],
                                       ident[0:width, 0:width])
                ins.then_inc(done, 1)

            def column_sums(L):
                pe.wait_ge(acc_done, 8 * (L + 1))
                for tt in range(TT):
                    ins = mm(ps[:, 7, tt:tt + 1], sqacc[:, tt * P:(tt + 1) * P], tri[:, 2, 0:1], start=True, stop=True)
                ins.then_inc(colsum_done, 1)

            def broadcast(L):
                pe.wait_ge(diag_done, L)
                mm(ps[:, 6, :], tri[:, 2, :], diag[:, :, :].rearrange("p t q -> p (t q)"), start=True, stop=True
                   ).then_inc(rbc_done, 1)

            def xs(kt):
                return xh[:, kt, :], xl[:, kt, :]

            def hs(kt):
                return hh[:, kt, :], hl[:, kt, :]

            def ys(kt):
                return yh[:, :, kt, :], yl[:, :, kt, :]

            def residual(name, x, ready=None, late=None):
                ks, n0, t0 = RES[name], CHUNK[name], EVAC[name]
                starts = [sum(ks[:q]) for q in range(len(ks))]
                per = 2 * len(ks)
                pe.wait_ge(evac, t0)

                def turn(i):
                    for p in range(2):
                        for q, nk in enumerate(ks):
                            def free(m):
                                if q == 0:
                                    pe.wait_ge(evac, i * 4 + (t0 + 2 * p + m - 3))

                            def between(m):
                                if late and isinstance(i, int) and i + p + q + m == 0:
                                    late()
                            if ready and q == 1:
                                ready()
                            chunk_F(n0 + p * len(ks) + q, i, per, x, range(starts[q], starts[q] + nk),
                                    (2 * p, 2 * p + 1), q == 0, q == len(ks) - 1, before=free, between=between)
                if late:
                    turn(0)
                    turn(1)
                else:
                    with pe.Fori(0, 2) as i:
                        turn(i)

            def ffn(up, down, L):
                n0, t0 = CHUNK[up], EVAC[up]
                pe.wait_ge(evac, t0)

                def between(m):
                    broadcast(L) if m else column_sums(L)
                chunk_F(n0, None, 0, xs, range(KT), (0, 1), True, True, between=between, each=fresh(L))
                chunk_F(n0 + 1, None, 0, xs, range(KT), (2, 3), True, True)
                with pe.Fori(0, FT // 2 - 1) as i:
                    def free(m):
                        pe.wait_ge(evac, i * 2 + (t0 + 1 + m))
                    chunk_F(n0 + 2, i, 2, xs, range(KT), (0, 1), True, True, before=free)
                    chunk_F(n0 + 3, i, 2, xs, range(KT), (2, 3), True, True)
                hidden = FT * (1 + (L == 3))
                pe.wait_ge(hl_done, hidden - 4)
                residual(down, hs, ready=lambda: pe.wait_ge(hl_done, hidden))

            chunk_T(0, None, 0, range(4), 512, True, False, each=fresh(0))
            pe.wait_ge(params_landed, 48)
            column_sums(0)
            chunk_T(1, None, 0, range(4, 8), 512, False, True, each=fresh(0))
            for kv in range(2):
                for gp in range(2):
                    for tt in range(TT):
                        pe.wait_ge(evac, tt + 1)
                        f = kv * 256 + gp * P
                        ins = pe.transpose(ps[:, 4 + 2 * kv + gp, tt * P:(tt + 1) * P], kvc[:, tt, f:f + P],
                                           ident[:, :])
                    ins.then_inc(kvT, 1)
            pe.wait_ge(tb_act, 2)
            pe.wait_ge(tb_vec, 2)
            narrow(CHUNK["gates"], 48, 4)
            for k in range(2):
                chunk_T(CHUNK["qkv"] + k, None, 0, range(4 * k, 4 * k + 4), 512, k == 0, k == 1)
                if k == 0:
                    pe.wait_ge(tb_act, 4)
                    pe.wait_ge(tb_vec, 4)
                    narrow_T(gates_f, 48, 5, gates_out, gates_T)
            pe.wait_ge(cw_landed, 32)
            for kv in range(2):
                pe.wait_ge(tbT_done, 2 * (kv + 1))
                for j in range(NJ):
                    ins = mm(ps[:, 6 + kv, 0:CMP_HIDDEN], tbT[:, kv, j, :, :].rearrange("p g c -> p (g c)"),
                             cw1[:, kv, j, :], start=j == 0, stop=j == NJ - 1)
                ins.then_inc(rows_mm, 1)

            def qk_transposes(g, heads, bank):
                pe.wait_ge(qk_normed, g * 4 + 4)
                for h in heads:
                    for tt in range(TT):
                        ins = pe.transpose(ps[:, bank(h), tt * P:(tt + 1) * P],
                                           qn[:, tt, h, :, :].rearrange("p a d -> p (a d)"), ident[:, :])
                    ins.then_inc(qkT, 1)

            def group(g, more):
                def qk(s):
                    h, i = divmod(s, TT)
                    w = (i + 1) * P
                    if s >= 2:
                        pe.wait_ge(expd, g * 32 + 2 * (s - 1))
                    for b in range(2):
                        o = ps[:, 2 * (s % 2) + b, :]
                        q = qA[:, h, i * P:(i + 1) * P]
                        mm(o[:, 0:w], q, kB1[:, b, 0:w], start=True, stop=False)
                        mm(o[:, 0:w], q, kB2[:, b, 0:w], start=False, stop=False)
                        ins = mm(o[:, i * P:w], ident_bf[:, :], negmask_bf[:, :], start=False, stop=True)
                    ins.then_inc(scores, 1)

                def cmp_scoresT():
                    pe.wait_ge(kc_staged, g + 1)
                    pe.wait_ge(o_lo, g * 2)
                    for h in range(HP):
                        for b in range(2):
                            ins = mm(ps[:, 6, :], Bh[:, b, h * P:(h + 1) * P], qA[:, h, :], start=h + b == 0,
                                     stop=h == HP - 1 and b == 1)
                    ins.then_inc(csT_mm, 1)

                def cmp_scores():
                    pe.wait_ge(csT_done, g + 1)
                    for tt in range(TT):
                        ins = pe.transpose(ps[:, 6, tt * P:(tt + 1) * P], pcT[:, tt * P:(tt + 1) * P], ident[:, :])
                    ins.then_inc(cs_mm, 1)

                def cmp_transposes():
                    pe.wait_ge(pc_done, g + 1)
                    for tt in range(TT):
                        ins = pe.transpose(ps[:, 6, tt * P:(tt + 1) * P], pc[:, tt, :, :].rearrange("p h c -> p (h c)"),
                                           ident[:, :])
                    ins.then_inc(pcT_mm, 1)

                def pT(s):
                    h, i = divmod(s, TT)
                    pe.wait_ge(normed, g * 32 + 2 * (s + 1))
                    if s:
                        pe.wait_ge(pT_done, g * 16 + s)
                    for b in range(2):
                        for j in range(i + 1):
                            ins = pe.transpose(ps[:, 4 + b, j * P:(j + 1) * P], Pm[:, s % 2, b, j * P:(j + 1) * P],
                                               ident[:, :])
                    ins.then_inc(pT_mm, 1)

                def pv(h):
                    o = ps[DH * (h % 2):DH * (h % 2 + 1), 6, :]
                    if h == 0:
                        pe.wait_ge(v_staged, g + 1)
                        pe.wait_ge(pcT_done, g + 1)
                        pe.wait_ge(vz_done, g * 4 + 4)
                    if h == 2:
                        pe.wait_ge(o_lo, g * 2 + 1)
                    pe.wait_ge(pT_done, g * 16 + 4 * (h + 1))
                    mm(o, vz[:, h, :], pcT[:, :], start=True, stop=False)
                    for b in range(2):
                        for j in range(TT):
                            ins = mm(o[:, j * P:], vst[:, j, b, :], PT[:, h % 2, b, j, j * P:], start=False,
                                     stop=b == 1 and j == TT - 1)
                    ins.then_inc(pv_done, 1)

                n0, t0 = CHUNK["qkv"] + 2, EVAC["qkv"] + 4

                def project(part):
                    tt, third = divmod(part, 3)
                    if part == 0:
                        pe.wait_ge(lo_done, g * 2 + (n0 + 2))
                    if third == 0:
                        pe.wait_ge(evac, g * 4 + (t0 + tt))
                    t = slice(tt * P, (tt + 1) * P)
                    for m in range(8 * third, 8 * third + 8):
                        kt, pss = divmod(m, 3)
                        slot, w = (n0 + kt // 4) % 2, slice((kt % 4) * 512, (kt % 4 + 1) * 512)
                        ins = mm(ps[:, 7, :], (xh, xl, xh)[pss][:, kt, t], (wh, wh, wl)[pss][:, slot, w],
                                 start=m == 0, stop=m == 23)
                    if third == 2:
                        ins.then_inc(products, 1)

                for k in range(18):
                    if k in (8, 12, 16):
                        pv((k - 8) // 4)
                    if k < 16:
                        qk(k)
                    if k == 0:
                        cmp_scoresT()
                    if k == 1:
                        cmp_scores()
                    if k == 5:
                        cmp_transposes()
                    if k >= 2:
                        pT(k - 2)
                    if more and k < 12:
                        project(k)
                    if more and k == 16:
                        pe.wait_ge(evac, g * 4 + (t0 + 4))
                        qk_transposes(g + 1, (0, 1, 2), lambda h: (h - 1) % 8)
                    if more and k == 17:
                        qk_transposes(g + 1, (3, 4), lambda h: h - 1)
                        pe.wait_ge(qkT_lo, g * 6 + 7)
                        qk_transposes(g + 1, (5,), lambda h: 7)
                pv(3)

            pe.wait_ge(evac, EVAC["qkv"])
            for kv in range(2):
                pe.wait_ge(rows_copied, kv + 1)
                for ht in range(2):
                    ins = pe.transpose(ps[:, 4 + kv, ht * P:(ht + 1) * P], hid_rows[:, kv, ht * P:(ht + 1) * P],
                                       ident[:, :])
                ins.then_inc(hid_mm, 1)
            qk_transposes(0, (0, 1, 2), lambda h: h)
            pe.wait_ge(hid_done, 4)
            for ht in range(2):
                mm(ps[:, 6, 0:DH], hidK[:, ht, :], cw2[:, 0, ht, :], start=ht == 0, stop=ht == 1)
            for g in range(GROUPS):
                for ht in range(2):
                    lhs = hidV[:, ht, g, :, :].rearrange("p h c -> p (h c)")
                    ins = mm(ps[:, 6, (g + 1) * DH:(g + 2) * DH], lhs, cw2[:, 1, ht, :], start=ht == 0, stop=ht == 1)
            ins.then_inc(cmp_mm, 1)
            qk_transposes(0, (3, 4, 5), lambda h: (3, 7, 4)[h - 3])
            pe.wait_ge(kcn_done, 1)
            pe.transpose(ps[:, 6, 3 * P:4 * P], kcn[:, :, :].rearrange("p a d -> p (a d)"), ident[:, :]
                         ).then_inc(kcT, 1)
            pe.wait_ge(masks_cast, 2)
            pe.wait_ge(qkT_lo, 6)
            with pe.Fori(0, GROUPS - 1) as g:
                group(g, True)
                pe.wait_ge(qkT_lo, g * 6 + 12)
            group(GROUPS - 1, False)
            pe.wait_ge(o_lo, 2 * GROUPS)
            residual("nsa_out", lambda kt: (xo[:, kt, :], xol[:, kt, :]))
            ffn("up0", "down0", 1)

            n0, t0 = CHUNK["xbc"], EVAC["xbc"]
            pe.wait_ge(evac, t0)

            def transposes(turn, j):
                pe.wait_ge(silu_done, turn * 4 + (8 + j + 1))
                after(pe, featT_done, turn * 4 + (j - 1))
                for tt in range(TT):
                    ins = pe.transpose(ps[:, 4 + j % 2, tt * P:(tt + 1) * P], xf[:, j, tt * P:(tt + 1) * P],
                                       ident[:, :])
                ins.then_inc(featT, 1)

            def conv_tiles(n, i, t, turn=None, each=None):
                def free(m):
                    pe.wait_ge(evac, at(t + m - 3, i, 4))

                def free2(m):
                    pe.wait_ge(evac, at(t + 2 + m - 3, i, 4))

                def between(m):
                    if each:
                        broadcast(2) if m else column_sums(2)
                    if turn is not None and not isinstance(turn, int):
                        transposes(turn - 1, 2 + m)

                def between2(m):
                    if turn is not None:
                        transposes(turn, m)
                chunk_F(n, i, 2, xs, range(KT), (0, 1), True, True, before=free, between=between, each=each)
                chunk_F(n + 1, i, 2, xs, range(KT), (2, 3), True, True, before=free2, between=between2)
            conv_tiles(n0, None, t0, each=fresh(2))
            conv_tiles(n0 + 2, None, t0 + 4)
            conv_tiles(n0 + 4, None, t0 + 8, 0)
            with pe.Fori(0, 3) as i:
                conv_tiles(n0 + 6, i, t0 + 12, i + 1)
            narrow(CHUNK["dt"], SH, 6)
            transposes(3, 2)
            transposes(3, 3)
            narrow_T(dt_f, SH, 7, dt_out, dt_T)
            n0, t0 = CHUNK["z"], EVAC["z"]
            pe.wait_ge(evac, EVAC["dt"])

            def z_bank(tt):
                if tt >= 2:
                    pe.wait_ge(featT_done, 13 + tt)
            chunk_T(n0, None, 0, range(4), 512, True, False, before=z_bank, bank=2)
            pe.wait_ge(dt_done, 1)
            for k in range(3):
                ins = mm(ps[:, 6, k * P:(k + 1) * P], tri[:, k, :], dtb[:, 1, :], start=True, stop=True)
            ins.then_inc(cum_mm, 1)

            def decays(g, j):
                for q in range(2):
                    pe.wait_ge(g_built, g * 8 + (2 * j + q + 1))
                    after(pe, seg_exp, g * 8 + (2 * j + q - 1))
                    mm(ps[:, q, :], tri[:, 1, :], Gm[:, q, :, :].rearrange("p h t -> p (h t)"), start=True, stop=True
                       ).then_inc(seg_mm, 1)
                pe.wait_ge(staged, g * 4 + (j + 1))
                after(pe, cb_done, g * 4 + j)
                mm(ps[:, 6, 0:P], bc[:, j % TT, 0, :], bc[:, j % TT, 1, :], start=True, stop=True)
                pe.transpose(ps[:, 6, P:2 * P], bc[:, j % TT, 0, :], ident[:, :]).then_inc(cb_mm, 1)

            def to_features(g, j):
                pe.wait_ge(y_scaled, g * 4 + (j + 1))
                after(pe, yT_done, g * 4 + j)
                for f in range(4):
                    ins = pe.transpose(ps[:, 7, f * P:(f + 1) * P], ybuf[:, j % 2, f * P:(f + 1) * P], ident[:, :])
                ins.then_inc(yT_mm, 1)

            def group(g, last):
                def z_part(tt, third):
                    if third == 0:
                        if tt == 0:
                            pe.wait_ge(lo_done, g * 2 + (n0 + 3))
                        pe.wait_ge(evac, g * 4 + (t0 + 4 + tt))
                    t = slice(tt * P, (tt + 1) * P)
                    for m in range(8 * third, 8 * third + 8):
                        kt, pss = divmod(m, 3)
                        slot, w = (n0 + kt // 4) % 2, slice((kt % 4) * 512, (kt % 4 + 1) * 512)
                        if m == 12 and tt == 0:
                            pe.wait_ge(lo_done, g * 2 + (n0 + 4))
                        ins = mm(ps[:, 5, :], (xh, xl, xh)[pss][:, kt, t], (wh, wh, wl)[pss][:, slot, w],
                                 start=m == 0, stop=m == 23)
                        if tt == 3 and m in (11, 23):
                            ins.then_inc(products, 2)
                        elif m == 23:
                            ins.then_inc(z_mm, 1)

                places = {0: ((), (), (0, 1, 2)), 1: ((0,), (1,), (2,)), 2: ((0,), (1,), (2,)), 3: ((0, 1), (2,), ())}
                for k in range(TT):
                    if k < 3 or not last:
                        decays(g, k + 1)

                    def z_at(place):
                        for third in () if last else places[k][place]:
                            z_part(k, third)
                    z_at(0)
                    after(pe, y_done, g * 4 + k)
                    pe.wait_ge(xdt_done, g * 12 + 3 * (k + 1))
                    if k:
                        pe.wait_ge(state_done, g * 3 + k)
                        mm(ps[:, 3, :], bc[:, k, 1, :], state[:, :], start=True, stop=True)
                    if k < 3:
                        after(pe, state_done, g * 3 + k)
                        mm(ps[:, 4, :], btst[:, k % 2, :], xdd[:, k % 2, :], start=True, stop=True
                           ).then_inc(state_mm, 1)
                    for q in range(2):
                        pe.wait_ge(m_built, g * 8 + (2 * k + q + 1))
                        for h in range(4):
                            x = slice((4 * q + h) * SP_, (4 * q + h + 1) * SP_)
                            ins = mm(ps[:, 2, x], Lx[:, k % 2, q, h, :], xdt[:, k % 2, x], start=True, stop=True)
                        ins.then_inc(y_mm, 1)
                    z_at(1)
                    if k or not isinstance(g, int) or g:
                        to_features(g, k - 1)
                    z_at(2)
            pe.wait_ge(cum_exp, 1)
            decays(0, 0)
            chunk_T(n0 + 1, None, 0, range(4, 8), 512, False, True, bank=2)
            pe.wait_ge(evac, t0 + 4)
            scan_groups(pe, group)
            pe.wait_ge(yl_done, TT)
            residual("ssm_out", ys, ready=lambda: pe.wait_ge(yl_done, TT + 1), late=lambda: to_features(SG - 1, 3))
            ffn("up1", "down1", 3)

        @block.scalar
        def _(act):
            A = act.activation

            def split_hi(n, i=None, per=0):
                act.wait_ge(landed[n % 2], 16 * (n // 2 + 1) if i is None else i * (8 * per) + 16 * (n // 2 + 1))
                if n >= 2:
                    act.wait_ge(products, at(2 * (n - 1), i, 2 * per))
                A(wh[:, n % 2, :], wraw[:, n % 2, :], ACT.Copy).then_inc(hi_done, 1)

            def square(mt, L, i, per, t):
                if L:
                    act.wait_ge(evac, at(t + mt + 1, i, per))
                if L or mt >= 2:
                    act.wait_ge(acc_done, at(8 * L + mt - 1, i, per))
                src = xT[:, mt, :] if i is None else xT[:, bass.ds(i * per + mt, 1), :].rearrange("p a n -> p (a n)")
                A(sq[:, mt % 2, :], src, ACT.Square).then_inc(sq_done, 1)

            def x_hi(L, kt):
                if isinstance(kt, int):
                    A(xh[:, kt, :], xT[:, kt, :], ACT.Copy, scale=col(NORMCOL[L] + kt)).then_inc(xh_done, 1)
                else:
                    k = bass.ds(kt, 1)
                    A(xh[:, k, :].rearrange("p a n -> p (a n)"), xT[:, k, :].rearrange("p a n -> p (a n)"), ACT.Copy,
                      scale=cols[:, bass.ds(kt + NORMCOL[L], 1)]).then_inc(xh_done, 1)

            def residual(name):
                ks, n0, t0 = RES[name], CHUNK[name], EVAC[name]
                per = 2 * len(ks)
                ahead = name in ("nsa_out", "ssm_out")

                def turn(i, shift):
                    for p in range(2):
                        for q in range(len(ks)):
                            n = n0 + p * len(ks) + q + 1 + shift * per
                            if n < NCHUNKS and not ahead:
                                split_hi(n, i, per)
                            if ahead and q < len(ks) - 1:
                                split_hi(n + 1)
                        if name in NORM:
                            for m in range(2):
                                t = 2 * p + m + 4 * shift
                                square(t, NORM[name], i, 4, t0)
                                if name in EARLY:
                                    x_hi(NORM[name], t if i is None else i * 4 + t)
                        if ahead and n + 1 <= n0 + 2 * per:
                            split_hi(n + 1)
                if n0 + 2 * per < NCHUNKS and not ahead:
                    with act.Fori(0, 2) as i:
                        turn(i, 0)
                else:
                    turn(None, 0)
                    turn(None, 1)
                if name in NORM and name not in EARLY:
                    for kt in range(KT):
                        x_hi(NORM[name], kt)

            def ffn(up, down, L):
                n0, t0, h0 = CHUNK[up], EVAC[up], FT * (L == 3)
                with act.Fori(0, FT // 2) as i:
                    split_hi(n0 + 1, i, 2)
                    for j in range(2):
                        act.wait_ge(gate_in, i * 2 + (h0 + j + 1))
                        A(gate[:, j, :], gate[:, j, :], ACT.Silu).then_inc(gate_done, 1)
                    split_hi(n0 + 2, i, 2)
                    for j in range(2):
                        act.wait_ge(evac, i * 2 + (t0 + j + 1))
                        A(hh[:, bass.ds(i * 2 + j, 1), :].rearrange("p a n -> p (a n)"), hid[:, j, :], ACT.Copy
                          ).then_inc(hh_done, 1)
                residual(down)

            act.wait_ge(cols_landed, 16)
            for kt in range(KT):
                if kt % 2 == 0:
                    act.wait_ge(x_landed[kt // 2], 16)
                x_hi(0, kt)
                if kt == 1:
                    split_hi(0)
            square(0, 0, None, 0, 0)
            square(1, 0, None, 0, 0)
            split_hi(1)
            for kt in range(2, KT):
                square(kt, 0, None, 0, 0)
            split_hi(2)
            act.wait_ge(rstd_done, 1)
            for tt in range(TT):
                act.wait_ge(products, 2 * 1 + 1 + tt // 2)
                A(kvc[:, tt, :], ps[:, tt, :], ACT.Copy, scale=stat[:, 24 + tt:25 + tt]).then_inc(evac, 1)
            split_hi(3)
            for kv in range(2):
                for gp in range(2):
                    act.wait_ge(kvT, 2 * kv + gp + 1)
                    for lp in range(2):
                        A(tb2[lp * DH:(lp + 1) * DH, kv, gp * 2 + 1, :], ps[DH:P, 4 + 2 * kv + gp, lp::2], ACT.Copy
                          ).then_inc(tb_act, 1)
            act.wait_ge(products, 2 * CHUNK["gates"] + 2)
            A(gates_f[:, :], ps[0:48, 4, :], ACT.Copy).then_inc(gates_out, 1)
            split_hi(4)
            act.wait_ge(angles_done, 1)
            A(sinT[:, :, :], ang[:, 8, :].rearrange("p (t f) -> p t f", f=8), ACT.Sin).then_inc(sincos_done, 1)
            A(cosT[:, :, :], ang[:, 9, :].rearrange("p (t f) -> p t f", f=8), ACT.Sin).then_inc(sincos_done, 1)
            n0, t0 = CHUNK["qkv"], EVAC["qkv"]

            def qkv_tile(tt, g, bank):
                if g is not None:
                    act.wait_ge(v_staged, g + 1)
                    act.wait_ge(qkT, g * 6 + 6)
                A(proj[:, tt, :, :].rearrange("p h d -> p (h d)"), ps[:, bank, :], ACT.Copy,
                  scale=stat[:, 24 + tt:25 + tt]).then_inc(evac, 1)
                act.wait_ge(evac, t0 + tt + 1 if g is None else g * 4 + (t0 + 4 + tt + 1))
                A(qn[:, tt, :, 0, :], proj[:, tt, 0:6, :], ACT.Square).then_inc(qk_squared, 1)

            split_hi(5)
            for tt in range(TT):
                act.wait_ge(products, 2 * n0 + 3 + tt // 2)
                qkv_tile(tt, None, tt)
            split_hi(6)
            act.wait_ge(evac, EVAC["qkv"])
            A(glin[:, :, :], glin[:, :, :], ACT.Exp, scale=-1.0).then_inc(gates_exp, 1)
            for kv in range(2):
                act.wait_ge(rows_mm, kv + 1)
                A(hid_rows[:, kv, :], ps[:, 6 + kv, 0:CMP_HIDDEN], ACT.Copy).then_inc(rows_copied, 1)
            for kv in range(2):
                act.wait_ge(hid_mm, kv + 1)
                for ht in range(2):
                    r = 2 * kv + ht
                    src, dst = ps[:, 4 + kv, ht * P:(ht + 1) * P], hidK[:, ht, :]
                    if kv:
                        src = src.rearrange("p (g c) -> p g c", g=GROUPS).unsqueeze(2).broadcast_to([P, GROUPS, HP, 32])
                        dst = hidV[:, ht, :, :, :]
                    A(dst, src, ACT.Silu, bias=col(COL_B1 + r)).then_inc(hid_done, 1)

            def transposed_hi(g, heads, bank):
                for h in heads:
                    act.wait_ge(qkT, g * 6 + (h + 1))
                    dst = qA[:, h, :] if h < HP else kB1[:, h - HP, :]
                    A(dst, ps[:, bank(h), :], ACT.Copy).then_inc(qkT_hi, 1)

            def group(g, more):
                def exps(s):
                    h, i = divmod(s, TT)
                    w, m = (i + 1) * P, 8 * (s % 2)
                    act.wait_ge(negmax, g * 16 + (s + 1))
                    if s >= 2:
                        act.wait_ge(pT_mm, g * 16 + (s - 1))
                    for b in range(2):
                        A(Pm[:, s % 2, b, 0:w], ps[:, 2 * (s % 2) + b, 0:w], ACT.Exp, bias=sm[:, 4, m + 2 + b:m + 3 + b],
                          scale=SCALE, accum_out=sm[:, 4, m + 4 + b:m + 5 + b]).then_inc(expd, 1)

                def pT_copy(s):
                    h, i = divmod(s, TT)
                    act.wait_ge(pT_mm, g * 16 + (s + 1))
                    if i == 0 and h >= 2:
                        act.wait_ge(pv_done, g * 4 + (h - 1))
                    A(PT[:, h % 2, :, 0:i + 1, i * P:(i + 1) * P],
                      ps[:, 4:6, 0:(i + 1) * P].rearrange("p b (j q) -> p b j q", q=P), ACT.Copy).then_inc(pT_done, 1)

                def o_copy(pr):
                    act.wait_ge(pv_done, g * 4 + 2 * (pr + 1))
                    A(xo[:, bass.ds(g * 2 + pr, 1), :].rearrange("p a n -> p (a n)"), ps[:, 6, :], ACT.Copy
                      ).then_inc(o_hi, 1)

                for k in range(18):
                    if 1 <= k <= 16:
                        exps(k - 1)
                    if more and k in (3, 6, 9, 12):
                        tt = k // 3 - 1
                        act.wait_ge(products, g * 4 + (2 * (n0 + 2) + tt + 1))
                        qkv_tile(tt, g, 7)
                    if k >= 2:
                        pT_copy(k - 2)
                    if k == 0:
                        act.wait_ge(csT_mm, g + 1)
                        A(pcT[:, :], ps[:, 6, :], ACT.Copy).then_inc(csT_done, 1)
                    if k == 2:
                        act.wait_ge(cs_shifted, g + 1)
                        A(pc[:, :, :, :], pc[:, :, :, :], ACT.Exp, scale=SCALE).then_inc(cs_exp, 1)
                    if k == 5:
                        act.wait_ge(pcT_mm, g + 1)
                        A(pcT[:, :], ps[:, 6, :], ACT.Copy).then_inc(pcT_done, 1)
                    if k == 13:
                        o_copy(0)
                    if more and k == 16:
                        transposed_hi(g + 1, (0, 1, 2), lambda h: (h - 1) % 8)
                    if more and k == 17:
                        transposed_hi(g + 1, (3, 4, 5), lambda h: h - 1 if h < 5 else 7)
                    if more and k in (14, 15):
                        act.wait_ge(products, g * 4 + 2 * (n0 + 4))
                        split_hi(n0 + 4 + k - 14, g, 2)
                o_copy(1)

            transposed_hi(0, (0, 1, 2), lambda h: h)
            act.wait_ge(cmp_mm, 1)
            A(kcn[:, 0, :], ps[:, 6, 0:DH], ACT.Square).then_inc(kc_sq, 1)
            transposed_hi(0, (3, 4, 5), lambda h: (3, 7, 4)[h - 3])
            act.wait_ge(kcT, 1)
            A(Bc[:, 0, :], ps[:, 6, 3 * P:4 * P], ACT.Copy).then_inc(kc_hi, 1)
            with act.Fori(0, GROUPS - 1) as g:
                group(g, True)
            group(GROUPS - 1, False)
            act.wait_ge(o_lo, 2 * GROUPS)
            act.dma_start(xT[:, :, :], xT_in).then_inc(x_again, 16)
            residual("nsa_out")
            ffn("up0", "down0", 1)

            n0, t0 = CHUNK["xbc"], EVAC["xbc"]

            def to_tokens(turn, j):
                act.wait_ge(featT, turn * 4 + (j + 1))
                A(xtok[:, :, bass.ds(turn * 512 + j * P, P)], ps[:, 4 + j % 2, :].rearrange("p (t f) -> p t f", f=P),
                  ACT.Copy).then_inc(featT_done, 1)

            def conv_tiles(n, i, t, u, dst, turn=None):
                def silu(j):
                    act.wait_ge(evac, at(t + j + 1, i, 4))
                    if turn is not None:
                        after(act, featT, turn * 4 + (j - 3))
                    c = col(COL_CB + u + j) if i is None else cols[:, bass.ds(i * 4 + (COL_CB + u + j), 1)]
                    A(dst(j), tmp[:, j % 2, :], ACT.Silu, bias=c).then_inc(silu_done, 1)
                for j in range(4):
                    if j % 2:
                        split_hi(n + 2 + j // 2, i, 2)
                    silu(j)
                    if turn is not None and (j >= 2 or not isinstance(turn, int)):
                        to_tokens(turn if j >= 2 else turn - 1, (j + 2) % 4)
            split_hi(n0 + 1)
            conv_tiles(n0, None, t0, 20, lambda j: BCf[:, 1, j, :])
            conv_tiles(n0 + 2, None, t0 + 4, 16, lambda j: BCf[:, 0, j, :])
            conv_tiles(n0 + 4, None, t0 + 8, 0, lambda j: xf[:, j, :], 0)
            with act.Fori(0, 3) as i:
                conv_tiles(n0 + 6, i, t0 + 12, 4, lambda j: xf[:, j, :], i + 1)
            to_tokens(3, 2)
            to_tokens(3, 3)
            act.wait_ge(products, 2 * CHUNK["dt"] + 2)
            A(dt_f[:, :], ps[0:SH, 6, :], ACT.Copy).then_inc(dt_out, 1)
            n0, t0 = CHUNK["z"], EVAC["z"]
            split_hi(n0 + 1)
            act.wait_ge(dt_in, 1)
            A(dtb[:, 2, :], dtb[:, 1, :], ACT.Exp, scale=-1.0).then_inc(dt_e, 1)
            A(dtb[:, 9, 0:SH], rows[:, ROW_AL:ROW_AL + SH], ACT.Exp).then_inc(a_exp, 1)
            act.wait_ge(dt_u, 1)
            A(dtb[:, 7, :], dtb[:, 3, :], ACT.Ln).then_inc(dt_ln, 1)
            act.wait_ge(cum_mm, 1)
            A(ex[:, :, :], ps[:, 6, 0:3 * P].rearrange("p (k h) -> p k h", k=3), ACT.Exp).then_inc(cum_exp, 1)

            def stage(g, j):
                c = j % TT
                after(act, y_mm, g * 8 + 2 * (j - 3))
                A(bc[:, c, :, :], BCf[:, :, bass.ds(g + j // TT, 1), c * P:(c + 1) * P].rearrange("p b a n -> p (b a) n"),
                  ACT.Copy).then_inc(staged, 1)

            def decays(g, j):
                for q in range(2):
                    act.wait_ge(seg_mm, g * 8 + (2 * j + q + 1))
                    after(act, y_mm, g * 8 + 2 * (j - 1))
                    A(Lx[:, j % 2, q, :, :], ps[:, q, :].rearrange("p (h t) -> p h t", h=4), ACT.Exp
                      ).then_inc(seg_exp, 1)

            def z_copy(g, tt):
                if tt in (-1, 3):
                    act.wait_ge(products, g * 4 + (2 * n0 + 4 + tt + 1))
                else:
                    act.wait_ge(z_mm, g * 3 + (tt + 1))
                A(zraw[:, tt % TT, :], ps[:, 5, :], ACT.Copy, scale=stat[:, 4 + tt % TT:5 + tt % TT]).then_inc(evac, 1)

            def group(g, last):
                first = isinstance(g, int) and g == 0
                for k in range(TT):
                    if k:
                        if not last:
                            z_copy(g, k - 1)
                    elif not first:
                        z_copy(g, -1)
                    if k == 0:
                        split_hi(n0 + 3, g, 2)
                    if k < 3 or not last:
                        decays(g, k + 1)
                    if k < 2 or not last:
                        stage(g, k + 2)
                    if k == 0:
                        if not first:
                            act.wait_ge(evac, g * 4 + (t0 + 4))
                            act.wait_ge(y_done, g * 4)
                            A(zs[:, :, :], zraw[:, :, :], ACT.Silu).then_inc(z_silu, 1)
                    if k == 3 and not last:
                        split_hi(n0 + 4, g, 2)
                    if last:
                        act.wait_ge(yT_done, 9 + k)
                        A(yh[:, k, 0:12, :], yT[:, k, 0:12, :], ACT.Copy).then_inc(yh_done, 1)
                    act.wait_ge(y_done, g * 4 + (k + 1))
                    after(act, y_sq, g * 4 + k)
                    A(ysq[:, :], ybuf[:, k % 2, :], ACT.Square, accum_out=yst[:, k % 2, 0:1]).then_inc(y_sq, 1)
            stage(0, 0)
            stage(0, 1)
            decays(0, 0)
            split_hi(n0 + 2)
            for tt in range(TT):
                act.wait_ge(products, 2 * n0 + 3 + tt // 2)
                A(zs[:, tt, :], ps[:, 2 + tt, :], ACT.Silu, scale=stat[:, 4 + tt:5 + tt]).then_inc(evac, 1)
            scan_groups(act, group)
            act.wait_ge(yT_done, 4 * SG)
            A(yh[:, :, 12:16, :], yT[:, :, 12:16, :], ACT.Copy).then_inc(yh_done, 1)
            residual("ssm_out")
            ffn("up1", "down1", 3)

        @block.vector
        def _(dve):
            V = Tally(vec)
            TTo, TS, STT = dve.tensor_tensor, dve.tensor_scalar, dve.scalar_tensor_tensor

            def step(ins):
                V.inc(ins)
                V.wait(dve)

            def split_lo(n, i=None, per=0):
                s = n % 2
                dve.wait_ge(hi_done, at(n + 1, i, per))
                TTo(wl[:, s, :], wraw[:, s, :], wh[:, s, :].bitcast(F32), ALU.subtract).then_inc(lo_done, 1)

            def x_lo(L, kt):
                dve.wait_ge(xh_done, kt + (8 * L + 1))
                k = slice(kt, kt + 1) if isinstance(kt, int) else bass.ds(kt, 1)
                w = col(NORMCOL[L] + kt) if isinstance(kt, int) else cols[:, bass.ds(kt + NORMCOL[L], 1)]

                def tile(t):
                    return t[:, k, :].rearrange("p a n -> p (a n)")
                STT(out=tile(xl), in0=tile(xT), scalar=w, in1=tile(xh).bitcast(F32), op0=ALU.mult, op1=ALU.subtract
                    ).then_inc(xl_done, 1)

            def mean_square(L):
                dve.wait_ge(colsum_done, L + 1)
                TS(stat[:, 0:4], ps[:, 7, 0:4], 1.0 / DM, EPS, ALU.mult, ALU.add).then_inc(mean_done, 1)

            def diagonal(L):
                dve.wait_ge(rstd_done, L + 1)
                for tt in range(TT):
                    ins = TS(diag[:, tt, :], ident[:, :], stat[:, 4 + tt:5 + tt], None, ALU.mult)
                ins.then_inc(diag_done, 1)

            def residual(name):
                ks, n0, t0 = RES[name], CHUNK[name], EVAC[name]
                per = 2 * len(ks)
                ahead = name in ("nsa_out", "ssm_out")

                def turn(i, shift):
                    for p in range(2):
                        for q in range(len(ks)):
                            n = n0 + p * len(ks) + q + 1 + shift * per
                            if n < NCHUNKS and not ahead:
                                split_lo(n, i, per)
                            if ahead and q < len(ks) - 1:
                                split_lo(n + 1)
                        for m in range(2):
                            t = 2 * p + m + 4 * shift
                            last = n0 + (p + 1) * len(ks) - 1 + shift * per
                            dve.wait_ge(products, at(2 * last + m + 1, i, 2 * per))
                            x = xT[:, t, :] if i is None else xT[:, bass.ds(i * 4 + t, 1), :].rearrange(
                                "p a n -> p (a n)")
                            TTo(x, ps[:, 2 * p + m, :], x, ALU.add).then_inc(evac, 1)
                        if name in EARLY:
                            for t in (2 * p + 4 * shift, 2 * p + 1 + 4 * shift):
                                x_lo(NORM[name], t if i is None else i * 4 + t)
                        if ahead and n + 1 <= n0 + 2 * per:
                            split_lo(n + 1)
                if n0 + 2 * per < NCHUNKS and not ahead:
                    with dve.Fori(0, 2) as i:
                        turn(i, 0)
                else:
                    turn(None, 0)
                    turn(None, 1)
                if name in NORM:
                    if name not in EARLY:
                        for kt in range(KT):
                            x_lo(NORM[name], kt)
                    mean_square(NORM[name])
                    diagonal(NORM[name])

            def ffn(up, down, L):
                n0, t0, h0 = CHUNK[up], EVAC[up], FT * (L == 3)

                def turn(i):
                    split_lo(n0 + 1, i, 2)
                    if isinstance(i, int):
                        dve.wait_ge(rbc_done, L)
                        step(dve.tensor_copy(tmp[:, 0, :], ps[:, 6, :]))
                    for j in range(2):
                        dve.wait_ge(products, i * 4 + (2 * n0 + j + 1))
                        dve.wait_ge(evac, i * 2 + (t0 - 1 + j))
                        TTo(gate[:, j, :], ps[:, j, :], tmp[:, 0, :], ALU.mult).then_inc(gate_in, 1)
                    split_lo(n0 + 2, i, 2)
                    for j in range(2):
                        dve.wait_ge(products, i * 4 + (2 * n0 + 3 + j))
                        after(dve, hh_done, i * 2 + (h0 + j - 1))
                        step(TTo(hid[:, j, :], ps[:, 2 + j, :], tmp[:, 0, :], ALU.mult))
                        dve.wait_ge(gate_done, i * 2 + (h0 + j + 1))
                        TTo(hid[:, j, :], hid[:, j, :], gate[:, j, :], ALU.mult).then_inc(evac, 1)
                        dve.wait_ge(hh_done, i * 2 + (h0 + j + 1))
                        h = bass.ds(i * 2 + j, 1)
                        TTo(hl[:, h, :].rearrange("p a n -> p (a n)"), hid[:, j, :],
                            hh[:, h, :].rearrange("p a n -> p (a n)").bitcast(F32), ALU.subtract).then_inc(hl_done, 1)
                turn(0)
                with dve.Fori(0, FT // 2 - 1) as i:
                    V.enter(i, 2)
                    turn(i + 1)
                V.leave(FT // 2 - 1, 2)
                residual(down)

            dve.wait_ge(cols_landed, 16)
            for kt in range(KT):
                if kt % 2 == 0:
                    dve.wait_ge(x_landed[kt // 2], 16)
                x_lo(0, kt)
                if kt == 1:
                    split_lo(0)
            split_lo(1)
            dve.wait_ge(params_landed, 48)
            dve.tensor_copy(ident_bf[:, :], ident[:, :]).then_inc(masks_cast, 1)
            step(TTo(diag[:, 0, :], tri[:, 1, :], ident[:, :], ALU.add))
            TS(negmask_bf[:, :], diag[:, 0, :], -NEG, NEG, ALU.mult, ALU.add).then_inc(masks_cast, 1)
            mean_square(0)
            split_lo(2)
            for kv in range(2):
                for gp in range(2):
                    dve.wait_ge(kvT, 2 * kv + gp + 1)
                    for lp in range(2):
                        dve.tensor_copy(tb2[lp * DH:(lp + 1) * DH, kv, gp * 2, :], ps[0:DH, 4 + 2 * kv + gp, lp::2]
                                        ).then_inc(tb_vec, 1)
            split_lo(3)
            dve.wait_ge(tb_vec, 8)
            dve.wait_ge(tb_act, 8)
            V.inc(dve.memset(tbT[:, :, :, :, :].rearrange("p k j g c -> p (k j g) c")[:, :, NCMP:32], 0.0))
            for kv in range(2):
                for jh in range(2):
                    src = tb2[:, kv, :, 8 * jh:8 * jh + 248].rearrange("p g (c j) -> p j g c", j=8)
                    pe_ = col(COL_PE + kv * NJ + 8 * jh, 8).unsqueeze(2).unsqueeze(3).broadcast_to([P, 8, GROUPS, NCMP])
                    TTo(tbT[:, kv, 8 * jh:8 * jh + 8, :, 0:NCMP], src, pe_, ALU.add).then_inc(tbT_done, 1)
            split_lo(4)
            dve.wait_ge(rest_landed, 32)
            step(dve.tensor_copy(stat[:, 16:21], posi[:, :]))
            a0 = ang[:, 0, :].rearrange("p (t f) -> p t f", f=8)
            step(TTo(a0, stat[:, 16:21].unsqueeze(2).broadcast_to([P, 5, 8]),
                     rows[:, ROW_INV:ROW_INV + 8].unsqueeze(1).broadcast_to([P, 5, 8]), ALU.mult))
            magic = 1.5 * 2.0 ** 23
            step(TS(ang[:, 1, :], ang[:, 0, :], float(1 / (2 * np.pi)), magic, ALU.mult, ALU.add))
            step(TS(ang[:, 2, :], ang[:, 1, :], magic, None, ALU.subtract))
            c1 = 6.28125
            c2 = float(np.float32(np.round((2 * np.pi - c1) * 2.0 ** 21) / 2.0 ** 21))
            c3 = float(np.float32(2 * np.pi - c1 - c2))
            for n, cc in enumerate((c1, c2, c3)):
                step(STT(out=ang[:, 3 + n, :], in0=ang[:, 2, :], scalar=-cc, in1=ang[:, 0 if n == 0 else 2 + n, :],
                         op0=ALU.mult, op1=ALU.add))
            step(TS(ang[:, 8, :], ang[:, 5, :], PI, -PI, ALU.min, ALU.max))
            step(TS(ang[:, 6, :], ang[:, 5, :], float(np.pi / 2), None, ALU.add))
            step(TS(ang[:, 7, :], ang[:, 6, :], PI, float(-2 * np.pi), ALU.is_gt, ALU.mult))
            step(TTo(ang[:, 6, :], ang[:, 6, :], ang[:, 7, :], ALU.add))
            TS(ang[:, 9, :], ang[:, 6, :], PI, -PI, ALU.min, ALU.max).then_inc(angles_done, 1)
            dve.wait_ge(gates_T, 1)
            TTo(glin[:, :, :], ps[:, 5, 0:TT * 48].rearrange("p (t f) -> p t f", t=TT),
                stat[:, 24:28].unsqueeze(2).broadcast_to([P, TT, 48]), ALU.mult).then_inc(evac, 1)
            n0 = CHUNK["qkv"]

            def qk_mean_square(tt, g):
                after(dve, qk_rstd, g * 4 + tt)
                dve.wait_ge(qk_squared, g * 4 + (tt + 1))
                step(dve.tensor_reduce(sm[:, 0, 0:6], qn[:, tt, :, 0, :], AX, ALU.add))
                TS(sm[:, 1, 0:6], sm[:, 0, 0:6], 1.0 / DH, EPS, ALU.mult, ALU.add).then_inc(qk_mean, 1)

            def qk_twice(tt, g):
                dve.wait_ge(qk_rotated, g * 8 + 2 * (tt + 1))
                dve.tensor_copy(qn[:, tt, :, 1, :], qn[:, tt, :, 0, :]).then_inc(qk_normed, 1)

            def transposed_lo(g, heads, bank):
                for h in heads:
                    dve.wait_ge(qkT_hi, g * 6 + (h + 1))
                    if h < HP:
                        lo = qA[DH:P, h, :]
                        TTo(lo, ps[DH:P, bank(h), :], lo.bitcast(F32), ALU.subtract).then_inc(qkT_lo, 1)
                    else:
                        TTo(kB2[:, h - HP, :], ps[:, bank(h), :], kB1[:, h - HP, :].bitcast(F32), ALU.subtract
                            ).then_inc(qkT_lo, 1)

            def stage_cmp_keys(g):
                after(dve, csT_mm, g)
                for b in range(2):
                    ins = dve.tensor_copy(
                        Bh[:, b, :].rearrange("p (h x) -> p h x", h=HP)[:, :, 0:32],
                        Bc[:, b, bass.ds(g * 32, 32)].bitcast(F32).unsqueeze(1).broadcast_to([P, HP, 32]))
                ins.then_inc(kc_staged, 1)

            def group(g, more):
                def stage_v():
                    dve.wait_ge(vz_zeroed, 1)
                    dve.wait_ge(pv_done, g * 4)
                    dve.tensor_copy(vst[:, :, :, :], proj[:, :, 6:8, :]).then_inc(v_staged, 1)
                    for h in range(HP):
                        b = slice(32 * h, 32 * (h + 1))
                        dve.tensor_copy(vz[b, h, :], VC4[b, bass.ds(g, 1), :].rearrange("p a d -> p (a d)")
                                        ).then_inc(vz_done, 1)

                pf = pc[:, :, :, :].rearrange("p t h c -> p (t h) c")
                gt = glin[:, :, bass.ds(g * 12, 12)].rearrange("p t (h b) -> p t h b", b=3)

                def cmp_shift():
                    dve.wait_ge(cs_mm, g + 1)
                    step(TTo(pc[:, :, :, :], ps[:, 6, :].rearrange("p (t h c) -> p t h c", t=TT, h=HP),
                             cmask[:, 0].unsqueeze(2).broadcast_to([P, TT, HP, 32]), ALU.add))
                    step(dve.tensor_reduce(sm[:, 0, 8:24], pf, AX, ALU.max))
                    TTo(pf, pf, sm[:, 0, 8:24].unsqueeze(2).broadcast_to([P, 16, 32]), ALU.subtract
                        ).then_inc(cs_shifted, 1)

                def cmp_probs():
                    dve.wait_ge(cs_exp, g + 1)
                    step(dve.tensor_reduce(sm[:, 1, 8:24], pf, AX, ALU.add))
                    step(dve.reciprocal(sm[:, 2, 8:24], sm[:, 1, 8:24]))
                    step(TTo(sm[:, 3, 8:24].rearrange("p (t h) -> p t h", t=TT),
                             sm[:, 2, 8:24].rearrange("p (t h) -> p t h", t=TT), gt[:, :, :, 0], ALU.mult))
                    step(TTo(pf, pf, sm[:, 3, 8:24].unsqueeze(2).broadcast_to([P, 16, 32]), ALU.mult))
                    TTo(pc[:, :, :, :], pc[:, :, :, :], cmask[:, 1].unsqueeze(2).broadcast_to([P, TT, HP, 32]), ALU.mult
                        ).then_inc(pc_done, 1)

                def maxima(s):
                    h, i = divmod(s, TT)
                    m = 8 * (s % 2)
                    dve.wait_ge(scores, g * 16 + (s + 1))
                    step(dve.tensor_reduce(sm[:, 4, m:m + 2], ps[:, 2 * (s % 2):2 * (s % 2) + 2, 0:(i + 1) * P], AX,
                                           ALU.max))
                    TS(sm[:, 4, m + 2:m + 4], sm[:, 4, m:m + 2], -SCALE, None, ALU.mult).then_inc(negmax, 1)

                def normalize(s):
                    h, i = divmod(s, TT)
                    m = 8 * (s % 2)
                    dve.wait_ge(expd, g * 32 + 2 * (s + 1))
                    step(dve.reciprocal(sm[:, 5, m:m + 2], sm[:, 4, m + 4:m + 6]))
                    step(TTo(sm[:, 5, m + 2:m + 4], sm[:, 5, m:m + 2], gt[:, i, h, 1:3], ALU.mult))
                    for b in range(2):
                        p_ = Pm[:, s % 2, b, 0:(i + 1) * P]
                        TS(p_, p_, sm[:, 5, m + 2 + b:m + 3 + b], None, ALU.mult).then_inc(normed, 1)

                def o_rest(pr):
                    dve.wait_ge(o_hi, g * 2 + (pr + 1))
                    o = bass.ds(g * 2 + pr, 1)
                    TTo(xol[:, o, :].rearrange("p a n -> p (a n)"), ps[:, 6, :],
                        xo[:, o, :].rearrange("p a n -> p (a n)").bitcast(F32), ALU.subtract).then_inc(o_lo, 1)

                for k in range(18):
                    if k < 16:
                        maxima(k)
                    if 1 <= k <= 16:
                        normalize(k - 1)
                    if k == 0:
                        stage_v()
                    if k == 1:
                        cmp_shift()
                    if k == 3:
                        cmp_probs()
                    if k == 14:
                        o_rest(0)
                    if more and k in (4, 7, 10, 13):
                        qk_mean_square(k // 3 - 1, g + 1)
                    if more and k in (6, 9, 12, 15):
                        qk_twice(k // 3 - 2, g + 1)
                    if more and k == 8:
                        stage_cmp_keys(g + 1)
                    if more and k == 16:
                        transposed_lo(g + 1, (0, 1, 2), lambda h: (h - 1) % 8)
                    if more and k == 17:
                        transposed_lo(g + 1, (3, 4, 5), lambda h: h - 1 if h < 5 else 7)
                    if more and k in (14, 15):
                        split_lo(n0 + 4 + k - 14, g, 2)
                o_rest(1)

            split_lo(5)
            for tt in range(TT):
                qk_mean_square(tt, 0)
                if tt:
                    qk_twice(tt - 1, 0)
            split_lo(6)
            qk_twice(3, 0)
            dve.wait_ge(gates_exp, 1)
            step(TS(glin[:, :, :], glin[:, :, :], 1.0, None, ALU.add))
            dve.reciprocal(glin[:, :, :], glin[:, :, :]).then_inc(gates_done, 1)
            transposed_lo(0, (0, 1, 2), lambda h: h)
            dve.wait_ge(kc_sq, 1)
            step(dve.tensor_reduce(stat[:, 8:9], kcn[:, 0, :], AX, ALU.add))
            TS(stat[:, 9:10], stat[:, 8:9], 1.0 / DH, EPS, ALU.mult, ALU.add).then_inc(kc_mean, 1)
            dve.tensor_copy(VC4[:, :, :], ps[:, 6, DH:(GROUPS + 1) * DH].rearrange("p (g d) -> p g d", g=GROUPS)
                            ).then_inc(vc_done, 1)
            dve.wait_ge(kc_rstd, 1)
            step(STT(out=kcn[:, 0, :], in0=ps[:, 6, 0:DH], scalar=stat[:, 11:12], in1=rows[:, ROW_KC:ROW_KC + DH],
                     op0=ALU.mult, op1=ALU.mult))
            c_, s_ = cosT[:, 4, :], sinT[:, 4, :]
            x1, x2 = kcn[:, 0, 0:8], kcn[:, 0, 8:16]
            V.inc(TTo(krp[:, 0, :], x1, c_, ALU.mult))
            V.inc(TTo(krp[:, 1, :], x2, s_, ALU.mult))
            V.inc(TTo(krp[:, 2, :], x2, c_, ALU.mult))
            step(TTo(krp[:, 3, :], x1, s_, ALU.mult))
            step(TTo(x1, krp[:, 0, :], krp[:, 1, :], ALU.subtract))
            step(TTo(x2, krp[:, 2, :], krp[:, 3, :], ALU.add))
            dve.tensor_copy(kcn[:, 1, :], kcn[:, 0, :]).then_inc(kcn_done, 1)
            transposed_lo(0, (3, 4, 5), lambda h: (3, 7, 4)[h - 3])
            dve.wait_ge(kc_hi, 1)
            TTo(Bc[:, 1, :], ps[:, 6, 3 * P:4 * P], Bc[:, 0, :].bitcast(F32), ALU.subtract).then_inc(kc_lo, 1)
            dve.wait_ge(kc_lo, 1)
            dve.wait_ge(kc_padded, 1)
            stage_cmp_keys(0)
            dve.wait_ge(gates_done, 1)
            with dve.Fori(0, GROUPS - 1) as g:
                V.enter(g, DVE_GROUP_STEPS)
                group(g, True)
            V.leave(GROUPS - 1, DVE_GROUP_STEPS)
            group(GROUPS - 1, False)
            dve.wait_ge(x_again, 16)
            residual("nsa_out")
            ffn("up0", "down0", 1)

            n0, t0 = CHUNK["xbc"], EVAC["xbc"]

            def conv_tiles(n, i, t, u):
                def taps(j):
                    dve.wait_ge(products, at(2 * (n + j // 2) + j % 2 + 1, i, 4))
                    if i is not None or t + j >= t0 + 2:
                        dve.wait_ge(silu_done, at(t - t0 + j - 1, i, 4))

                    def w(tap):
                        c0 = COL_CW + tap * 24 + u + j
                        return col(c0) if i is None else cols[:, bass.ds(i * 4 + c0, 1)]
                    c, x = tmp[:, j % 2, :], raw[:, j % 2, :]
                    step(TTo(x, ps[:, j, :], rbs[:, :], ALU.mult))
                    step(TS(c, x, w(3), None, ALU.mult))
                    for d in range(1, 4):
                        ins = STT(out=c[:, d:], in0=x[:, 0:SEQ - d], scalar=w(3 - d), in1=c[:, d:],
                                  op0=ALU.mult, op1=ALU.add)
                        if d < 3:
                            step(ins)
                        else:
                            ins.then_inc(evac, 1)
                if n == CHUNK["xbc"]:
                    dve.wait_ge(rbc_done, 2)
                    step(dve.tensor_copy(rbs[:, :], ps[:, 6, :]))
                taps(0)
                taps(1)
                split_lo(n + 2, i, 2)
                taps(2)
                taps(3)
                split_lo(n + 3, i, 2)
            split_lo(n0 + 1)
            conv_tiles(n0, None, t0, 20)
            conv_tiles(n0 + 2, None, t0 + 4, 16)
            with dve.Fori(0, 4) as i:
                V.enter(i, 16)
                conv_tiles(n0 + 4, i, t0 + 8, 0)
            V.leave(4, 16)
            bias = rows[:, ROW_DTB:ROW_DTB + SH]
            dve.wait_ge(dt_T, 1)
            dt3 = dtb[:, 0, :].rearrange("p (t h) -> p t h", t=TT)
            step(TTo(dt3, ps[:, 7, 0:TT * SH].rearrange("p (t h) -> p t h", t=TT),
                     stat[:, 4:8].unsqueeze(2).broadcast_to([P, TT, SH]), ALU.mult))
            TTo(dt3, dt3, bias.unsqueeze(1).broadcast_to([P, TT, SH]), ALU.add).then_inc(evac, 1)
            dve.wait_ge(evac, EVAC["z"])
            step(TS(dtb[:, 4, :], dtb[:, 0, :], -1.0, None, ALU.mult))
            TTo(dtb[:, 1, :], dtb[:, 0, :], dtb[:, 4, :], ALU.max).then_inc(dt_in, 1)
            split_lo(CHUNK["z"] + 1)
            dve.wait_ge(dt_e, 1)
            TS(dtb[:, 3, :], dtb[:, 2, :], 1.0, None, ALU.add).then_inc(dt_u, 1)
            dve.wait_ge(dt_u, 1)
            step(TS(dtb[:, 4, :], dtb[:, 3, :], 1.0, None, ALU.subtract))
            step(TS(dtb[:, 5, :], dtb[:, 4, :], 0.0, None, ALU.is_equal))
            step(TTo(dtb[:, 4, :], dtb[:, 4, :], dtb[:, 5, :], ALU.add))
            step(dve.reciprocal(dtb[:, 6, :], dtb[:, 4, :]))
            dve.wait_ge(dt_ln, 1)
            step(TTo(dtb[:, 7, :], dtb[:, 7, :], dtb[:, 6, :], ALU.mult))
            step(TTo(dtb[:, 7, :], dtb[:, 7, :], dtb[:, 5, :], ALU.add))
            step(TTo(dtb[:, 7, :], dtb[:, 7, :], dtb[:, 2, :], ALU.mult))
            step(STT(out=dtb[:, 0, :], in0=dtb[:, 0, :], scalar=0.0, in1=dtb[:, 7, :], op0=ALU.max, op1=ALU.add))
            dve.wait_ge(a_exp, 1)
            STT(out=dtb[:, 1, :].rearrange("p (t h) -> p t h", t=TT), in0=dtb[:, 0, :].rearrange("p (t h) -> p t h", t=TT),
                scalar=-1.0, in1=dtb[:, 9, 0:SH].unsqueeze(1).broadcast_to([P, TT, SH]), op0=ALU.mult, op1=ALU.mult
                ).then_inc(dt_done, 1)
            dve.wait_ge(dt_done, 1)
            n0 = CHUNK["z"]

            def build_g(g, j):
                for q in range(2):
                    after(dve, seg_mm, g * 8 + (2 * j + q - 1))
                    at_ = g * SHP + ((j // TT) * SHP + (j % TT) * SH + 4 * q)
                    TTo(Gm[:, q, :, :], tri[:, 0, :].unsqueeze(1).broadcast_to([P, 4, P]),
                        dtb[:, 1, bass.ds(at_, 4)].unsqueeze(2).broadcast_to([P, 4, P]), ALU.mult).then_inc(g_built, 1)

            def stage(g, j):
                dve.wait_ge(cb_mm, g * 4 + (j + 1))
                after(dve, m_built, g * 8 + 2 * (j - 1))
                TTo(cbm[:, j % 2, :], ps[:, 6, 0:P], tri[:, 0, :], ALU.mult)
                after(dve, y_mm, g * 8 + 2 * (j - 1))
                dve.tensor_copy(btst[:, j % 2, :], ps[:, 6, P:2 * P]).then_inc(cb_done, 1)

            def y_mean_square(g, j):
                dve.wait_ge(y_sq, g * 4 + (j + 1))
                TS(yst[:, j % 2, 1:2], yst[:, j % 2, 0:1], 1.0 / GW, EPS, ALU.mult, ALU.add).then_inc(y_var, 1)

            def scale_y(g, j):
                dve.wait_ge(y_rs, g * 4 + (j + 1))
                y = ybuf[:, j % 2, :]
                TS(y, y, yst[:, j % 2, 2:3], None, ALU.mult).then_inc(y_scaled, 1)

            def to_features(g, j):
                dve.wait_ge(yT_mm, g * 4 + (j + 1))
                f = g * 4 + (j // TT) * 4
                w = cols[:, bass.ds(g * 4 + (COL_SSMN + (j // TT) * 4), 4)].unsqueeze(2).broadcast_to([P, 4, P])
                TTo(yT[:, j % TT, bass.ds(f, 4), :], ps[:, 7, :].rearrange("p (k n) -> p k n", k=4), w, ALU.mult
                    ).then_inc(yT_done, 1)

            def heads(ap):
                return ap.rearrange("p (h d) -> p h d", h=SHP)

            def group(g, last):
                first = isinstance(g, int) and g == 0

                def per_head(n, c):
                    return ex[:, n, bass.ds(g * SHP + c * SH, SHP)].unsqueeze(2).broadcast_to([P, SHP, SP_])
                for k in range(TT):
                    if k or not first:
                        y_mean_square(g, k - 1)
                    if k < 3 or not last:
                        stage(g, k + 1)
                    if k or not first:
                        scale_y(g, k - 1)
                    if k < 2 or not last:
                        build_g(g, k + 2)
                    if k == 0:
                        split_lo(n0 + 3, g, 2)
                    if k == 3 and not last:
                        split_lo(n0 + 4, g, 2)
                    y = ybuf[:, k % 2, :]
                    after(dve, yT_mm, g * 4 + (k - 1))
                    if k < 3:
                        dve.wait_ge(state_mm, g * 3 + (k + 1))
                    if k:
                        dve.wait_ge(y_mm, g * 8 + (2 * k + 1))
                        V.inc(TTo(heads(y), heads(ps[:, 3, :]), per_head(0, k), ALU.mult))
                    if k in (1, 2):
                        step(TTo(heads(state[:, :]), heads(state[:, :]), per_head(2, k), ALU.mult))
                        TTo(state[:, :], state[:, :], ps[:, 4, :], ALU.add).then_inc(state_done, 1)
                    if k == 0:
                        dve.tensor_copy(state[:, :], ps[:, 4, :]).then_inc(state_done, 1)
                    dve.wait_ge(y_mm, g * 8 + 2 * (k + 1))
                    dve.wait_ge(xdt_done, g * 12 + 3 * (k + 1))
                    V.wait(dve)
                    step(TTo(y, y if k else dxs[:, k % 2, :], ps[:, 2, :], ALU.add))
                    if k:
                        step(TTo(y, y, dxs[:, k % 2, :], ALU.add))
                    if k == 0 and not first:
                        dve.wait_ge(z_silu, g)
                    TTo(y, y, zs[:, k, :], ALU.mult).then_inc(y_done, 1)
                    if k or not first:
                        to_features(g, k - 1)
                    if last:
                        dve.wait_ge(yh_done, k + 1)
                        dve.wait_ge(yT_done, 9 + k)
                        TTo(yl[:, k, 0:12, :], yT[:, k, 0:12, :], yh[:, k, 0:12, :].bitcast(F32), ALU.subtract
                            ).then_inc(yl_done, 1)
            build_g(0, 0)
            dve.wait_ge(cum_exp, 1)
            stage(0, 0)
            build_g(0, 1)
            split_lo(n0 + 2)
            scan_groups(dve, group, lambda i: V.enter(i, DVE_SCAN_STEPS), lambda: V.leave(SG - 2, DVE_SCAN_STEPS))
            y_mean_square(SG - 1, 3)
            scale_y(SG - 1, 3)
            to_features(SG - 1, 3)
            dve.wait_ge(yh_done, TT + 1)
            TTo(yl[:, :, 12:16, :], yT[:, :, 12:16, :], yh[:, :, 12:16, :].bitcast(F32), ALU.subtract).then_inc(yl_done, 1)
            residual("ssm_out")
            ffn("up1", "down1", 3)

        @block.gpsimd
        def _(pool):
            TTo = pool.tensor_tensor

            def rstd(dst, src, ready, value, done):
                pool.wait_ge(ready, value)
                n = src.shape[-1]
                TTo(dst, src, mhalf[:, 0:n], ALU.pow).then_inc(done, 1)
            pool.memset(mhalf[:, :], -0.5).then_inc(mhalf_set, 1)
            pool.wait_ge(mhalf_set, 1)

            def square_sum(L):
                if L:
                    pool.wait_ge(colsum_done, L)
                pool.memset(sqacc[:, :], 0.0).then_inc(zeroed, 1)
                pool.wait_ge(zeroed, L + 1)

                def add(mt, i):
                    pool.wait_ge(sq_done, at(8 * L + mt + 1, i, 2))
                    pool.wait_ge(acc_done, at(8 * L + mt, i, 2))
                    TTo(sqacc[:, :], sqacc[:, :], sq[:, mt % 2, :], ALU.add).then_inc(acc_done, 1)
                with pool.Fori(0, 4) as i:
                    add(0, i)
                    add(1, i)
                r0 = 4 if L else 24
                rstd(stat[:, r0:r0 + 4], stat[:, 0:4], mean_done, L + 1, rstd_done)
            square_sum(0)
            pool.wait_ge(rstd_done, 1)
            pool.wait_ge(masks_cast, 2)
            pool.memset(vz[:, :, :], 0.0).then_inc(vz_zeroed, 1)
            pool.wait_ge(vz_zeroed, 1)
            pool.memset(Bh[:, :, :].bitcast(F32), 0.0).then_inc(kc_padded, 1)
            G = Tally(pool_self)
            QK_STEPS = 4 * 3

            def step(ins):
                G.inc(ins)
                G.wait(pool)

            def qk_norm(tt, g):
                rstd(sm[:, 3, 0:6], sm[:, 1, 0:6], qk_mean, g * 4 + (tt + 1), qk_rstd)
                pool.wait_ge(qk_rstd, g * 4 + (tt + 1))
                q6 = qn[:, tt, :, 0, :]
                step(TTo(q6, proj[:, tt, 0:6, :], sm[:, 3, 0:6].unsqueeze(2).broadcast_to([P, 6, DH]), ALU.mult))
                step(TTo(q6, q6, rows[:, ROW_W6:ROW_W6 + 384].rearrange("p (h d) -> p h d", d=DH), ALU.mult))
                cc = cosT[:, tt, :].unsqueeze(1).broadcast_to([P, 6, 8])
                ss = sinT[:, tt, :].unsqueeze(1).broadcast_to([P, 6, 8])
                x1, x2 = q6[:, :, 0:8], q6[:, :, 8:16]
                after(pool, qk_rotated, g * 8 + 2 * tt)
                TTo(rp[:, 0], x1, cc, ALU.mult)
                TTo(rp[:, 1], x2, ss, ALU.mult)
                TTo(rp[:, 2], x2, cc, ALU.mult)
                step(TTo(rp[:, 3], x1, ss, ALU.mult))
                TTo(x1, rp[:, 0], rp[:, 1], ALU.subtract).then_inc(qk_rotated, 1)
                TTo(x2, rp[:, 2], rp[:, 3], ALU.add).then_inc(qk_rotated, 1)
            pool.wait_ge(sincos_done, 2)
            for tt in range(TT):
                qk_norm(tt, 0)
            rstd(stat[:, 11:12], stat[:, 9:10], kc_mean, 1, kc_rstd)
            with pool.Fori(0, GROUPS - 1) as g:
                G.enter(g, QK_STEPS)
                for tt in range(TT):
                    qk_norm(tt, g + 1)
            G.leave(GROUPS - 1, QK_STEPS)
            pool.wait_ge(o_lo, 2 * GROUPS)
            square_sum(1)
            square_sum(2)
            pool.wait_ge(cum_exp, 1)

            def heads(ap):
                return ap.rearrange("p (h d) -> p h d", h=SHP)

            def inputs(g, j):
                c, b = j % TT, j % 2
                x = xtok[:, c, bass.ds(g * GW + (j // TT) * GW, GW)].rearrange("p (h d) -> p h d", d=SP_)
                hd = g * SHP + (j // TT) * SHP

                def per_head(row):
                    return row.unsqueeze(2).broadcast_to([P, SHP, SP_])
                after(pool, y_mm, g * 8 + 2 * (j - 1))
                after(pool, y_done, g * 4 + (j - 1))
                TTo(heads(xdt[:, b, :]), x, per_head(dtb[:, 0, bass.ds(hd + c * SH, SHP)]), ALU.mult).then_inc(xdt_done, 1)
                TTo(heads(dxs[:, b, :]), x, per_head(rows[:, bass.ds(hd + ROW_D, SHP)]), ALU.mult).then_inc(xdt_done, 1)
                pool.wait_ge(xdt_done, g * 12 + (3 * j + 1))
                TTo(heads(xdd[:, b, :]), heads(xdt[:, b, :]), per_head(ex[:, 1, bass.ds(hd + c * SH, SHP)]), ALU.mult
                    ).then_inc(xdt_done, 1)
                pool.wait_ge(cb_done, g * 4 + (j + 1))
                for q in range(2):
                    pool.wait_ge(seg_exp, g * 8 + (2 * j + q + 1))
                    TTo(Lx[:, b, q, :, :], Lx[:, b, q, :, :], cbm[:, b, :].unsqueeze(1).broadcast_to([P, 4, P]),
                        ALU.mult).then_inc(m_built, 1)

            def group(g, last):
                for k in range(TT):
                    if k or not isinstance(g, int) or g:
                        rstd(yst[:, (k - 1) % 2, 2:3], yst[:, (k - 1) % 2, 1:2], y_var, g * 4 + k, y_rs)
                    if k < 3 or not last:
                        inputs(g, k + 1)
            inputs(0, 0)
            scan_groups(pool, group)
            rstd(yst[:, 1, 2:3], yst[:, 1, 1:2], y_var, 4 * SG, y_rs)
            square_sum(3)


def kernel(x, positions, mix_norm_w, ffn_norm_w, ffn_w_gate, ffn_w_up, ffn_w_down, nsa_w_in, nsa_q_norm, nsa_k_norm,
           nsa_cmp_pe, nsa_cmp_w1, nsa_cmp_b1, nsa_cmp_w2, nsa_w_out, ssm_w_in, ssm_conv_w, ssm_conv_b, ssm_dt_bias,
           ssm_a_log, ssm_d, ssm_norm_w, ssm_w_out):
    import concourse.bacc as bacc
    from concourse.bass_utils import run_bass_kernel_spmd

    def arr(a):
        return np.asarray(a)

    def f_chunks(w, kgroups):
        out = []
        for c in range(0, w.shape[1], 256):
            k0 = 0
            for nk in kgroups:
                part = w[k0 * P:(k0 + nk) * P, c:c + 256].reshape(nk, P, 256).transpose(1, 0, 2).reshape(P, -1)
                out.append(np.pad(part, ((0, 0), (0, CH - part.shape[1]))))
                k0 += nk
        return out

    def t_chunks(w):
        out = []
        for c in range(0, w.shape[1], 512):
            for k0 in (0, 4):
                out.append(w[k0 * P:(k0 + 4) * P, c:c + 512].reshape(4, P, 512).transpose(1, 0, 2).reshape(P, -1))
        return out

    def n_chunk(w):
        part = w.reshape(KT, P, w.shape[1]).transpose(1, 0, 2).reshape(P, -1)
        return [np.pad(part, ((0, 0), (0, CH - part.shape[1])))]

    w_in, s_in = arr(nsa_w_in)[0], arr(ssm_w_in)[0]
    stream = t_chunks(w_in[:, 1024:1536])
    stream += n_chunk(w_in[:, 2560:2608])
    for g in range(GROUPS):
        at = [slice(g * 256, (g + 1) * 256)] + [slice(b + g * DH, b + (g + 1) * DH) for b in (1536, 2048, 1792, 2304)]
        stream += t_chunks(np.concatenate([w_in[:, a] for a in at], 1))
    stream += f_chunks(arr(nsa_w_out)[0], [8])

    def ffn_stream(layer):
        g = f_chunks(arr(ffn_w_gate)[layer], [8])
        u = f_chunks(arr(ffn_w_up)[layer], [8])
        return [c for pair in zip(g, u) for c in pair] + f_chunks(arr(ffn_w_down)[layer], [8, 8, 6])
    stream += ffn_stream(0)
    xbc = s_in[:, DI:DI + 3072]
    stream += f_chunks(np.concatenate([xbc[:, 2560:3072], xbc[:, 2048:2560], xbc[:, 0:2048]], 1), [8])
    stream += n_chunk(s_in[:, DI + 3072:])
    stream += t_chunks(s_in[:, 0:DI])
    stream += f_chunks(arr(ssm_w_out)[0], [8, 8])
    stream += ffn_stream(1)
    assert len(stream) == NCHUNKS

    def columns(a):
        return np.asarray(a).reshape(-1, P).T
    cols = np.concatenate(
        [columns(mix_norm_w), columns(ffn_norm_w), columns(ssm_norm_w), columns(ssm_conv_b), columns(ssm_conv_w),
         columns(nsa_cmp_b1), columns(nsa_cmp_pe)], 1)
    inv = np.power(np.float32(THETA), -np.arange(ROPE_HALF, dtype=np.float32) / ROPE_HALF).astype(np.float32)
    qn_, kn_ = arr(nsa_q_norm)[0], arr(nsa_k_norm)[0]
    row = np.concatenate([qn_, qn_, qn_, qn_, kn_[1], kn_[2], kn_[0], arr(ssm_d)[0], arr(ssm_dt_bias)[0],
                          arr(ssm_a_log)[0], inv])
    rows = np.broadcast_to(row, (P, NROWS))
    pos = arr(positions)[0]
    blocks = np.concatenate([pos[CMP_BLOCK - 1::CMP_STRIDE][:NCMP], pos[-1:]])
    pos5 = np.concatenate([pos.reshape(TT, P).T, np.tile(blocks, GROUPS)[:, None]], 1).astype(np.int32)
    idx = np.arange(P)
    tri = np.stack([idx[:, None] <= idx[None, :], idx[:, None] > idx[None, :], np.ones((P, P), bool)], 1)
    t = np.arange(SEQ).reshape(TT, P).T[:, :, None]
    cend = np.arange(32) * CMP_STRIDE + CMP_BLOCK - 1
    seen = (cend[None, None, :] <= t) & (np.arange(32) < NCMP)
    cmask = np.stack([np.where(seen, 0.0, NEG), seen], 1).astype(np.float32)
    arrays = {
        "wstream": np.stack(stream),
        "xT_in": arr(x)[0].T.reshape(KT, P, SEQ).transpose(1, 0, 2),
        "cols_in": cols,
        "rows_in": rows,
        "pos_in": pos5,
        "cw1_in": arr(nsa_cmp_w1)[0].reshape(2, NJ, P, CMP_HIDDEN).transpose(2, 0, 1, 3),
        "cw2_in": arr(nsa_cmp_w2)[0].reshape(2, 2, P, DH).transpose(2, 0, 1, 3),
        "ident_in": np.eye(P, dtype=np.float32),
        "tri_in": tri.astype(np.float32),
        "cmask_in": cmask,
    }
    arrays = {k: np.ascontiguousarray(v) for k, v in arrays.items()}
    nc = bacc.Bacc("TRN2", target_bir_lowering=False, num_devices=1, dynamic_dma_scratch_size=1024)
    args = [nc.dram_tensor(k, v.shape, mybir.dt.from_np(v.dtype), kind="ExternalInput").ap()
            for k, v in arrays.items()]
    out = nc.dram_tensor("out", (P, KT, SEQ), F32, kind="ExternalOutput").ap()
    trunk(nc, *args, out)
    r = run_bass_kernel_spmd(nc, [arrays], core_ids=[0])
    return r.results[0]["out"].transpose(1, 0, 2).reshape(DM, SEQ).T[None]
```
